# Optimizing a Trainium2 kernel written in Bass

```python
import jax
import jax.numpy as jnp
from jax import lax
import numpy as np
import jax, jax.numpy as jnp

D_MODEL = 1024
BATCH = 1
SEQ = 256
DEPTH = 2

GRID_W = 64
CTX_LEN = 256
N_MIXERS = 2
RET_HEADS = 4
RET_QK_DIM = D_MODEL // RET_HEADS
RET_V_DIM = 2 * D_MODEL // RET_HEADS
RET_CHUNK = 128
NAT_HEAD_DIM = 32
NAT_HEADS = D_MODEL // NAT_HEAD_DIM
NAT_WIN_ROWS = 8
NAT_WIN_COLS = 16
MLP_HIDDEN = 4 * D_MODEL
ROPE_BASE = 10000.0
LN_EPS = 1e-5
DN_ALPHA = (2.0 * DEPTH) ** 0.25
DN_BETA = (8.0 * DEPTH) ** -0.25
N_RET_LAYERS = (DEPTH + 1) // 2
N_NAT_LAYERS = DEPTH // 2


def layer_norm(x, g, b):
    xf = x.astype(jnp.float32)
    mu = jnp.mean(xf, axis=-1, keepdims=True)
    var = jnp.mean(jnp.square(xf - mu), axis=-1, keepdims=True)
    return ((xf - mu) * lax.rsqrt(var + LN_EPS) * g + b).astype(x.dtype)

def axial_rope_angles(n, axis_dim):
    t = jnp.arange(n)
    row = (t // GRID_W).astype(jnp.float32)
    col = (t % GRID_W).astype(jnp.float32)
    inv = 1.0 / (ROPE_BASE ** (jnp.arange(0, axis_dim, 2, dtype=jnp.float32) / axis_dim))
    return row[:, None] * inv, col[:, None] * inv

def rope_rotate(x, ang):
    cos = jnp.cos(ang).astype(x.dtype)
    sin = jnp.sin(ang).astype(x.dtype)
    x1, x2 = jnp.split(x, 2, axis=-1)
    return jnp.concatenate([x1 * cos - x2 * sin, x2 * cos + x1 * sin], axis=-1)

def axial_rope(x, ang_row, ang_col):
    xr, xc = jnp.split(x, 2, axis=-1)
    return jnp.concatenate([rope_rotate(xr, ang_row), rope_rotate(xc, ang_col)], axis=-1)

def retention_chunk_scan(q, k, v, log_gamma, state0, with_out):
    b, h, n, dk = q.shape
    dv = v.shape[-1]
    cs = RET_CHUNK
    nc = n // cs
    dt = v.dtype
    pos = jnp.arange(cs, dtype=jnp.float32)
    lg = log_gamma.astype(jnp.float32)[:, None]
    rel = pos[:, None] - pos[None, :]
    intra = jnp.where(rel >= 0, jnp.exp(lg[:, :, None] * jnp.maximum(rel, 0.0)), 0.0).astype(dt)
    q_dec = jnp.exp(lg * (pos + 1.0))[..., None].astype(dt)
    k_dec = jnp.exp(lg * (cs - 1.0 - pos))[..., None].astype(dt)
    chunk_dec = jnp.exp(lg * cs)[..., None].astype(dt)

    def to_chunks(t):
        return jnp.moveaxis(t.reshape(b, h, nc, cs, t.shape[-1]), 2, 0)

    def step(state, qkv):
        qc, kc, vc = qkv
        new_state = state * chunk_dec + jnp.einsum('bhsd,bhse->bhde', kc * k_dec, vc)
        if with_out:
            scores = jnp.einsum('bhcd,bhsd->bhcs', qc, kc) * intra
            out = (jnp.einsum('bhcs,bhse->bhce', scores, vc)
                   + jnp.einsum('bhcd,bhde->bhce', qc * q_dec, state))
            return new_state, out
        return new_state, None

    state, outs = lax.scan(step, state0, (to_chunks(q), to_chunks(k), to_chunks(v)))
    if with_out:
        outs = jnp.moveaxis(outs, 0, 2).reshape(b, h, n, dv)
    return state, outs

def retention_mixer(h_lat, h_ctx, w_in, w_o, decay_param, ang_row, ang_col, ctx_out):
    b = h_lat.shape[0]
    qk_w = RET_HEADS * RET_QK_DIM
    v_w = RET_HEADS * RET_V_DIM

    def heads(t, hd):
        return t.reshape(b, t.shape[1], RET_HEADS, hd).transpose(0, 2, 1, 3)

    def project(h, w):
        p = h @ w
        q = heads(p[..., :qk_w], RET_QK_DIM)
        k = heads(p[..., qk_w:2 * qk_w], RET_QK_DIM) * (RET_QK_DIM ** -0.5)
        v = heads(p[..., 2 * qk_w:2 * qk_w + v_w], RET_V_DIM)
        return q, k, v, p[..., 2 * qk_w + v_w:]

    def flip(t):
        return t[:, :, ::-1]

    def finish(o, g):
        of = o.astype(jnp.float32)
        mu = jnp.mean(of, axis=-1, keepdims=True)
        var = jnp.mean(jnp.square(of - mu), axis=-1, keepdims=True)
        on = ((of - mu) * lax.rsqrt(var + LN_EPS)).astype(o.dtype)
        on = on.transpose(0, 2, 1, 3).reshape(b, o.shape[2], v_w)
        return (on * jax.nn.silu(g)) @ w_o

    log_gamma = -jnp.exp(decay_param.astype(jnp.float32))
    w_ctx = w_in if ctx_out else w_in[:, :2 * qk_w + v_w]
    q_c, k_c, v_c, g_c = project(h_ctx, w_ctx)
    zeros = jnp.zeros((b, RET_HEADS, RET_QK_DIM, RET_V_DIM), v_c.dtype)
    s_f, o_cf = retention_chunk_scan(q_c, k_c, v_c, log_gamma[0], zeros, ctx_out)
    s_b, o_cb = retention_chunk_scan(flip(q_c), flip(k_c), flip(v_c), log_gamma[1], zeros, ctx_out)

    q_l, k_l, v_l, g_l = project(h_lat, w_in)
    q_l = axial_rope(q_l, ang_row, ang_col)
    k_l = axial_rope(k_l, ang_row, ang_col)
    _, o_lf = retention_chunk_scan(q_l, k_l, v_l, log_gamma[0], s_f, True)
    _, o_lb = retention_chunk_scan(flip(q_l), flip(k_l), flip(v_l), log_gamma[1], s_b, True)
    y_lat = finish(o_lf + flip(o_lb), g_l)
    y_ctx = finish(o_cf + flip(o_cb), g_c) if ctx_out else None
    return y_lat, y_ctx

def neighbourhood_mixer(h_lat, h_ctx, w_in, w_o, rpb, ctx_out):
    b, n, d = h_lat.shape
    rows = n // GRID_W
    kh = min(NAT_WIN_ROWS, rows)
    kw = NAT_WIN_COLS
    nh, hd = NAT_HEADS, NAT_HEAD_DIM
    scale = hd ** -0.5

    p = h_lat @ w_in
    q = p[..., :d].reshape(b, rows, GRID_W, nh, hd) * scale
    k = p[..., d:2 * d].reshape(b, rows, GRID_W, nh, hd)
    v = p[..., 2 * d:].reshape(b, rows, GRID_W, nh, hd)

    pc = h_ctx @ (w_in if ctx_out else w_in[:, d:])
    pc = pc[..., d:] if ctx_out else pc
    L = h_ctx.shape[1]
    k_c = pc[..., :d].reshape(b, L, nh, hd)
    v_c = pc[..., d:].reshape(b, L, nh, hd)

    row_start = jnp.clip(jnp.arange(rows) - kh // 2, 0, rows - kh)
    cols = jnp.arange(GRID_W)
    col_start = jnp.clip(cols - kw // 2, 0, GRID_W - kw)
    col_in = (cols[None, :] >= col_start[:, None]) & (cols[None, :] < col_start[:, None] + kw)
    dc_idx = jnp.clip(cols[None, :] - cols[:, None] + NAT_WIN_COLS - 1, 0, 2 * NAT_WIN_COLS - 2)
    rpb_f = rpb.astype(jnp.float32)
    band = kh * GRID_W

    def row_block(args):
        q_r, r = args
        start = row_start[r]
        k_band = lax.dynamic_slice_in_dim(k, start, kh, axis=1)
        v_band = lax.dynamic_slice_in_dim(v, start, kh, axis=1)
        dr_idx = start + jnp.arange(kh) - r + NAT_WIN_ROWS - 1
        bias = rpb_f[:, dr_idx[None, :, None], dc_idx[:, None, :]]
        bias = jnp.where(col_in[:, None, :], bias, -jnp.inf)
        s_loc = jnp.einsum('bqhd,bikhd->bhqik', q_r, k_band).astype(jnp.float32) + bias
        s_ctx = jnp.einsum('bqhd,blhd->bhql', q_r, k_c).astype(jnp.float32)
        s = jnp.concatenate([s_loc.reshape(b, nh, GRID_W, band), s_ctx], axis=-1)
        prob = jax.nn.softmax(s, axis=-1).astype(v.dtype)
        p_loc = prob[..., :band].reshape(b, nh, GRID_W, kh, GRID_W)
        return (jnp.einsum('bhqik,bikhd->bqhd', p_loc, v_band)
                + jnp.einsum('bhql,blhd->bqhd', prob[..., band:], v_c))

    o = lax.map(row_block, (jnp.moveaxis(q, 1, 0), jnp.arange(rows)))
    y_lat = jnp.moveaxis(o, 0, 1).reshape(b, n, d) @ w_o

    y_ctx = None
    if ctx_out:
        q_c = pc_q = (h_ctx @ w_in[:, :d]).reshape(b, L, nh, hd) * scale
        s = jnp.einsum('blhd,bmhd->bhlm', q_c, k_c).astype(jnp.float32)
        prob = jax.nn.softmax(s, axis=-1).astype(v_c.dtype)
        y_ctx = jnp.einsum('bhlm,bmhd->blhd', prob, v_c).reshape(b, L, d) @ w_o
    return y_lat, y_ctx

def sq_relu_mlp(h, w1, w2):
    return jnp.square(jax.nn.relu(h @ w1)) @ w2

def first_inputs(seed: int = 0) -> dict:
    key = jax.random.key(seed)
    ks = jax.random.split(key, 17)
    f32 = jnp.float32

    def nrm(k, shape, scale):
        return jax.random.normal(k, shape, f32) * scale

    qk_w = RET_HEADS * RET_QK_DIM
    v_w = RET_HEADS * RET_V_DIM
    base_decay = jnp.log(-jnp.log(1.0 - 2.0 ** (-5.0 - jnp.arange(RET_HEADS, dtype=f32))))
    return {
        'x': nrm(ks[0], (BATCH, SEQ, D_MODEL), 1.0),
        'c': nrm(ks[1], (BATCH, D_MODEL), 1.0),
        'ctx': nrm(ks[2], (BATCH, CTX_LEN, D_MODEL), 1.0),
        'c_ctx': nrm(ks[3], (D_MODEL,), 1.0),
        'ada_w': nrm(ks[4], (DEPTH, D_MODEL, 6 * D_MODEL), 0.5 * D_MODEL ** -0.5),
        'ada_b': nrm(ks[5], (DEPTH, 6 * D_MODEL), 0.02),
        'ret_w_in': nrm(ks[6], (N_RET_LAYERS, D_MODEL, 2 * qk_w + 2 * v_w), D_MODEL ** -0.5),
        'ret_w_o': nrm(ks[7], (N_RET_LAYERS, v_w, D_MODEL), DN_BETA * v_w ** -0.5),
        'ret_decay': base_decay + nrm(ks[8], (N_RET_LAYERS, 2, RET_HEADS), 0.1),
        'nat_w_in': nrm(ks[9], (N_NAT_LAYERS, D_MODEL, 3 * D_MODEL), D_MODEL ** -0.5),
        'nat_w_o': nrm(ks[10], (N_NAT_LAYERS, D_MODEL, D_MODEL), DN_BETA * D_MODEL ** -0.5),
        'nat_rpb': nrm(ks[11], (N_NAT_LAYERS, NAT_HEADS, 2 * NAT_WIN_ROWS - 1, 2 * NAT_WIN_COLS - 1), 0.1),
        'mlp_w1': nrm(ks[12], (DEPTH, D_MODEL, MLP_HIDDEN), D_MODEL ** -0.5),
        'mlp_w2': nrm(ks[13], (DEPTH, MLP_HIDDEN, D_MODEL), DN_BETA * MLP_HIDDEN ** -0.5),
        'ln_g': 1.0 + nrm(ks[14], (DEPTH, 2, D_MODEL), 0.02),
        'ln_b': nrm(ks[15], (DEPTH, 2, D_MODEL), 0.02),
    }

def first_block(x, c, ctx, c_ctx, ada_w, ada_b, ret_w_in, ret_w_o, ret_decay,
              nat_w_in, nat_w_o, nat_rpb, mlp_w1, mlp_w2, ln_g, ln_b):
    n = x.shape[1]
    ang_row, ang_col = axial_rope_angles(n, RET_QK_DIM // 2)
    silu_c = jax.nn.silu(c)
    silu_cc = jax.nn.silu(c_ctx)
    for i in range(DEPTH):
        last = i == DEPTH - 1
        j = i // N_MIXERS
        mod = (silu_c @ ada_w[i] + ada_b[i])[:, None, :]
        mod_c = silu_cc @ ada_w[i] + ada_b[i]
        sh1, sc1, g1, sh2, sc2, g2 = jnp.split(mod, 6, axis=-1)
        sh1c, sc1c, g1c, sh2c, sc2c, g2c = jnp.split(mod_c, 6, axis=-1)

        h = x * (1.0 + sc1) + sh1
        hc = ctx * (1.0 + sc1c) + sh1c
        if i % N_MIXERS == 0:
            y, yc = retention_mixer(h, hc, ret_w_in[j], ret_w_o[j], ret_decay[j],
                                    ang_row, ang_col, not last)
        else:
            y, yc = neighbourhood_mixer(h, hc, nat_w_in[j], nat_w_o[j], nat_rpb[j], not last)

        x = layer_norm(DN_ALPHA * x + g1 * y, ln_g[i, 0], ln_b[i, 0])
        h = x * (1.0 + sc2) + sh2
        x = layer_norm(DN_ALPHA * x + g2 * sq_relu_mlp(h, mlp_w1[i], mlp_w2[i]), ln_g[i, 1], ln_b[i, 1])

        if not last:
            ctx = layer_norm(DN_ALPHA * ctx + g1c * yc, ln_g[i, 0], ln_b[i, 0])
            hc = ctx * (1.0 + sc2c) + sh2c
            ctx = layer_norm(DN_ALPHA * ctx + g2c * sq_relu_mlp(hc, mlp_w1[i], mlp_w2[i]),
                             ln_g[i, 1], ln_b[i, 1])
    return x


PLE_DIM = 256
D_FF = 2752
M_HEADS = 4
M_HEAD_DIM = 256
M_WIDTH = M_HEADS * M_HEAD_DIM
M_CHUNK = 64
CONV_K = 4
A_Q_HEADS = 16
A_KV_HEADS = 4
A_HEAD_DIM = 64
A_GROUP = A_Q_HEADS // A_KV_HEADS
A_WIDTH = A_Q_HEADS * A_HEAD_DIM
A_KV_WIDTH = A_KV_HEADS * A_HEAD_DIM
WINDOW = 128
A_BLOCK = 128
EPS = 1e-6
N_IN = 4 * M_WIDTH + 2 * M_HEADS + A_WIDTH + 2 * A_KV_WIDTH + 2 * D_MODEL


def rmsnorm(x, g):
    xf = x.astype(jnp.float32)
    y = xf * lax.rsqrt(jnp.mean(xf * xf, axis=-1, keepdims=True) + EPS)
    return (y * g.astype(jnp.float32)).astype(x.dtype)

def head_rmsnorm(x, g):
    xf = x.astype(jnp.float32)
    y = xf * lax.rsqrt(jnp.mean(xf * xf, axis=-1, keepdims=True) + EPS)
    return y * g.astype(jnp.float32)

def swiglu(x, w_gate, w_up, w_down):
    return (jax.nn.silu(x @ w_gate) * (x @ w_up)) @ w_down

def causal_dwconv(x, w, b):
    c = x.shape[-1]
    y = lax.conv_general_dilated(x, w[:, None, :].astype(x.dtype), window_strides=(1,),
                                 padding=[(CONV_K - 1, 0)],
                                 dimension_numbers=("NWC", "WIO", "NWC"),
                                 feature_group_count=c)
    return y + b

def mlstm_chunkwise(q, k, v, ig, lf):
    bsz, t, nh, dh = q.shape
    nc = t // M_CHUNK

    def to_chunks(z):
        return z.reshape(bsz, nc, M_CHUNK, nh, dh).transpose(1, 0, 3, 2, 4)

    def g_chunks(z):
        return z.reshape(bsz, nc, M_CHUNK, nh).transpose(1, 0, 3, 2)

    causal = jnp.tril(jnp.ones((M_CHUNK, M_CHUNK), dtype=bool))

    def step(carry, xs):
        c_st, n_st, m_st = carry
        qc, kc, vc, ic, fc = xs
        b = jnp.cumsum(fc, axis=-1)
        dlog = jnp.where(causal, b[..., :, None] - b[..., None, :] + ic[..., None, :], -jnp.inf)
        inter = b + m_st[..., None]
        m_t = jnp.maximum(inter, jnp.max(dlog, axis=-1))
        w_intra = jnp.exp(dlog - m_t[..., None])
        w_inter = jnp.exp(inter - m_t)
        s = jnp.einsum("bhtk,bhsk->bhts", qc, kc) * w_intra
        num = jnp.einsum("bhts,bhsv->bhtv", s, vc) + w_inter[..., None] * jnp.einsum("bhtk,bhvk->bhtv", qc, c_st)
        den = jnp.sum(s, axis=-1) + w_inter * jnp.einsum("bhtk,bhk->bht", qc, n_st)
        h = num / jnp.maximum(jnp.abs(den), jnp.exp(-m_t))[..., None]
        b_last = b[..., -1]
        a = b_last[..., None] - b + ic
        m_new = jnp.maximum(b_last + m_st, jnp.max(a, axis=-1))
        w_state = jnp.exp(a - m_new[..., None])
        decay = jnp.exp(b_last + m_st - m_new)
        c_new = decay[..., None, None] * c_st + jnp.einsum("bhsv,bhsk->bhvk", vc * w_state[..., None], kc)
        n_new = decay[..., None] * n_st + jnp.einsum("bhs,bhsk->bhk", w_state, kc)
        return (c_new, n_new, m_new), h

    init = (jnp.zeros((bsz, nh, dh, dh), jnp.float32),
            jnp.zeros((bsz, nh, dh), jnp.float32),
            jnp.zeros((bsz, nh), jnp.float32))
    xs = (to_chunks(q), to_chunks(k), to_chunks(v), g_chunks(ig), g_chunks(lf))
    _, hs = lax.scan(step, init, xs)
    return hs.transpose(1, 0, 3, 2, 4).reshape(bsz, t, nh, dh)

def swa_gqa_sinks(q, k, v, sinks):
    bsz, t = q.shape[0], q.shape[1]
    nb = t // A_BLOCK
    qb = q.reshape(bsz, nb, A_BLOCK, A_KV_HEADS, A_GROUP, A_HEAD_DIM)

    def windows(z):
        zp = jnp.pad(z, ((0, 0), (A_BLOCK, 0), (0, 0), (0, 0)))
        zb = zp.reshape(bsz, nb + 1, A_BLOCK, A_KV_HEADS, A_HEAD_DIM)
        return jnp.concatenate([zb[:, :-1], zb[:, 1:]], axis=2)

    kw, vw = windows(k), windows(v)
    scores = jnp.einsum("bnqhgd,bnkhd->bnhgqk", qb, kw).astype(jnp.float32) * (A_HEAD_DIM ** -0.5)
    qi = jnp.arange(A_BLOCK)[:, None]
    kj = jnp.arange(2 * A_BLOCK)[None, :]
    rel = A_BLOCK + qi - kj
    band = (rel >= 0) & (rel < WINDOW)
    key_pos = jnp.arange(nb)[:, None, None] * A_BLOCK + kj[None] - A_BLOCK
    valid = band[None] & (key_pos >= 0)
    scores = jnp.where(valid[None, :, None, None], scores, -jnp.inf)
    sink = sinks.astype(jnp.float32).reshape(A_KV_HEADS, A_GROUP)[None, None, :, :, None, None]
    mx = jnp.maximum(jnp.max(scores, axis=-1, keepdims=True), sink)
    pr = jnp.exp(scores - mx)
    den = jnp.sum(pr, axis=-1, keepdims=True) + jnp.exp(sink - mx)
    attn = (pr / den).astype(v.dtype)
    out = jnp.einsum("bnhgqk,bnkhd->bnqhgd", attn, vw)
    return out.reshape(bsz, t, A_WIDTH)

def hybrid_layer(h, p_i, ffn1_norm, ffn1_w_gate, ffn1_w_up, ffn1_w_down, mix_norm, w_in,
                 m_conv_w, m_conv_b, m_igate_b, m_fgate_b, m_out_norm, a_q_norm, a_k_norm,
                 a_sinks, w_branch_m, w_branch_a, w_out, ffn2_norm, ffn2_w_gate, ffn2_w_up,
                 ffn2_w_down, ple_norm, ple_gate_w, ple_proj_w):
    bsz, t, _ = h.shape
    h = h + 0.5 * swiglu(rmsnorm(h, ffn1_norm), ffn1_w_gate, ffn1_w_up, ffn1_w_down)

    u = rmsnorm(h, mix_norm)
    z = u @ w_in
    sizes = [2 * M_WIDTH, M_WIDTH, M_WIDTH, M_HEADS, M_HEADS, A_WIDTH, A_KV_WIDTH, A_KV_WIDTH, D_MODEL, D_MODEL]
    offs = [int(o) for o in np.cumsum(sizes)[:-1]]
    m_qk, m_v, m_o, m_i, m_f, a_q, a_k, a_v, g_m, g_a = jnp.split(z, offs, axis=-1)

    m_qk = jax.nn.silu(causal_dwconv(m_qk, m_conv_w, m_conv_b))
    m_q, m_k = jnp.split(m_qk, 2, axis=-1)
    mq = m_q.astype(jnp.float32).reshape(bsz, t, M_HEADS, M_HEAD_DIM) * (M_HEAD_DIM ** -0.5)
    mk = m_k.astype(jnp.float32).reshape(bsz, t, M_HEADS, M_HEAD_DIM)
    mv = m_v.astype(jnp.float32).reshape(bsz, t, M_HEADS, M_HEAD_DIM)
    ig = m_i.astype(jnp.float32) + m_igate_b.astype(jnp.float32)
    lf = jax.nn.log_sigmoid(m_f.astype(jnp.float32) + m_fgate_b.astype(jnp.float32))
    hm = mlstm_chunkwise(mq, mk, mv, ig, lf)
    hm = head_rmsnorm(hm, m_out_norm.reshape(M_HEADS, M_HEAD_DIM)).reshape(bsz, t, M_WIDTH)
    hm = (jax.nn.sigmoid(m_o.astype(jnp.float32)) * hm).astype(h.dtype)

    aq = head_rmsnorm(a_q.reshape(bsz, t, A_Q_HEADS, A_HEAD_DIM), a_q_norm).astype(h.dtype)
    ak = head_rmsnorm(a_k.reshape(bsz, t, A_KV_HEADS, A_HEAD_DIM), a_k_norm).astype(h.dtype)
    av = a_v.reshape(bsz, t, A_KV_HEADS, A_HEAD_DIM)
    ha = swa_gqa_sinks(aq, ak, av, a_sinks)

    merged = jax.nn.sigmoid(g_m) * (hm @ w_branch_m) + jax.nn.sigmoid(g_a) * (ha @ w_branch_a)
    h = h + merged @ w_out

    h = h + 0.5 * swiglu(rmsnorm(h, ffn2_norm), ffn2_w_gate, ffn2_w_up, ffn2_w_down)

    h = h + jax.nn.sigmoid(rmsnorm(h, ple_norm) @ ple_gate_w) * (p_i @ ple_proj_w)
    return h

def second_inputs(seed: int = 0) -> dict:
    key = jax.random.key(seed)
    ks = jax.random.split(key, 32)

    def w(k, fan_in, fan_out, scale=1.0):
        return jax.random.normal(k, (DEPTH, fan_in, fan_out), jnp.float32) * (scale * fan_in ** -0.5)

    def gain(k, n):
        return 1.0 + 0.05 * jax.random.normal(k, (DEPTH, n), jnp.float32)

    f_bias = jnp.linspace(3.0, 6.0, M_HEADS, dtype=jnp.float32)[None, :] + 0.1 * jax.random.normal(ks[10], (DEPTH, M_HEADS), jnp.float32)
    return {
        "x": jax.random.normal(ks[0], (BATCH, SEQ, D_MODEL), jnp.float32),
        "p": jax.random.normal(ks[1], (DEPTH, BATCH, SEQ, PLE_DIM), jnp.float32),
        "ffn1_norm": gain(ks[2], D_MODEL),
        "ffn1_w_gate": w(ks[3], D_MODEL, D_FF),
        "ffn1_w_up": w(ks[4], D_MODEL, D_FF),
        "ffn1_w_down": w(ks[5], D_FF, D_MODEL, 0.5),
        "mix_norm": gain(ks[6], D_MODEL),
        "w_in": w(ks[7], D_MODEL, N_IN),
        "m_conv_w": jax.random.normal(ks[8], (DEPTH, CONV_K, 2 * M_WIDTH), jnp.float32) * (CONV_K ** -0.5),
        "m_conv_b": 0.02 * jax.random.normal(ks[9], (DEPTH, 2 * M_WIDTH), jnp.float32),
        "m_igate_b": 0.1 * jax.random.normal(ks[11], (DEPTH, M_HEADS), jnp.float32),
        "m_fgate_b": f_bias,
        "m_out_norm": gain(ks[12], M_WIDTH),
        "a_q_norm": gain(ks[13], A_HEAD_DIM),
        "a_k_norm": gain(ks[14], A_HEAD_DIM),
        "a_sinks": 0.5 * jax.random.normal(ks[15], (DEPTH, A_Q_HEADS), jnp.float32),
        "w_branch_m": w(ks[16], M_WIDTH, D_MODEL),
        "w_branch_a": w(ks[17], A_WIDTH, D_MODEL),
        "w_out": w(ks[18], D_MODEL, D_MODEL, 0.5),
        "ffn2_norm": gain(ks[19], D_MODEL),
        "ffn2_w_gate": w(ks[20], D_MODEL, D_FF),
        "ffn2_w_up": w(ks[21], D_MODEL, D_FF),
        "ffn2_w_down": w(ks[22], D_FF, D_MODEL, 0.5),
        "ple_norm": gain(ks[23], D_MODEL),
        "ple_gate_w": w(ks[24], D_MODEL, D_MODEL),
        "ple_proj_w": w(ks[25], PLE_DIM, D_MODEL, 0.5),
    }

def second_block(x, p, ffn1_norm, ffn1_w_gate, ffn1_w_up, ffn1_w_down, mix_norm, w_in,
              m_conv_w, m_conv_b, m_igate_b, m_fgate_b, m_out_norm, a_q_norm, a_k_norm,
              a_sinks, w_branch_m, w_branch_a, w_out, ffn2_norm, ffn2_w_gate, ffn2_w_up,
              ffn2_w_down, ple_norm, ple_gate_w, ple_proj_w):
    h = x
    for i in range(DEPTH):
        h = hybrid_layer(h, p[i], ffn1_norm[i], ffn1_w_gate[i], ffn1_w_up[i], ffn1_w_down[i],
                         mix_norm[i], w_in[i], m_conv_w[i], m_conv_b[i], m_igate_b[i],
                         m_fgate_b[i], m_out_norm[i], a_q_norm[i], a_k_norm[i], a_sinks[i],
                         w_branch_m[i], w_branch_a[i], w_out[i], ffn2_norm[i], ffn2_w_gate[i],
                         ffn2_w_up[i], ffn2_w_down[i], ple_norm[i], ple_gate_w[i], ple_proj_w[i])
    return h


def setup_inputs(seed=0):
    out = dict(first_inputs(seed))
    for name, value in second_inputs(seed + 1).items():
        if name != "x":
            out[name + "_2"] = value
    return out


def reference(
    x, c, ctx, c_ctx, ada_w, ada_b, ret_w_in, ret_w_o, ret_decay, nat_w_in, nat_w_o, nat_rpb,
    mlp_w1, mlp_w2, ln_g, ln_b, p_2, ffn1_norm_2, ffn1_w_gate_2, ffn1_w_up_2, ffn1_w_down_2,
    mix_norm_2, w_in_2, m_conv_w_2, m_conv_b_2, m_igate_b_2, m_fgate_b_2, m_out_norm_2,
    a_q_norm_2, a_k_norm_2, a_sinks_2, w_branch_m_2, w_branch_a_2, w_out_2, ffn2_norm_2,
    ffn2_w_gate_2, ffn2_w_up_2, ffn2_w_down_2, ple_norm_2, ple_gate_w_2, ple_proj_w_2,
):
    x = first_block(
        x, c, ctx, c_ctx, ada_w, ada_b, ret_w_in, ret_w_o, ret_decay, nat_w_in, nat_w_o,
        nat_rpb, mlp_w1, mlp_w2, ln_g, ln_b,
    )
    return second_block(
        x, p_2, ffn1_norm_2, ffn1_w_gate_2, ffn1_w_up_2, ffn1_w_down_2, mix_norm_2, w_in_2,
        m_conv_w_2, m_conv_b_2, m_igate_b_2, m_fgate_b_2, m_out_norm_2, a_q_norm_2, a_k_norm_2,
        a_sinks_2, w_branch_m_2, w_branch_a_2, w_out_2, ffn2_norm_2, ffn2_w_gate_2, ffn2_w_up_2,
        ffn2_w_down_2, ple_norm_2, ple_gate_w_2, ple_proj_w_2,
    )


_drawn_inputs = setup_inputs


def setup_inputs(seed=0):
    import zlib

    import numpy as np

    out = dict(_drawn_inputs(seed))
    spreads = {}
    factors = {'ada_b': 3.061,
     'nat_rpb': 8.0,
     'ffn1_norm_2': 3.969,
     'mix_norm_2': 3.4,
     'm_conv_b_2': 52.312,
     'm_igate_b_2': 200.0,
     'm_out_norm_2': 5.407,
     'a_q_norm_2': 8.0,
     'a_k_norm_2': 8.0,
     'a_sinks_2': 39.318,
     'ffn2_norm_2': 4.056,
     'ple_norm_2': 36.355}
    for name, (base, spread) in spreads.items():
        noise = np.random.default_rng([zlib.crc32(name.encode()), seed]).standard_normal(out[name].shape)
        drawn = base * np.exp(spread * noise) if base else spread * noise
        out[name] = jnp.asarray(drawn.astype(out[name].dtype))
    for name, factor in factors.items():
        out[name] = (out[name] * factor).astype(out[name].dtype)
    return out
```

```python
from contextlib import ExitStack

import numpy as np
import concourse.bass as bass
from concourse import mybir

F32 = mybir.dt.float32
F32R = mybir.dt.float32r
ALU = mybir.AluOpType
ACT = mybir.ActivationFunctionType
AX = mybir.AxisListType.X

P = 128
D = 1024
KT = D // P
T = 256
TT = T // P
BANK = 512
DEPTH = 2
ALPHA = (2.0 * DEPTH) ** 0.25
LN_EPS = 1e-5
EPS = 1e-6
GRID_W = 64
ROWS = T // GRID_W
RET_HEADS = 4
RET_V = 512
NAT_HEADS = 32
NAT_HD = 32
NAT_BIAS_ROWS = 15
NAT_BIAS_COLS = 31
MLP_CHUNKS = 4
D_FF = 2752
FF_TILES = 22
FF_GROUPS = 11
MH = 4
MHD = 256
AH = 16
AKV = 4
AHD = 64
CONV_K = 4
BIG = -1e30
RING = 3
N_LAYER_DMAS = 15
BLOCK = 2048

O_QK, O_V, O_O, O_I, O_AQ, O_AK, O_GM, O_GA = 0, 2048, 3072, 4096, 4104, 5128, 5640, 6664

C_ID, C_ROPE, C_WIN, C_ABS, C_REL, C_MF, C_MB, C_TRI = 0, 128, 264, 328, 712, 1096, 1480, 1864
C_ALL = C_TRI + 384

V_FFN1, V_MIX, V_CW, V_CB, V_MO, V_FFN2, V_PLE, V_AQ, V_AK, V_ROWS = 0, 8, 16, 80, 96, 104, 112, 120, 121, 122

PER_LAYER = {
    "psum_full": 185, "weights_used": 65, "values_done": 8, "act_out": 53, "dve_out": 132, "act_part": 96,
    "dve_part": 26, "act_own": 1, "dve_own": 193, "high_done": 120, "split_done": 120, "x_ready": 1,
    "u_ready": 8, "var_ready": 18, "rstd_dve": 14, "rstd_act": 4, "layer_start": 1, "layer_start_act": 1,
    "layer_start_pool": 1, "row_ready": 1, "conv_done": 1, "squares_used": 6, "raw_in0": 640, "raw_in1": 640,
    "raw_in2": 640, "lay_in": 240,
}


def constants():
    c = np.zeros((P, C_ALL), np.float32)
    p = np.arange(P)
    c[:, C_ID:C_ID + P] = np.eye(P)
    inv = (1.0 / (np.float32(10000.0) ** (np.arange(0, P, 2, dtype=np.float32) / np.float32(P)))).astype(np.float32)
    sign = np.where(p < 64, -1.0, 1.0)[:, None]
    for off, n in ((0, ROWS), (2 * ROWS, GRID_W)):
        ang = (inv[p % 64][:, None] * np.arange(n, dtype=np.float32)[None]).astype(np.float32)
        c[:, C_ROPE + off:C_ROPE + off + n] = np.cos(ang)
        c[:, C_ROPE + off + n:C_ROPE + off + 2 * n] = np.sin(ang) * sign
    q = (GRID_W - 1 - p % GRID_W)[:, None]
    start = np.clip(q - 8, 0, GRID_W - 16)
    kc = np.arange(GRID_W)[None]
    c[:, C_WIN:C_WIN + GRID_W] = np.where((kc >= start) & (kc < start + 16), 0.0, BIG)
    rel = np.arange(384)[None] - 128 - p[:, None]
    c[:, C_ABS:C_ABS + 384] = np.abs(rel)
    c[:, C_REL:C_REL + 384] = rel
    c[:, C_MF:C_MF + 384] = (rel >= 0) / 16.0
    c[:, C_MB:C_MB + 384] = (rel <= 0) / 16.0
    f = np.arange(P)[None]
    c[:, C_TRI:C_TRI + P] = np.where(p[:, None] > f, BIG, 0.0)
    c[:, C_TRI + P:C_TRI + 2 * P] = np.where(f <= p[:, None], BIG, 0.0)
    c[:, C_TRI + 2 * P:C_TRI + 3 * P] = np.where(f > p[:, None], BIG, 0.0)
    return c


class Signal:

    def __init__(self, sem, name, loop, unit=1):
        self.sem, self.name, self.loop, self.unit = sem, name, loop, unit
        self.sent = self.taken = 0

    def up(self):
        self.sent += self.unit
        return self.unit

    def at(self, value):
        assert value > 0, self.name
        i, step = self.loop.get("i"), PER_LAYER.get(self.name, 0)
        return value if i is None or not step else i * step + value

    def now(self):
        return self.at(self.sent)

    def next(self, n=1):
        self.taken += n * self.unit
        return self.at(self.taken)


def build(nc, a, out, upto=99, counts=None):
    loop = {}
    with ExitStack() as ctx:
        def sb(name, shape, dt=F32):
            return ctx.enter_context(nc.sbuf_tensor(name, shape, dt))

        signals = {}

        def signal(name, unit=1):
            signals[name] = Signal(ctx.enter_context(nc.semaphore(name)), name, loop, unit)
            return signals[name]

        psum = ctx.enter_context(nc.psum_tensor("psum", [P, 8, BANK], F32))
        raw = sb("raw", [P, RING, BLOCK])
        wgt_hi = sb("wgt_hi", [P, RING, BLOCK], F32R)
        wgt_lo = sb("wgt_lo", [P, RING, BLOCK], F32R)
        X = sb("X", [P, 4, D])
        xh = sb("xh", [P, KT, 2 * T], F32R)
        xl = sb("xl", [P, KT, 2 * T], F32R)
        yh = sb("yh", [P, 4096], F32R)
        yl = sb("yl", [P, 4096], F32R)
        W = sb("W", [P, 13200])
        cst = sb("cst", [P, 328])
        vt = sb("vt", [P, P])
        mod = sb("mod", [P, DEPTH, 6, KT, 2])
        silc = sb("silc", [P, KT, 2])
        small = sb("small", [P, 352])
        yh_pad, yl_pad = xh[0:P // 2, 5, T:2 * T], xl[0:P // 2, 5, T:2 * T]

        ident = cst[:, C_ID:C_ID + P]
        U = X[:, 2:4, :]

        psum_full = signal("psum_full")
        weights_used = signal("weights_used")
        mod_used = signal("mod_used")
        values_done = signal("values_done")
        act_out = signal("act_out")
        dve_out = signal("dve_out")
        act_part = signal("act_part")
        dve_part = signal("dve_part")
        act_own = signal("act_own")
        dve_own = signal("dve_own")
        pool_own = signal("pool_own")
        high_done = signal("high_done")
        split_done = signal("split_done")
        x_ready = signal("x_ready")
        u_ready = signal("u_ready")
        var_ready = signal("var_ready")
        rstd_dve = signal("rstd_dve")
        rstd_act = signal("rstd_act")
        bias_ready = signal("bias_ready")
        bias_used = signal("bias_used")
        tab_free = signal("tab_free")
        layer_start = signal("layer_start")
        layer_start_act = signal("layer_start_act")
        layer_start_pool = signal("layer_start_pool")
        row_ready = signal("row_ready")
        conv_done = signal("conv_done")
        squares_used = signal("squares_used")
        raw_in = [signal(f"raw_in{s}", 16) for s in range(RING)]
        x_in = signal("x_in", 16)
        decay_in = signal("decay_in", 16)
        tab_in = signal("tab_in", 16)
        tri_in = signal("tri_in", 16)
        out_done = signal("out_done", 16)
        const_in = signal("const_in", 16)
        rows_in = signal("rows_in", 16)
        lay_in = signal("lay_in", 16)
        ln_in = signal("ln_in", 16)
        bias_in = [signal(f"bias_in{s}", 16) for s in range(2)]

        units = {}
        blocks, split_blocks = [], []
        bank = {"next": 0, "last": [None] * 8}
        owned = {"act": 0, "dve": 0}
        freed = {"act": act_out, "dve": dve_out}

        def open_unit(pe, key, owner):
            b = bank["next"]
            while bank["last"][b] and "freed" not in units[bank["last"][b]]:
                b = (b + 1) % 8
            bank["next"] = (b + 1) % 8
            if bank["last"][b]:
                last = units[bank["last"][b]]
                pe.wait_ge(freed[last["owner"]].sem, freed[last["owner"]].at(last["freed"]))
            assert key not in units, key
            units[key] = {"bank": b, "owner": owner}
            bank["last"][b] = key
            return psum[:, b, :]

        def close_unit(key, ins):
            u = units[key]
            owned[u["owner"]] += 1
            u["freed"] = owned[u["owner"]]
            ins.then_inc(psum_full.sem, psum_full.up())
            u["full"] = psum_full.sent
            u["need"] = len(split_blocks)
            u["raw"] = len(blocks)

        def out_of(key):
            return freed[units[key]["owner"]].sem

        def emptied(key):
            return freed[units[key]["owner"]].at(units[key]["freed"])

        def filled(key):
            return psum_full.at(units[key]["full"])

        def bank_of(key):
            return psum[:, units[key]["bank"], :]

        def take_block(pe, source, split=True):
            n, shape = len(blocks), source(0).shape
            slot = n % RING
            raw_in[slot].sent += 16
            blocks.append({"index": n, "source": source, "shape": shape, "size": shape[1] * shape[2], "slot": slot,
                           "landed": raw_in[slot].sent, "release": None})
            view = lambda t, s: t[:, s, :blocks[n]["size"]].rearrange("p (a b) -> p a b", a=shape[1])
            if not split:
                pe.wait_ge(raw_in[slot].sem, raw_in[slot].at(blocks[n]["landed"]))
                return view(raw, slot)
            s = len(split_blocks)
            split_blocks.append({"block": blocks[n], "release": None})
            blocks[n]["release"] = (split_done, s + 1)
            pe.wait_ge(split_done.sem, split_done.at(s + 1))
            return view(wgt_hi, s % RING), view(wgt_lo, s % RING), s

        def release(s, ins=None, key=None):
            if key is None:
                ins.then_inc(weights_used.sem, weights_used.up())
            split_blocks[s]["release"] = (weights_used, weights_used.sent) if key is None else (psum_full, units[key]["full"])

        def wblock(w, k0, kn, c0, cn):
            return lambda i: w[k0 * P:(k0 + kn) * P, c0:c0 + cn].rearrange("(k p) n -> p k n", p=P)

        def lblock(w, k0, kn, c0, cn):
            return lambda i: w[i][k0 * P:(k0 + kn) * P, c0:c0 + cn].rearrange("(k p) n -> p k n", p=P)

        def view(lo, a_, b_):
            return W[:, lo:lo + a_ * b_].rearrange("p (a b) -> p a b", a=a_)

        gate_b, ln_gb = view(0, 2, D), view(2048, 2, D)
        r_tab, r_strip = view(2048, 4, 384), view(3584, 2, 384)
        rq, rk = view(4352, 2, 2 * T), view(5376, 2, 2 * T)
        rv, rg, rs = view(6400, 4, RET_V), view(8448, 4, RET_V), view(10496, 6, T)
        r_exp, r_swap = view(10496, 4, 384), view(12032, 2, T)
        nq, nk, nv = view(0, KT, T), view(2048, KT, 2 * T), view(6144, 4, D)
        n_prob, n_probT, n_bias = view(10240, 2, 512), view(11264, 2, 512), view(12288, 2, 384)
        nat_steps = [(qt, h) for h in range(NAT_HEADS) for qt in range(TT)]
        tri = W[:, 0:384]
        sink, gbias = W[:, 384:400], W[:, 400:408]
        l_rows, l_p = W[:, 512:640], view(640, TT, 256)
        rowv = [W[0:MH, 1152 + 256 * n:1408 + 256 * n] for n in range(8)]
        qk_post, qk_pre = view(3200, 16, T), view(7296, 16, T + 3)
        v_ext = W[:, 7296:7296 + 2 * MH * 257].rearrange("p (s h n) -> p s h n", s=2, h=MH)
        sig_o = view(9352, TT, D)
        m_arg, m_s = view(11440, 2, 384), view(12208, 2, 384)
        sig_g, merged = view(3200, TT, D), view(5248, TT, D)
        qn, kn, kT, av = view(7296, TT, D), view(9344, TT, 512), view(1152, AKV, T), view(2176, TT, 256)
        qT = view(10368, KT, T)
        a_prob = [W[:, 12416:12928], W[:, 2688:3200]]
        a_probT = view(7296, 2, 512)
        f_sil, f_v = view(11440, 2, T), view(11952, 2, T)
        v_ext_ones = v_ext[:, :, :, MHD:MHD + 1]
        a_groups = [(0, range(8 * (g // 2) + g % 2, 8 * (g // 2) + 8, 2)) for g in range(4)] + \
            [(1, range(8 * (g // 4) + g % 4 // 2 + 4 * (g % 2), 8 * (g // 4) + g % 4 // 2 + 4 * (g % 2) + 4, 2)) for g in range(8)]

        def hid(t, n_tok):
            return lambda kt, tt: t[:, kt * n_tok + tt * P:kt * n_tok + (tt + 1) * P]

        def x_op(t):
            return lambda kt, tt: t[:, kt, tt * P:(tt + 1) * P]

        def ff_at(t, x, kt):
            return t[:, kt * T:(kt + 1) * T] if kt < 16 else x[:, kt - 16, T:2 * T]

        seen = {}

        def rows_of(x):
            return x.rearrange("p (r c) -> p r c", c=GRID_W)

        def turned(x):
            return rows_of(x)[:, :, ::-1]

        block = ctx.enter_context(nc.Block())
        start = {}

        @block.tensor
        def _(pe):
            def mm(o, l, r, start_, stop):
                return pe.matmul(o, l, r, start=start_, stop=stop, skip_group_check=True)

            def mm3(o, lh, ll, rh, rl, start_, stop):
                mm(o, lh, rh, start_, False)
                mm(o, lh, rl, False, False)
                return mm(o, ll, rh, False, stop)

            def transposes(key, owner, tiles):
                o = open_unit(pe, key, owner)
                at = 0
                for t in tiles:
                    n, m = t.shape
                    ins = pe.transpose(o[0:m, at:at + n], t, ident[0:n, 0:n])
                    at += n
                close_unit(key, ins)

            def tokens_by_features(name, kts, col0, ncols, tts, oh, ol, owner, mkblock, split_k=None):
                split_k = split_k or [(k, min(4, kts - k)) for k in range(0, kts, 4)]
                for c in range(ncols // BANK):
                    outs = {}
                    for k0, kn_ in split_k:
                        wh, wl, n = take_block(pe, mkblock(k0, kn_, col0 + c * BANK, BANK))
                        for tt in tts:
                            if k0 == 0:
                                outs[tt] = open_unit(pe, (name, c, tt), owner)
                            for k in range(kn_):
                                kt = k0 + k
                                ins = mm3(outs[tt], oh(kt, tt), ol(kt, tt), wh[:, k, :], wl[:, k, :],
                                          kt == 0, kt == kts - 1)
                            if kt == kts - 1:
                                close_unit((name, c, tt), ins)
                        if kt < kts - 1:
                            release(n, ins)
                        else:
                            release(n, key=(name, c, tts[-1]))

            def features_by_tokens(name, col0, ntiles, n_tok, owner, mkblock, base=0):
                for g in range(ntiles // 2):
                    wh, wl, n = take_block(pe, mkblock(0, KT, col0 + g * 2 * P, 2 * P))
                    for j in range(2):
                        key = (name, base + 2 * g + j)
                        o = open_unit(pe, key, owner)
                        for kt in range(KT):
                            ins = mm3(o[:, 0:n_tok], wh[:, kt, j * P:(j + 1) * P], wl[:, kt, j * P:(j + 1) * P],
                                      xh[:, kt, 0:n_tok], xl[:, kt, 0:n_tok], kt == 0, kt == KT - 1)
                        close_unit(key, ins)
                    release(n, key=key)

            def modulation(layer, part):
                key = ("mod", layer, part)
                o = open_unit(pe, key, "dve")
                for g in range(4):
                    w = take_block(pe, wblock(a["ada_w"][layer], 0, KT, part * D + g * 2 * P, 2 * P), split=False)
                    for j in range(2):
                        t = 2 * g + j
                        for kt in range(KT):
                            ins = mm(o[:, 2 * t:2 * t + 2], w[:, kt, j * P:(j + 1) * P], silc[:, kt, :],
                                     kt == 0, kt == KT - 1)
                    if g < 3:
                        ins.then_inc(mod_used.sem, mod_used.up())
                        blocks[-1]["release"] = (mod_used, mod_used.sent)
                close_unit(key, ins)
                blocks[-1]["release"] = (psum_full, units[key]["full"])

            def gates(layer, part, streams):
                pe.wait_ge(out_of(("mod", layer, part)), emptied(("mod", layer, part)))
                for s in range(streams):
                    for c in range(2):
                        key = ("gate", layer, part, s, c)
                        o = open_unit(pe, key, "act")
                        for j in range(4):
                            col = mod[:, layer, part, 4 * c + j, s:s + 1]
                            ins = mm(o[:, j * P:(j + 1) * P], col.to_broadcast([P, P]), ident, True, True)
                        close_unit(key, ins)

            def features_of(name, src, tts):
                per = 4 // len(tts)
                for u in range(KT // per):
                    transposes((name, u), "dve", [src[:, tt, kt * P:(kt + 1) * P]
                                                  for kt in range(per * u, per * u + per) for tt in tts])
                return (name, KT // per - 1)

            def mlp(layer, tts, last):
                n_tok = len(tts) * P
                pe.wait_ge(out_of(last), emptied(last))
                for c in range(MLP_CHUNKS):
                    features_by_tokens(("up", layer), c * D, KT, n_tok, "dve",
                                       lambda *k: wblock(a["mlp_w1"][layer], *k), base=c * KT)
                    pe.wait_ge(out_of((("up", layer), c * KT + KT - 1)), emptied((("up", layer), c * KT + KT - 1)))
                    tokens_by_features(("down", layer, c), KT, 0, D, tts, hid(yh, n_tok), hid(yl, n_tok), "dve",
                                       lambda k0, kn_, c0, cn: wblock(a["mlp_w2"][layer], c * KT + k0, kn_, c0, cn))

            pe.wait_ge(const_in.sem, const_in.at(16))
            pe.wait_ge(rows_in.sem, rows_in.at(16 * 4))
            transposes(("vec",), "dve", [W[0:112, 0:P]])
            pe.wait_ge(act_part.sem, act_part.at(1))
            pe.wait_ge(out_of(("vec",)), emptied(("vec",)))
            modulation(0, 0)
            modulation(0, 1)
            pe.wait_ge(x_in.sem, x_in.at(32))
            last = features_of("h0", X, range(4))
            modulation(0, 2)
            gates(0, 2, 2)

            pe.wait_ge(out_of(last), emptied(last))
            wb = lambda *k: wblock(a["ret_w_in"][0], *k)
            for h in range(RET_HEADS):
                features_by_tokens(("rq", h), h * T, 2, 2 * T, "dve", wb)
                features_by_tokens(("rk", h), D + h * T, 2, 2 * T, "dve", wb)
                tokens_by_features(("rv", h), KT, 2 * D + h * RET_V, RET_V, range(4), x_op(xh), x_op(xl), "act", wb)
                pe.wait_ge(out_of((("rk", h), 1)), emptied((("rk", h), 1)))
                for s in range(4):
                    n = T if s < 2 else 2 * T
                    o = open_unit(pe, ("rs", h, s), "dve")
                    for d in range(2):
                        ins = mm(o[:, 0:n], rk[:, d, s * P:(s + 1) * P], rq[:, d, 0:n], d == 0, d == 1)
                    close_unit(("rs", h, s), ins)
                tokens_by_features(("rg", h), KT, 4 * D + h * RET_V, RET_V, range(4), x_op(xh), x_op(xl), "act", wb)
                pe.wait_ge(out_of(("rs", h, 3)), emptied(("rs", h, 3)))
                pe.wait_ge(out_of((("rv", h), 0, 3)), emptied((("rv", h), 0, 3)))
                for tt in range(4):
                    o = open_unit(pe, ("ro", h, tt), "dve")
                    if tt < 2:
                        pairs = [(s, rs[:, s, tt * P:(tt + 1) * P]) for s in range(4)]
                    else:
                        pairs = [(s, rs[:, s + 2, (tt - 2) * P:(tt - 1) * P]) for s in (2, 3)]
                    for n, (s, l) in enumerate(pairs):
                        ins = mm(o, l, rv[:, s, :], n == 0, n == len(pairs) - 1)
                    close_unit(("ro", h, tt), ins)
                pe.wait_ge(x_ready.sem, x_ready.next(4))
                for f in range(4):
                    transposes(("ron", h, f), "dve", [rg[:, tt, f * P:(f + 1) * P] for tt in range(4)])
                pe.wait_ge(out_of(("ron", h, 3)), emptied(("ron", h, 3)))
                tokens_by_features(("ry", h), 4, 0, D, range(4), hid(yh, 2 * T), hid(yl, 2 * T), "dve",
                                   lambda k0, kn_, c0, cn: wblock(a["ret_w_o"][0], 4 * h + k0, kn_, c0, cn))
            for part in (3, 4, 5):
                modulation(0, part)
            pe.wait_ge(x_ready.sem, x_ready.next(4))
            last = features_of("h0m", X, range(4))
            gates(0, 5, 2)
            mlp(0, range(4), last)
            for part in (0, 1, 2):
                modulation(1, part)

            pe.wait_ge(x_ready.sem, x_ready.next(4))
            last = features_of("h1", X, range(4))
            wb = lambda *k: wblock(a["nat_w_in"][0], *k)
            pe.wait_ge(out_of(last), emptied(last))
            features_by_tokens("nq", 0, KT, T, "act", wb)
            features_by_tokens("nk", D, KT, 2 * T, "act", wb)
            tokens_by_features("nv", KT, 2 * D, D, range(4), x_op(xh), x_op(xl), "act", wb)
            pe.wait_ge(out_of(("nv", 1, 3)), emptied(("nv", 1, 3)))

            def nat_scores(n):
                qt, h = nat_steps[n]
                p0 = NAT_HD * (h % 4)
                o = open_unit(pe, ("ns", n), "act")
                close_unit(("ns", n), mm(o, nq[p0:p0 + NAT_HD, h // 4, qt * P:(qt + 1) * P],
                                         nk[p0:p0 + NAT_HD, h // 4, :], True, True))

            def nat_transposes(n):
                pe.wait_ge(out_of(("ns", n)), emptied(("ns", n)))
                transposes(("nt", n), "dve" if n % 2 else "act", [n_prob[:, n % 2, s * P:(s + 1) * P] for s in range(4)])

            def nat_values(n):
                qt, h = nat_steps[n]
                key = ("no", qt, h // 16)
                if h % 16 == 0:
                    open_unit(pe, key, "dve")
                o = psum[:, units[key]["bank"], :]
                pe.wait_ge(out_of(("nt", n)), emptied(("nt", n)))
                c = (h % 16) * NAT_HD
                for s in range(4):
                    ins = mm(o[:, c:c + NAT_HD], n_probT[:, n % 2, s * P:(s + 1) * P],
                             nv[:, s, h * NAT_HD:(h + 1) * NAT_HD], s == 0, s == 3)
                if h % 16 == 15:
                    close_unit(key, ins)
                    seen["n", n] = (psum_full, units[key]["full"])
                else:
                    ins.then_inc(values_done.sem, values_done.up())
                    seen["n", n] = (values_done, values_done.sent)

            n_steps = len(nat_steps)
            for n in range(n_steps + 2):
                if n < n_steps:
                    nat_scores(n)
                if 1 <= n <= n_steps:
                    nat_transposes(n - 1)
                if n >= 2:
                    nat_values(n - 2)
            pe.wait_ge(out_of(("no", 1, 1)), emptied(("no", 1, 1)))
            last = features_of("noT", U, range(2))
            gates(1, 2, 1)
            pe.wait_ge(out_of(last), emptied(last))
            tokens_by_features("ny", KT, 0, D, range(2), hid(yh, T), hid(yl, T), "dve", lambda *k: wblock(a["nat_w_o"][0], *k))
            for part in (3, 4, 5):
                modulation(1, part)
            pe.wait_ge(x_ready.sem, x_ready.next(2))
            last = features_of("h1m", X, range(2))
            gates(1, 5, 1)
            mlp(1, range(2), last)
            start["pe"] = {n: s_.sent for n, s_ in signals.items()}
            start.update(units=len(units), blocks=len(blocks), split=len(split_blocks), owned=dict(owned))
            if upto < 1:
                return

            def normed(name):
                pe.wait_ge(u_ready.sem, u_ready.next(2))
                return features_of(name, U, range(2))

            def feed_forward(n, last):
                pe.wait_ge(out_of(last), emptied(last))
                gate, up, down = (a[f"ffn{n}_w_{x}_2"] for x in ("gate", "up", "down"))
                for g in range(FF_GROUPS):
                    cn, at = (2 * P, P) if g < FF_GROUPS - 1 else (D_FF - 2 * P * g, P // 2)
                    outs = {}
                    for half, w in ((0, gate), (1, up)):
                        wh, wl, s = take_block(pe, lblock(w, 0, KT, g * 2 * P, cn))
                        for j in range(2):
                            key = ("ff", n, 2 * g + j)
                            if half == 0:
                                outs[j] = open_unit(pe, key, "dve")
                            for kt in range(KT):
                                ins = mm3(outs[j][:, half * T:(half + 1) * T], wh[:, kt, j * at:j * at + P],
                                          wl[:, kt, j * at:j * at + P], xh[:, kt, 0:T], xl[:, kt, 0:T],
                                          kt == 0, kt == KT - 1)
                            if half:
                                close_unit(key, ins)
                        if half == 0:
                            release(s, ins)
                        else:
                            release(s, key=key)
                pe.wait_ge(out_of(("ff", n, FF_TILES - 1)), emptied(("ff", n, FF_TILES - 1)))

                def rows(k0, kn_, c0, cn):
                    r0 = k0 * P if k0 < FF_TILES - 1 else D_FF - P
                    return lambda i: down[i][r0:r0 + kn_ * P, c0:c0 + cn].rearrange("(k p) n -> p k n", p=P)

                op = lambda t, x: lambda kt, tt: ff_at(t, x, kt)[:, tt * P:(tt + 1) * P]
                tokens_by_features(("fd", n), FF_TILES, 0, D, range(2), op(yh, xh), op(yl, xl), "dve", rows,
                                   [(0, 4), (4, 4), (8, 4), (12, 4), (16, 4), (20, 1), (21, 1)])

            def hybrid_layer():
                pe.wait_ge(lay_in.sem, lay_in.at(16 * N_LAYER_DMAS))
                transposes(("lvec",), "act", [l_rows[0:V_ROWS, :]])
                feed_forward(1, normed("f1"))
                w = a["w_in_2"]
                wb = lambda *k: lblock(w, *k)
                last = normed("mx")
                pe.wait_ge(out_of(last), emptied(last))
                for g in range(8):
                    wh, wl, s = take_block(pe, wb(0, KT, O_QK + g * 2 * P, 2 * P))
                    o = open_unit(pe, ("mqk", g), "act")
                    for j in range(2):
                        for kt in range(KT):
                            ins = mm3(o[:, j * T:(j + 1) * T], wh[:, kt, j * P:(j + 1) * P], wl[:, kt, j * P:(j + 1) * P],
                                      xh[:, kt, 0:T], xl[:, kt, 0:T], kt == 0, kt == KT - 1)
                    close_unit(("mqk", g), ins)
                    release(s, key=("mqk", g))
                wh, wl, s = take_block(pe, wb(0, KT, O_I, 2 * MH))
                o = open_unit(pe, ("mif",), "dve")
                for tt in range(TT):
                    for kt in range(KT):
                        ins = mm3(o[:, tt * 8:tt * 8 + 8], xh[:, kt, tt * P:(tt + 1) * P], xl[:, kt, tt * P:(tt + 1) * P],
                                  wh[:, kt, :], wl[:, kt, :], kt == 0, kt == KT - 1)
                close_unit(("mif",), ins)
                release(s, key=("mif",))
                tokens_by_features("mv", KT, O_V, D, range(2), x_op(xh), x_op(xl), "act", wb)
                pe.wait_ge(out_of(("mif",)), emptied(("mif",)))
                g8 = small[:, 64:80].rearrange("p (t g) -> p t g", t=TT)
                transposes(("mifT",), "dve", [g8[:, tt, c:c + MH] for c in (0, MH) for tt in range(TT)])
                tokens_by_features("mo", KT, O_O, D, range(2), x_op(xh), x_op(xl), "act", wb)
                pe.wait_ge(x_ready.sem, x_ready.next())
                pe.wait_ge(row_ready.sem, row_ready.next())
                o = open_unit(pe, ("mcol",), "dve")
                for n in range(4):
                    ins = mm(o[:, MH * n:MH * (n + 1)], rowv[4 if n < 2 else 7][:, (n % 2) * P:(n % 2 + 1) * P],
                             ident[0:MH, 0:MH], True, True)
                close_unit(("mcol",), ins)

                def mscores(h):
                    o = open_unit(pe, ("mb", h), "dve")
                    close_unit(("mb", h), mm(o[:, 0:T], ident[0:MH, h:h + 1].to_broadcast([MH, P]), rowv[6], True, True))
                    if h == 0:
                        pe.wait_ge(conv_done.sem, conv_done.next())
                    o = open_unit(pe, ("ms", h), "dve")
                    for lo, s, t0 in ((0, 0, 0), (T, 1, P)):
                        for d in range(2):
                            ins = mm(o[:, lo:lo + T - t0], qk_post[:, 8 + 2 * h + d, s * P:(s + 1) * P],
                                     qk_post[:, 2 * h + d, t0:T], d == 0, d == 1)
                    close_unit(("ms", h), ins)

                def mvalues(h):
                    pe.wait_ge(out_of(("ms", h)), emptied(("ms", h)))
                    if h == 0:
                        pe.wait_ge(out_of(("mv", 1, 1)), emptied(("mv", 1, 1)))
                    for tt in range(TT):
                        o = open_unit(pe, ("mn", h, tt), "dve")
                        for n, lo in enumerate((0,) if tt == 0 else (P, T)):
                            ins = mm(o[:, 0:MHD + 1], m_s[:, h % 2, lo:lo + P], v_ext[:, n, h, :], n == 0, n == tt)
                        close_unit(("mn", h, tt), ins)

                for h in range(MH + 1):
                    if h < MH:
                        mscores(h)
                    if h:
                        mvalues(h - 1)
                tokens_by_features("gm", KT, O_GM, D, range(2), x_op(xh), x_op(xl), "act", wb)
                pe.wait_ge(out_of(("mn", MH - 1, 1)), emptied(("mn", MH - 1, 1)))
                last = features_of("hmT", U, range(2))
                pe.wait_ge(out_of(last), emptied(last))
                tokens_by_features("bm", KT, 0, D, range(2), hid(yh, T), hid(yl, T), "dve",
                                   lambda *k: lblock(a["w_branch_m_2"], *k))
                tokens_by_features("aq", KT, O_AQ, D, range(2), x_op(xh), x_op(xl), "dve", wb)
                tokens_by_features("ak", KT, O_AK, BANK, range(2), x_op(xh), x_op(xl), "dve", wb)
                tokens_by_features("ga", KT, O_GA, D, range(2), x_op(xh), x_op(xl), "act", wb)
                pe.wait_ge(out_of(("aq", 1, 1)), emptied(("aq", 1, 1)))
                for u in range(4):
                    transposes(("qT", u), "act", [qn[:, tt, kt * P:(kt + 1) * P] for kt in (2 * u, 2 * u + 1) for tt in range(TT)])
                pe.wait_ge(out_of(("ak", 0, 1)), emptied(("ak", 0, 1)))
                for u in range(2):
                    transposes(("kT", u), "act", [kn[:, tt, j * P:(j + 1) * P] for j in (2 * u, 2 * u + 1) for tt in range(TT)])
                pe.wait_ge(out_of(("kT", 1)), emptied(("kT", 1)))

                def ascores(n):
                    qt, heads = a_groups[n]
                    o = open_unit(pe, ("as", n), "act")
                    w_ = BANK // len(heads)
                    for j, h in enumerate(heads):
                        p0 = AHD * (h % 2)
                        ins = mm(o[:, j * w_:(j + 1) * w_], qT[p0:p0 + AHD, h // 2, qt * P:(qt + 1) * P],
                                 kT[p0:p0 + AHD, h // 4, 0:w_], True, True)
                    close_unit(("as", n), ins)

                def atransposes(n):
                    pe.wait_ge(out_of(("as", n)), emptied(("as", n)))
                    transposes(("at", n), "act" if n % 2 else "dve", [a_prob[n % 2][:, s * P:(s + 1) * P] for s in range(4)])

                def avalues(n):
                    qt, heads = a_groups[n]
                    per = 2 if qt == 0 else 4
                    m = n if qt == 0 else n - 4
                    key = ("ao", qt, m // per)
                    if m % per == 0:
                        open_unit(pe, key, "dve")
                    o = psum[:, units[key]["bank"], :]
                    pe.wait_ge(out_of(("at", n)), emptied(("at", n)))
                    for j, h in enumerate(heads):
                        c = (h % 8) * AHD
                        for s in range(qt + 1):
                            at = (j * (qt + 1) + s) * P
                            ins = mm(o[:, c:c + AHD], a_probT[:, n % 2, at:at + P],
                                     av[:, s, (h // 4) * AHD:(h // 4 + 1) * AHD], s == 0, s == qt)
                    if m % per == per - 1:
                        close_unit(key, ins)
                        seen["a", n] = (psum_full, units[key]["full"])
                    else:
                        ins.then_inc(values_done.sem, values_done.up())
                    seen["a", n] = (values_done, values_done.sent)

                for n in range(len(a_groups) + 2):
                    if n < len(a_groups):
                        ascores(n)
                    if 1 <= n <= len(a_groups):
                        atransposes(n - 1)
                    if n >= 2:
                        avalues(n - 2)
                pe.wait_ge(out_of(("ao", 1, 1)), emptied(("ao", 1, 1)))
                last = features_of("haT", U, range(2))
                pe.wait_ge(out_of(last), emptied(last))
                tokens_by_features("ba", KT, 0, D, range(2), hid(yh, T), hid(yl, T), "dve",
                                   lambda *k: lblock(a["w_branch_a_2"], *k))
                pe.wait_ge(out_of(("ba", 1, 1)), emptied(("ba", 1, 1)))
                last = features_of("mg", merged, range(2))
                pe.wait_ge(out_of(last), emptied(last))
                tokens_by_features("wo", KT, 0, D, range(2), x_op(xh), x_op(xl), "dve",
                                   lambda *k: lblock(a["w_out_2"], *k))
                feed_forward(2, normed("f2"))
                last = normed("pl")
                transposes(("pT",), "dve", [l_p[:, tt, kt * P:(kt + 1) * P] for kt in range(2) for tt in range(TT)])
                pe.wait_ge(out_of(last), emptied(last))
                tokens_by_features("pg", KT, 0, D, range(2), x_op(xh), x_op(xl), "act",
                                   lambda *k: lblock(a["ple_gate_w_2"], *k))
                pe.wait_ge(out_of(("pT",)), emptied(("pT",)))
                wh, wl, s = take_block(pe, lblock(a["ple_proj_w_2"], 0, 2, 0, D))
                for c in range(2):
                    for tt in range(TT):
                        o = open_unit(pe, ("pp", c, tt), "dve")
                        for kt in range(2):
                            ins = mm3(o, hid(yh, T)(kt, tt), hid(yl, T)(kt, tt), wh[:, kt, c * BANK:(c + 1) * BANK],
                                      wl[:, kt, c * BANK:(c + 1) * BANK], kt == 0, kt == 1)
                        close_unit(("pp", c, tt), ins)
                release(s, key=("pp", 1, 1))

            with pe.Fori(0, DEPTH) as i:
                loop["i"] = i
                pe.wait_ge(act_out.sem, act_out.at(owned["act"]))
                pe.wait_ge(dve_out.sem, dve_out.at(owned["dve"]))
                pe.wait_ge(layer_start.sem, layer_start.next())
                bank["next"], bank["last"] = 0, [None] * 8
                hybrid_layer()
            loop["i"] = None

        @block.scalar
        def _(act):
            def act_(o, i, f=ACT.Copy, **k):
                return nc.scalar.activation(o, i, f, **k)

            def operand(key, dst, affine=()):
                act.wait_ge(psum_full.sem, filled(key))
                o = bank_of(key)
                for n, (c, sc, sh) in enumerate(affine):
                    ins = act_(o[:, c[0]:c[1]], o[:, c[0]:c[1]], ACT.Identity, scale=sc, bias=sh)
                if affine:
                    ins.then_inc(act_own.sem, act_own.up())
                    act.wait_ge(act_own.sem, act_own.now())
                act_(dst, o[:, 0:int(np.prod(dst.shape[1:]))]).then_inc(act_part.sem, act_part.up())

            def operand_x(name, layer, part, streams):
                dve_owner = ("mod", layer, part + 1)
                act.wait_ge(out_of(dve_owner), emptied(dve_owner))
                for kt in range(KT):
                    m = lambda j, s: mod[:, layer, part + j, kt, s:s + 1]
                    if streams == 2:
                        operand((name, kt), xh[:, kt, :],
                                [((s * T, (s + 1) * T), m(1, s), m(0, s)) for s in range(2)])
                    elif kt % 2:
                        k0 = kt - 1
                        operand((name, kt // 2), xh[:, k0:k0 + 2, 0:T],
                                [((j * T, (j + 1) * T), mod[:, layer, part + 1, k0 + j, 0:1],
                                  mod[:, layer, part, k0 + j, 0:1]) for j in range(2)])

            def gates(layer, part, streams):
                for s in range(streams):
                    for c in range(2):
                        act.wait_ge(psum_full.sem, filled(("gate", layer, part, s, c)))
                        o = bank_of(("gate", layer, part, s, c))
                        act_(gate_b[:, s, c * BANK:(c + 1) * BANK], o).then_inc(act_out.sem, act_out.up())

            def mlp(layer, tts):
                n = len(tts) * P
                for t in range(MLP_CHUNKS * KT):
                    kt = t % KT
                    act.wait_ge(psum_full.sem, filled((("up", layer), t)))
                    o = bank_of((("up", layer), t))[:, 0:n]
                    act_(o, o, ACT.Relu).then_inc(act_own.sem, act_own.up())
                    act.wait_ge(act_own.sem, act_own.now())
                    act_(o, o, ACT.Square).then_inc(act_own.sem, act_own.up())
                    act.wait_ge(act_own.sem, act_own.now())
                    act_(yh[:, kt * n:(kt + 1) * n], o).then_inc(act_part.sem, act_part.up())

            for r, x, n in ((0, a["c"], 8), (8, a["c_ctx"].unsqueeze(0), 8), (16, a["ada_b"][0:1], 48), (64, a["ada_b"][1:2], 48)):
                act.dma_start(W[r:r + n, 0:P], x.rearrange("a (r n) -> (a r) n", n=P)).then_inc(rows_in.sem, rows_in.up())
            act.dma_start(cst[:, :], a["consts"][:, 0:328]).then_inc(const_in.sem, const_in.up())
            act.dma_start(small[:, 0:8], a["ret_decay"].rearrange("a b h -> a (b h)").to_broadcast([P, 8])).then_inc(decay_in.sem, decay_in.up())
            act.dma_start(X[:, 0:TT, :], a["x"][0].rearrange("(t p) n -> p t n", p=P)).then_inc(x_in.sem, x_in.up())
            act.dma_start(X[:, TT:2 * TT, :], a["ctx"][0].rearrange("(t p) n -> p t n", p=P)).then_inc(x_in.sem, x_in.up())
            act.dma_start(r_tab, a["consts"][:, C_ABS:C_ABS + 1536].rearrange("p (a b) -> p a b", a=4)).then_inc(tab_in.sem, tab_in.up())
            act.wait_ge(psum_full.sem, filled(("vec",)))
            o = bank_of(("vec",))
            act_(silc[:, :, :], o[:, 0:16].rearrange("p (s k) -> p k s", s=2), ACT.Silu).then_inc(act_part.sem, act_part.up())
            act.wait_ge(decay_in.sem, decay_in.at(16))
            act_(small[:, 8:16], small[:, 0:8], ACT.Exp).then_inc(act_part.sem, act_part.up())
            operand_x("h0", 0, 0, 2)
            gates(0, 2, 2)

            for h in range(RET_HEADS):
                if h == 0:
                    act.wait_ge(dve_part.sem, dve_part.next())
                    act.wait_ge(tab_in.sem, tab_in.at(16))
                f, b = small[:, 16 + h:17 + h], small[:, 20 + h:21 + h]
                b_pos = small[:, 12 + h:13 + h]
                f256, b256 = small[:, 24 + h:25 + h], small[:, 28 + h:29 + h]
                act_(r_exp[:, 0, :], r_tab[:, 0, :], ACT.Exp, scale=f)
                act_(r_exp[:, 1, :], r_tab[:, 0, :], ACT.Exp, scale=b)
                act_(r_exp[:, 2, :], r_tab[:, 1, :], ACT.Exp, scale=f, bias=f256)
                act_(r_exp[:, 3, :], r_tab[:, 1, :], ACT.Exp, scale=b_pos, bias=b256).then_inc(act_part.sem, act_part.up())
                for name, dst in (("rq", rq), ("rk", rk)):
                    for d in range(2):
                        key = ((name, h), d)
                        act.wait_ge(psum_full.sem, filled(key))
                        o = bank_of(key)
                        prev = (("rq", h), d) if name == "rk" else (("rk", h - 1), d)
                        if prev in units:
                            act.wait_ge(out_of(prev), emptied(prev))
                        sw = r_swap[:, d, :]
                        act_(sw[0:64, :], o[64:128, 0:T])
                        act_(sw[64:128, :], o[0:64, 0:T])
                        act_(dst[:, d, T:2 * T], o[:, T:2 * T]).then_inc(act_part.sem, act_part.up())
                for tt in range(4):
                    act.wait_ge(psum_full.sem, filled((("rv", h), 0, tt)))
                    act_(rv[:, tt, :], bank_of((("rv", h), 0, tt))).then_inc(act_out.sem, act_out.up())
                for tt in range(4):
                    act.wait_ge(psum_full.sem, filled((("rg", h), 0, tt)))
                    act_(rg[:, tt, :], bank_of((("rg", h), 0, tt)), ACT.Silu).then_inc(act_out.sem, act_out.up())
                for ft in range(4):
                    operand(("ron", h, ft), yh[:, ft * 2 * T:(ft + 1) * 2 * T])

            operand_x("h0m", 0, 3, 2)
            gates(0, 5, 2)
            mlp(0, range(4))

            operand_x("h1", 1, 0, 2)
            for t in range(KT):
                act.wait_ge(psum_full.sem, filled(("nq", t)))
                act_(rows_of(nq[:, t, :]), turned(bank_of(("nq", t))[:, 0:T]), scale=NAT_HD ** -0.5).then_inc(act_out.sem, act_out.up())
            for t in range(KT):
                act.wait_ge(psum_full.sem, filled(("nk", t)))
                act_(nk[:, t, :], bank_of(("nk", t))).then_inc(act_out.sem, act_out.up())
            for c in range(2):
                for tt in range(4):
                    act.wait_ge(psum_full.sem, filled(("nv", c, tt)))
                    act_(nv[:, tt, c * BANK:(c + 1) * BANK], bank_of(("nv", c, tt))).then_inc(act_out.sem, act_out.up())
            n_steps = len(nat_steps)
            for n in range(n_steps + 1):
                if n < n_steps:
                    qt, h = nat_steps[n]
                    c = 32 * qt + h
                    act.wait_ge(dve_part.sem, dve_part.next())
                    if n >= 2:
                        act.wait_ge(psum_full.sem, psum_full.at(units[("nt", n - 2)]["full"]))
                    o = psum[:, units[("ns", n)]["bank"], :]
                    act_(n_prob[:, n % 2, :], o, ACT.Exp, bias=small[:, 192 + c:193 + c],
                                      accum_out=small[:, 256 + c:257 + c]).then_inc(act_out.sem, act_out.up())
                if n >= 1 and units[("nt", n - 1)]["owner"] == "act":
                    act.wait_ge(psum_full.sem, filled(("nt", n - 1)))
                    o = bank_of(("nt", n - 1))
                    if n >= 3:
                        s_, v_ = seen["n", n - 3]
                        act.wait_ge(s_.sem, s_.at(v_))
                    act_(n_probT[:, (n - 1) % 2, :], o).then_inc(act_out.sem, act_out.up())
            for u in range(4):
                act.wait_ge(psum_full.sem, filled(("noT", u)))
                act_(rows_of(yh[:, u * 512:(u + 1) * 512]), turned(bank_of(("noT", u)))).then_inc(act_part.sem, act_part.up())
            gates(1, 2, 1)
            operand_x("h1m", 1, 3, 1)
            gates(1, 5, 1)
            mlp(1, range(2))
            if upto < 1:
                return

            def normed(name, col, final):
                if final is not None:
                    act.wait_ge(out_of(final), emptied(final))
                for tt in range(TT):
                    ins = act_(U[:, tt, :], X[:, tt, :], ACT.Square, accum_out=small[:, 80 + tt:81 + tt])
                ins.then_inc(act_part.sem, act_part.up())
                act.wait_ge(rstd_act.sem, rstd_act.next())
                for tt in range(TT):
                    act_(U[:, tt, :], X[:, tt, :], scale=small[:, 84 + tt:85 + tt]).then_inc(u_ready.sem, u_ready.up())
                for u in range(4):
                    act.wait_ge(psum_full.sem, filled((name, u)))
                    o = bank_of((name, u))
                    for j in range(2):
                        ins = act_(xh[:, 2 * u + j, 0:T], o[:, j * T:(j + 1) * T], scale=vt[:, col + 2 * u + j:col + 2 * u + j + 1])
                    ins.then_inc(act_part.sem, act_part.up())

            def feed_forward(n):
                for t in range(FF_TILES):
                    act.wait_ge(psum_full.sem, filled(("ff", n, t)))
                    o = bank_of(("ff", n, t))
                    if t >= 2:
                        act.wait_ge(out_of(("ff", n, t - 2)), emptied(("ff", n, t - 2)))
                    act_(f_sil[:, t % 2, :], o[:, 0:T], ACT.Silu).then_inc(act_part.sem, act_part.up())

            def hybrid_layer():
                act.wait_ge(psum_full.sem, filled(("lvec",)))
                act_(vt[:, 0:V_ROWS], bank_of(("lvec",))[:, 0:V_ROWS]).then_inc(act_out.sem, act_out.up())
                act.wait_ge(out_of(("lvec",)), emptied(("lvec",)))
                normed("f1", V_FFN1, None)
                feed_forward(1)
                normed("mx", V_MIX, (("fd", 1), 1, 1))
                for g in range(8):
                    act.wait_ge(psum_full.sem, filled(("mqk", g)))
                    o = bank_of(("mqk", g))
                    act_(qk_pre[:, 2 * g:2 * g + 2, 3:T + 3], o.rearrange("p (j t) -> p j t", j=2)).then_inc(act_out.sem, act_out.up())
                for g in range(4):
                    act.wait_ge(dve_part.sem, dve_part.next())
                    ins = act_(qk_post[:, 4 * g:4 * g + 4, :], qk_post[:, 4 * g:4 * g + 4, :], ACT.Silu)
                ins.then_inc(conv_done.sem, conv_done.up())
                for c in range(2):
                    for tt in range(TT):
                        act.wait_ge(psum_full.sem, filled(("mv", c, tt)))
                        o = bank_of(("mv", c, tt)).rearrange("p (h n) -> p h n", h=2)
                        act_(v_ext[:, tt, 2 * c:2 * c + 2, 0:MHD], o).then_inc(act_out.sem, act_out.up())
                act.wait_ge(dve_part.sem, dve_part.next())
                act_(rowv[2], rowv[2], ACT.Exp).then_inc(act_own.sem, act_own.up())
                act.wait_ge(act_own.sem, act_own.now())
                act_(rowv[2], rowv[2], ACT.Ln, bias=1.0).then_inc(act_part.sem, act_part.up())
                act.wait_ge(dve_part.sem, dve_part.next())
                act_(rowv[7], rowv[5], ACT.Exp, scale=-1.0).then_inc(row_ready.sem, row_ready.up())
                for c in range(2):
                    for tt in range(TT):
                        act.wait_ge(psum_full.sem, filled(("mo", c, tt)))
                        act_(sig_o[:, tt, c * BANK:(c + 1) * BANK], bank_of(("mo", c, tt)), ACT.Sigmoid).then_inc(act_out.sem, act_out.up())
                for h in range(MH + 1):
                    if h < MH:
                        act.wait_ge(out_of(("mb", h)), emptied(("mb", h)))
                        act_(m_arg[:, h % 2, :], m_arg[:, h % 2, :], ACT.Exp).then_inc(act_part.sem, act_part.up())
                    if h:
                        for tt in range(TT):
                            act.wait_ge(psum_full.sem, filled(("mn", h - 1, tt)))
                            o = bank_of(("mn", h - 1, tt))
                            act.wait_ge(dve_part.sem, dve_part.next())
                            act_(U[:, tt, (h - 1) * MHD:h * MHD], o[:, 0:MHD], ACT.Square, scale=small[:, 88:89],
                                               accum_out=small[:, 89:90]).then_inc(act_part.sem, act_part.up())
                for c in range(2):
                    for tt in range(TT):
                        act.wait_ge(psum_full.sem, filled(("gm", c, tt)))
                        act_(sig_g[:, tt, c * BANK:(c + 1) * BANK], bank_of(("gm", c, tt)), ACT.Sigmoid).then_inc(act_out.sem, act_out.up())
                for u in range(4):
                    act.wait_ge(psum_full.sem, filled(("hmT", u)))
                    o = bank_of(("hmT", u))
                    for j in range(2):
                        ins = act_(yh[:, (2 * u + j) * T:(2 * u + j + 1) * T], o[:, j * T:(j + 1) * T],
                                   scale=vt[:, V_MO + 2 * u + j:V_MO + 2 * u + j + 1])
                    ins.then_inc(act_part.sem, act_part.up())
                for name in (("aq", 0), ("aq", 1), ("ak", 0)):
                    for tt in range(TT):
                        act.wait_ge(psum_full.sem, filled((*name, tt)))
                        o = bank_of((*name, tt))
                        n = 512 if name[0] == "aq" else 256
                        if name[0] == "ak":
                            act_(av[:, tt, :], o[:, 256:512])
                        if name != ("aq", 0):
                            act.wait_ge(squares_used.sem, squares_used.next())
                        act_(a_prob[tt][:, 0:n], o[:, 0:n], ACT.Square).then_inc(act_part.sem, act_part.up())
                act.wait_ge(squares_used.sem, squares_used.next(2))
                act.wait_ge(out_of(("bm", 1, 1)), emptied(("bm", 1, 1)))
                for c in range(2):
                    for tt in range(TT):
                        act.wait_ge(psum_full.sem, filled(("ga", c, tt)))
                        act_(sig_g[:, tt, c * BANK:(c + 1) * BANK], bank_of(("ga", c, tt)), ACT.Sigmoid).then_inc(act_out.sem, act_out.up())
                for u in range(4):
                    act.wait_ge(psum_full.sem, filled(("qT", u)))
                    o = bank_of(("qT", u)).rearrange("p (j t) -> p j t", j=2)
                    act_(qT[:, 2 * u:2 * u + 2, :], o, scale=vt[:, V_AQ:V_AQ + 1]).then_inc(act_out.sem, act_out.up())
                for u in range(2):
                    act.wait_ge(psum_full.sem, filled(("kT", u)))
                    o = bank_of(("kT", u)).rearrange("p (j t) -> p j t", j=2)
                    act_(kT[:, 2 * u:2 * u + 2, :], o, scale=vt[:, V_AK:V_AK + 1]).then_inc(act_out.sem, act_out.up())
                for n in range(len(a_groups) + 1):
                    if n < len(a_groups):
                        qt, heads = a_groups[n]
                        w_ = BANK // len(heads)
                        act.wait_ge(dve_part.sem, dve_part.next())
                        if n >= 2:
                            act.wait_ge(psum_full.sem, psum_full.at(units[("at", n - 2)]["full"]))
                        o = psum[:, units[("as", n)]["bank"], :]
                        for j, h in enumerate(heads):
                            c = 16 * qt + h
                            ins = act_(a_prob[n % 2][:, j * w_:(j + 1) * w_], o[:, j * w_:(j + 1) * w_], ACT.Exp,
                                       scale=AHD ** -0.5, bias=small[:, 96 + c:97 + c], accum_out=small[:, 128 + c:129 + c])
                        c = 16 * qt + heads[0]
                        es = small[:, 160 + c:160 + c + 2 * len(heads) - 1:2]
                        act_(es, es, ACT.Exp).then_inc(act_out.sem, act_out.up())
                    if n >= 1 and units[("at", n - 1)]["owner"] == "act":
                        act.wait_ge(psum_full.sem, filled(("at", n - 1)))
                        o = bank_of(("at", n - 1))
                        if n >= 3:
                            s_, v_ = seen["a", n - 3]
                            act.wait_ge(s_.sem, s_.at(v_))
                        act_(a_probT[:, (n - 1) % 2, :], o).then_inc(act_out.sem, act_out.up())
                for u in range(4):
                    operand(("haT", u), yh[:, u * 512:(u + 1) * 512])
                for u in range(4):
                    operand(("mg", u), xh[:, 2 * u:2 * u + 2, 0:T])
                normed("f2", V_FFN2, ("wo", 1, 1))
                feed_forward(2)
                normed("pl", V_PLE, (("fd", 2), 1, 1))
                operand(("pT",), yh[:, 0:512])
                for c in range(2):
                    for tt in range(TT):
                        act.wait_ge(psum_full.sem, filled(("pg", c, tt)))
                        act_(sig_g[:, tt, c * BANK:(c + 1) * BANK], bank_of(("pg", c, tt)), ACT.Sigmoid).then_inc(act_out.sem, act_out.up())

            start["act"] = {n: s_.sent for n, s_ in signals.items()}
            with act.Fori(0, DEPTH) as i:
                loop["i"] = i
                act.wait_ge(layer_start_act.sem, layer_start_act.next())
                hybrid_layer()
            loop["i"] = None

        @block.vector
        def _(dve):
            v = nc.vector
            split = {"next": 0, "limit": start["split"]}

            def keep_up(key):
                u = units[key]
                while split["next"] < min(u["need"] + 2, split["limit"]):
                    s = split["next"]
                    b = split_blocks[s]["block"]
                    if any(x["release"][0] is not split_done for x in blocks[u["raw"]:b["index"] - RING + 1]):
                        break
                    split["next"] += 1
                    size = b["size"]
                    dve.wait_ge(raw_in[b["slot"]].sem, raw_in[b["slot"]].at(b["landed"]))
                    if s - RING >= split["base"]:
                        sig, val = split_blocks[s - RING]["release"]
                        dve.wait_ge(sig.sem, sig.at(val))
                    r = raw[:, b["slot"], :size]
                    v.tensor_copy(wgt_hi[:, s % RING, :size], r).then_inc(high_done.sem, high_done.up())
                    dve.wait_ge(high_done.sem, high_done.now())
                    v.tensor_tensor(wgt_lo[:, s % RING, :size], r, wgt_hi[:, s % RING, :size], ALU.subtract).then_inc(split_done.sem, split_done.up())

            split["base"] = 0

            def low(key, dst_lo, dst_hi):
                keep_up(key)
                dve.wait_ge(psum_full.sem, filled(key))
                o = bank_of(key)
                dve.wait_ge(act_part.sem, act_part.next())
                n = int(np.prod(dst_lo.shape[1:]))
                v.tensor_tensor(dst_lo, like(o[:, 0:n], dst_lo), dst_hi, ALU.subtract).then_inc(dve_out.sem, dve_out.up())

            def like(o, dst):
                return o if len(dst.shape) == 2 else o.rearrange("p (a b) -> p a b", a=dst.shape[1])

            def low_scaled(key, cols, lo, hi):
                keep_up(key)
                dve.wait_ge(psum_full.sem, filled(key))
                o = bank_of(key)
                dve.wait_ge(act_part.sem, act_part.next())
                for j, c in enumerate(cols):
                    ins = v.scalar_tensor_tensor(out=lo(j), in0=o[:, j * T:(j + 1) * T], scalar=vt[:, c:c + 1],
                                                 in1=hi(j), op0=ALU.mult, op1=ALU.subtract)
                ins.then_inc(dve_out.sem, dve_out.up())

            def low_x(name, tts):
                for u in range(KT // (4 // len(tts))):
                    if len(tts) == 4:
                        low((name, u), xl[:, u, :], xh[:, u, :])
                    else:
                        low((name, u), xl[:, 2 * u:2 * u + 2, 0:T], xh[:, 2 * u:2 * u + 2, 0:T])

            def modulation(layer, part):
                keep_up(("mod", layer, part))
                dve.wait_ge(psum_full.sem, filled(("mod", layer, part)))
                o = bank_of(("mod", layer, part))
                c = 16 + 48 * layer + 8 * part
                bias = vt[:, c:c + 8].unsqueeze(2).to_broadcast([P, KT, 2])
                v.scalar_tensor_tensor(
                    out=mod[:, layer, part], in0=o[:, 0:16].rearrange("p (k s) -> p k s", s=2),
                    scalar=1.0 if part in (1, 4) else 0.0, in1=bias, op0=ALU.add, op1=ALU.add).then_inc(dve_out.sem, dve_out.up())

            def prescale(tts):
                for tt in tts:
                    ins = v.tensor_scalar(X[:, tt, :], X[:, tt, :], ALPHA, None, ALU.mult)
                ins.then_inc(dve_own.sem, dve_own.up())
                dve.wait_ge(dve_own.sem, dve_own.now())

            def add_gated(key, tt, c, gate):
                keep_up(key)
                dve.wait_ge(psum_full.sem, filled(key))
                o = bank_of(key)
                s = tt // TT
                dve.wait_ge(out_of(gate), emptied(gate))
                v.tensor_tensor(o, o, gate_b[:, s, c * BANK:(c + 1) * BANK], ALU.mult).then_inc(dve_own.sem, dve_own.up())
                dve.wait_ge(dve_own.sem, dve_own.now())
                x = X[:, tt, c * BANK:(c + 1) * BANK]
                v.tensor_tensor(x, o, x, ALU.add).then_inc(dve_out.sem, dve_out.up())

            def layer_norm(tts):
                n = len(tts)
                st = small[:, 32:32 + 12 * n].rearrange("p (t s) -> p t s", t=n)
                mv = small[:, 80:80 + 2 * n].rearrange("p (t s) -> p t s", t=n)
                ve, rstd = small[:, 88:88 + n], small[:, 92:92 + n]
                dve.wait_ge(dve_out.sem, dve_out.now())
                for tt in tts:
                    for c in range(2):
                        ins = v.bn_stats(st[:, tt, 6 * c:6 * c + 6], X[:, tt, c * BANK:(c + 1) * BANK])
                ins.then_inc(dve_own.sem, dve_own.up())
                dve.wait_ge(dve_own.sem, dve_own.now())
                for tt in tts:
                    ins = v.bn_aggr(mv[:, tt, :], st[:, tt, :])
                ins.then_inc(dve_own.sem, dve_own.up())
                dve.wait_ge(dve_own.sem, dve_own.now())
                v.tensor_scalar(ve, mv[:, :, 1], LN_EPS, None, ALU.add).then_inc(var_ready.sem, var_ready.up())
                dve.wait_ge(rstd_dve.sem, rstd_dve.next())
                for tt in tts:
                    ins = v.tensor_scalar(X[:, tt, :], X[:, tt, :], mv[:, tt, 0:1], rstd[:, tt:tt + 1], ALU.subtract, ALU.mult)
                ins.then_inc(dve_own.sem, dve_own.up())
                dve.wait_ge(dve_own.sem, dve_own.now())
                dve.wait_ge(ln_in.sem, ln_in.next(2))
                for tt in tts:
                    ins = v.tensor_tensor(X[:, tt, :], X[:, tt, :], ln_gb[:, 0, :], ALU.mult)
                ins.then_inc(dve_own.sem, dve_own.up())
                dve.wait_ge(dve_own.sem, dve_own.now())
                for tt in tts:
                    v.tensor_tensor(X[:, tt, :], X[:, tt, :], ln_gb[:, 1, :], ALU.add).then_inc(x_ready.sem, x_ready.up())

            def mlp(layer, tts):
                n = len(tts) * P
                for c in range(MLP_CHUNKS):
                    for kt in range(KT):
                        low((("up", layer), c * KT + kt), yl[:, kt * n:(kt + 1) * n], yh[:, kt * n:(kt + 1) * n])
                    for g in range(2):
                        for tt in tts:
                            add_gated((("down", layer, c), g, tt), tt, g, ("gate", layer, 5, len(tts) // 2 - 1, 1))

            keep_up(("vec",))
            dve.wait_ge(psum_full.sem, filled(("vec",)))
            o = bank_of(("vec",))
            dve.wait_ge(act_part.sem, act_part.next())
            v.tensor_copy(vt[:, 0:112], o[:, 0:112]).then_inc(dve_out.sem, dve_out.up())
            dve.wait_ge(dve_out.sem, dve_out.now())
            dve.wait_ge(act_part.sem, act_part.next())
            v.tensor_scalar(small[:, 16:24], small[:, 8:16], -1.0, None, ALU.mult)
            v.tensor_scalar(small[:, 24:32], small[:, 8:16], -256.0, None, ALU.mult).then_inc(dve_part.sem, dve_part.up())
            modulation(0, 0)
            modulation(0, 1)
            low_x("h0", range(4))
            prescale(range(4))
            modulation(0, 2)

            rows4 = lambda t: t.rearrange("p (a b) -> p a b", a=ROWS)
            for h in range(RET_HEADS):
                dve.wait_ge(act_part.sem, act_part.next())
                v.tensor_tensor(r_exp[:, 0, :], r_exp[:, 0, :], r_tab[:, 2, :], ALU.mult)
                v.tensor_tensor(r_exp[:, 1, :], r_exp[:, 1, :], r_tab[:, 3, :], ALU.mult)
                v.tensor_tensor(r_exp[:, 2, :], r_exp[:, 2, :], r_exp[:, 3, :], ALU.add).then_inc(dve_own.sem, dve_own.up())
                dve.wait_ge(dve_own.sem, dve_own.now())
                v.tensor_tensor(r_strip[:, 0, :], r_exp[:, 0, :], r_exp[:, 1, :], ALU.add)
                v.tensor_scalar(r_strip[:, 1, :], r_exp[:, 2, :], 1.0 / 16.0, None, ALU.mult).then_inc(dve_own.sem, dve_own.up())
                dve.wait_ge(dve_own.sem, dve_own.now())
                for name, dst in (("rq", rq), ("rk", rk)):
                    for d in range(2):
                        keep_up(((name, h), d))
                        dve.wait_ge(psum_full.sem, filled(((name, h), d)))
                        o = rows4(bank_of(((name, h), d))[:, 0:T])
                        dve.wait_ge(act_part.sem, act_part.next())
                        c0 = C_ROPE + 8 * d
                        n = ROWS if d == 0 else GRID_W
                        cos, sin = cst[:, c0:c0 + n], cst[:, c0 + n:c0 + 2 * n]
                        if d == 0:
                            cos, sin = (x.unsqueeze(2).to_broadcast([P, ROWS, GRID_W]) for x in (cos, sin))
                        else:
                            cos, sin = (x.unsqueeze(1).to_broadcast([P, ROWS, GRID_W]) for x in (cos, sin))
                        sw, lat = rows4(r_swap[:, d, :]), rows4(dst[:, d, 0:T])
                        v.tensor_tensor(lat, o, cos, ALU.mult)
                        v.tensor_tensor(sw, sw, sin, ALU.mult).then_inc(dve_own.sem, dve_own.up())
                        dve.wait_ge(dve_own.sem, dve_own.now())
                        v.tensor_tensor(lat, lat, sw, ALU.add).then_inc(dve_out.sem, dve_out.up())
                for s in range(4):
                    keep_up(("rs", h, s))
                    dve.wait_ge(psum_full.sem, filled(("rs", h, s)))
                    o = bank_of(("rs", h, s))
                    u = s % 2
                    lo = P - P * u
                    strip = r_strip[:, 0 if s < 2 else 1, lo:lo + T]
                    ins = v.tensor_tensor(rs[:, s, :], o[:, 0:T], strip, ALU.mult)
                    if s >= 2:
                        ins = v.tensor_tensor(rs[:, s + 2, :], o[:, T:2 * T], r_strip[:, 0, lo:lo + T], ALU.mult)
                    ins.then_inc(dve_out.sem, dve_out.up())
                st, mv = small[:, 32:56], small[:, 80:88]
                for tt in range(4):
                    keep_up(("ro", h, tt))
                    dve.wait_ge(psum_full.sem, filled(("ro", h, tt)))
                    o = bank_of(("ro", h, tt))
                    ins = v.bn_stats(st[:, 6 * tt:6 * tt + 6], o)
                ins.then_inc(dve_own.sem, dve_own.up())
                dve.wait_ge(dve_own.sem, dve_own.now())
                for tt in range(4):
                    ins = v.bn_aggr(mv[:, 2 * tt:2 * tt + 2], st[:, 6 * tt:6 * tt + 6])
                ins.then_inc(dve_own.sem, dve_own.up())
                dve.wait_ge(dve_own.sem, dve_own.now())
                v.tensor_scalar(small[:, 88:92], mv.rearrange("p (t s) -> p t s", s=2)[:, :, 1], LN_EPS, None, ALU.add).then_inc(var_ready.sem, var_ready.up())
                for tt in range(4):
                    dve.wait_ge(out_of((("rg", h), 0, tt)), emptied((("rg", h), 0, tt)))
                    o = psum[:, units[("ro", h, tt)]["bank"], :]
                    v.scalar_tensor_tensor(out=rg[:, tt, :], in0=o, scalar=mv[:, 2 * tt:2 * tt + 1],
                                                        in1=rg[:, tt, :], op0=ALU.subtract, op1=ALU.mult).then_inc(dve_out.sem, dve_out.up())
                dve.wait_ge(rstd_dve.sem, rstd_dve.next())
                dve.wait_ge(dve_out.sem, dve_out.now())
                for tt in range(4):
                    v.tensor_scalar(rg[:, tt, :], rg[:, tt, :], small[:, 92 + tt:93 + tt], None, ALU.mult).then_inc(x_ready.sem, x_ready.up())
                for ft in range(4):
                    low(("ron", h, ft), yl[:, ft * 2 * T:(ft + 1) * 2 * T], yh[:, ft * 2 * T:(ft + 1) * 2 * T])
                if h == RET_HEADS - 1:
                    v.memset(small[:, 320:321], 0.0).then_inc(tab_free.sem, tab_free.up())
                for c in range(2):
                    for tt in range(4):
                        add_gated((("ry", h), c, tt), tt, c, ("gate", 0, 2, 1, 1))
            for part in (3, 4, 5):
                modulation(0, part)
            layer_norm(range(4))
            low_x("h0m", range(4))
            prescale(range(4))
            v.memset(small[:, 321:322], 0.0).then_inc(tab_free.sem, tab_free.up())
            mlp(0, range(4))
            for part in (0, 1, 2):
                modulation(1, part)
            layer_norm(range(4))

            low_x("h1", range(4))
            prescale(range(2))
            n_steps = len(nat_steps)
            for n in range(n_steps + 2):
                if n < n_steps:
                    qt, h = nat_steps[n]
                    keep_up(("ns", n))
                    dve.wait_ge(psum_full.sem, filled(("ns", n)))
                    o = bank_of(("ns", n))
                    if qt == 0:
                        dve.wait_ge(bias_ready.sem, bias_ready.next())
                    e0 = 2 - 2 * qt
                    b = n_bias[:, h % 2, :].rearrange("p (e k) -> p e k", k=GRID_W)[:, e0:e0 + ROWS, :]
                    ins = v.tensor_tensor(rows4(o[:, 0:T]), rows4(o[:, 0:T]), b, ALU.add)
                    if qt == 0:
                        ins.then_inc(dve_own.sem, dve_own.up())
                        dve.wait_ge(dve_own.sem, dve_own.now())
                    else:
                        ins.then_inc(bias_used.sem, bias_used.up())
                        dve.wait_ge(bias_used.sem, bias_used.now())
                    c = 32 * qt + h
                    mx = small[:, 192 + c:193 + c]
                    v.tensor_reduce(mx, o, AX, ALU.max).then_inc(dve_own.sem, dve_own.up())
                    dve.wait_ge(dve_own.sem, dve_own.now())
                    v.tensor_scalar(mx, mx, -1.0, None, ALU.mult).then_inc(dve_part.sem, dve_part.up())
                if 1 <= n <= n_steps and units[("nt", n - 1)]["owner"] == "dve":
                    keep_up(("nt", n - 1))
                    dve.wait_ge(psum_full.sem, filled(("nt", n - 1)))
                    o = bank_of(("nt", n - 1))
                    if n >= 3:
                        s_, v_ = seen["n", n - 3]
                        dve.wait_ge(s_.sem, s_.at(v_))
                    v.tensor_copy(n_probT[:, (n - 1) % 2, :], o).then_inc(dve_out.sem, dve_out.up())
                if n >= 2 and nat_steps[n - 2][1] % 16 == 15:
                    qt, h = nat_steps[n - 2]
                    u = h // 16
                    keep_up(("no", qt, u))
                    dve.wait_ge(psum_full.sem, filled(("no", qt, u)))
                    o = bank_of(("no", qt, u)).rearrange("p (h d) -> p h d", h=16)
                    r = small[:, 256 + 32 * qt + 16 * u:272 + 32 * qt + 16 * u]
                    dve.wait_ge(out_of(("ns", n - 2)), emptied(("ns", n - 2)))
                    v.reciprocal(r, r).then_inc(dve_own.sem, dve_own.up())
                    dve.wait_ge(dve_own.sem, dve_own.now())
                    dst = U[:, qt, u * BANK:(u + 1) * BANK].rearrange("p (h d) -> p h d", h=16)
                    v.tensor_tensor(dst, o, r.unsqueeze(2).to_broadcast([P, 16, NAT_HD]), ALU.mult).then_inc(dve_out.sem, dve_out.up())
            v.memset(small[:, 322:323], 0.0).then_inc(tab_free.sem, tab_free.up())
            for u in range(4):
                keep_up(("noT", u))
                dve.wait_ge(psum_full.sem, filled(("noT", u)))
                o = bank_of(("noT", u))
                dve.wait_ge(act_part.sem, act_part.next())
                v.tensor_tensor(rows_of(yl[:, u * 512:(u + 1) * 512]), turned(o),
                                             rows_of(yh[:, u * 512:(u + 1) * 512]), ALU.subtract).then_inc(dve_out.sem, dve_out.up())
            for c in range(2):
                for tt in range(2):
                    add_gated(("ny", c, tt), tt, c, ("gate", 1, 2, 0, 1))
            for part in (3, 4, 5):
                modulation(1, part)
            layer_norm(range(2))
            low_x("h1m", range(2))
            prescale(range(2))
            v.memset(small[:, 323:324], 0.0).then_inc(tab_free.sem, tab_free.up())
            mlp(1, range(2))
            layer_norm(range(2))
            if upto < 1:
                return

            v.memset(yh_pad.bitcast(F32), 0.0)
            v.memset(yl_pad.bitcast(F32), 0.0)
            v.memset(small[:, 324:325], 0.0).then_inc(tab_free.sem, tab_free.up())

            def normed(name, col):
                dve.wait_ge(act_part.sem, act_part.next())
                v.tensor_scalar(small[:, 82:84], small[:, 80:82], 1.0 / D, EPS, ALU.mult, ALU.add).then_inc(var_ready.sem, var_ready.up())
                for u in range(4):
                    low_scaled((name, u), (col + 2 * u, col + 2 * u + 1),
                               lambda j: xl[:, 2 * u + j, 0:T], lambda j: xh[:, 2 * u + j, 0:T])

            def add_to_x(name, factor):
                for c in range(2):
                    for tt in range(TT):
                        x = X[:, tt, c * BANK:(c + 1) * BANK]
                        keep_up((name, c, tt))
                        dve.wait_ge(psum_full.sem, filled((name, c, tt)))
                        o = bank_of((name, c, tt))
                        v.scalar_tensor_tensor(out=x, in0=o, scalar=factor, in1=x,
                                                            op0=ALU.mult, op1=ALU.add).then_inc(dve_out.sem, dve_out.up())

            def feed_forward(n):
                for t in range(FF_TILES):
                    keep_up(("ff", n, t))
                    dve.wait_ge(psum_full.sem, filled(("ff", n, t)))
                    o = bank_of(("ff", n, t))
                    dve.wait_ge(act_part.sem, act_part.next())
                    p0 = 0 if t < FF_TILES - 1 else P // 2
                    f = f_v[p0:, t % 2, :]
                    hi, lo = ff_at(yh, xh, t)[p0:], ff_at(yl, xl, t)[p0:]
                    v.tensor_tensor(f, f_sil[p0:, t % 2, :], o[p0:, T:2 * T], ALU.mult).then_inc(dve_own.sem, dve_own.up())
                    dve.wait_ge(dve_own.sem, dve_own.now())
                    v.tensor_copy(hi, f).then_inc(dve_own.sem, dve_own.up())
                    dve.wait_ge(dve_own.sem, dve_own.now())
                    v.tensor_tensor(lo, f, hi, ALU.subtract).then_inc(dve_out.sem, dve_out.up())
                add_to_x(("fd", n), 0.5)

            def hybrid_layer():
                v.memset(qk_pre[:, :, 0:3], 0.0)
                dve.wait_ge(out_of(("lvec",)), emptied(("lvec",)))
                normed("f1", V_FFN1)
                feed_forward(1)
                normed("mx", V_MIX)
                for g in range(4):
                    keep_up(("mqk", 2 * g + 1))
                    dve.wait_ge(out_of(("mqk", 2 * g + 1)), emptied(("mqk", 2 * g + 1)))
                    for j in range(CONV_K):
                        for t in range(4 * g, 4 * g + 4):
                            w = vt[:, V_CW + 16 * j + t:V_CW + 16 * j + t + 1]
                            x = qk_pre[:, t, j:j + T]
                            if j == 0:
                                ins = v.tensor_scalar(qk_post[:, t, :], x, w, vt[:, V_CB + t:V_CB + t + 1], ALU.mult, ALU.add)
                            else:
                                ins = v.scalar_tensor_tensor(out=qk_post[:, t, :], in0=x, scalar=w, in1=qk_post[:, t, :],
                                                             op0=ALU.mult, op1=ALU.add)
                        if j < CONV_K - 1:
                            ins.then_inc(dve_own.sem, dve_own.up())
                            dve.wait_ge(dve_own.sem, dve_own.now())
                    ins.then_inc(dve_part.sem, dve_part.up())
                keep_up(("mif",))
                dve.wait_ge(psum_full.sem, filled(("mif",)))
                o = bank_of(("mif",))
                dve.wait_ge(lay_in.sem, lay_in.at(16 * N_LAYER_DMAS))
                g8 = small[:, 64:80].rearrange("p (t g) -> p t g", t=TT)
                v.tensor_tensor(g8, o[:, 0:16].rearrange("p (t g) -> p t g", t=TT),
                                             gbias.unsqueeze(1).to_broadcast([P, TT, 8]), ALU.add).then_inc(dve_out.sem, dve_out.up())
                v.memset(v_ext_ones, 1.0)
                keep_up(("mifT",))
                dve.wait_ge(psum_full.sem, filled(("mifT",)))
                v.tensor_copy(W[0:MH, 1152:1664], bank_of(("mifT",))[0:MH, :]).then_inc(dve_out.sem, dve_out.up())
                dve.wait_ge(dve_out.sem, dve_out.now())
                v.scalar_tensor_tensor(out=rowv[2], in0=rowv[1], scalar=-1.0, in1=rowv[1], op0=ALU.mult, op1=ALU.min).then_inc(dve_part.sem, dve_part.up())
                v.memset(rowv[5], 0.0)
                dve.wait_ge(act_part.sem, act_part.next())
                v.scalar_tensor_tensor(out=rowv[3], in0=rowv[1], scalar=0.0, in1=rowv[2], op0=ALU.min, op1=ALU.subtract).then_inc(dve_own.sem, dve_own.up())
                dve.wait_ge(dve_own.sem, dve_own.now())
                v.tensor_tensor_scan(rowv[1], rowv[3], rowv[5], 0.0, ALU.add, ALU.add).then_inc(dve_own.sem, dve_own.up())
                dve.wait_ge(dve_own.sem, dve_own.now())
                v.tensor_tensor(rowv[4], rowv[0], rowv[1], ALU.subtract).then_inc(dve_own.sem, dve_own.up())
                dve.wait_ge(dve_own.sem, dve_own.now())
                v.tensor_tensor_scan(rowv[6], rowv[4], rowv[4], 0.0, ALU.max, ALU.max).then_inc(dve_own.sem, dve_own.up())
                dve.wait_ge(dve_own.sem, dve_own.now())
                v.tensor_tensor(rowv[5], rowv[1], rowv[6], ALU.add).then_inc(dve_part.sem, dve_part.up())
                dve.wait_ge(dve_part.sem, dve_part.now())
                v.tensor_scalar(rowv[6], rowv[6], -1.0, None, ALU.mult).then_inc(x_ready.sem, x_ready.up())
                keep_up(("mcol",))
                dve.wait_ge(psum_full.sem, filled(("mcol",)))
                v.tensor_copy(small[:, 192:208], bank_of(("mcol",))[:, 0:16]).then_inc(dve_out.sem, dve_out.up())
                dve.wait_ge(dve_out.sem, dve_out.now())

                def mvalues(h):
                    for tt in range(TT):
                        keep_up(("mn", h, tt))
                        dve.wait_ge(psum_full.sem, filled(("mn", h, tt)))
                        o = bank_of(("mn", h, tt))
                        e = small[:, 200 + 4 * tt + h:201 + 4 * tt + h]
                        den = o[:, MHD:MHD + 1]
                        v.tensor_scalar(small[:, 93:94], den, -1.0, e, ALU.mult, ALU.max).then_inc(dve_own.sem, dve_own.up())
                        dve.wait_ge(dve_own.sem, dve_own.now())
                        v.tensor_tensor(small[:, 93:94], den, small[:, 93:94], ALU.max).then_inc(dve_own.sem, dve_own.up())
                        dve.wait_ge(dve_own.sem, dve_own.now())
                        v.reciprocal(small[:, 88:89], small[:, 93:94]).then_inc(dve_part.sem, dve_part.up())
                        dve.wait_ge(dve_part.sem, dve_part.now())
                        dve.wait_ge(act_part.sem, act_part.next())
                        v.tensor_scalar(small[:, 90:91], small[:, 89:90], 1.0 / MHD, EPS, ALU.mult, ALU.add).then_inc(var_ready.sem, var_ready.up())
                        dve.wait_ge(rstd_dve.sem, rstd_dve.next())
                        v.tensor_tensor(small[:, 92:93], small[:, 88:89], small[:, 91:92], ALU.mult).then_inc(dve_own.sem, dve_own.up())
                        dve.wait_ge(dve_own.sem, dve_own.now())
                        if h == 0:
                            dve.wait_ge(out_of(("mo", 1, tt)), emptied(("mo", 1, tt)))
                        cols = slice(h * MHD, (h + 1) * MHD)
                        v.scalar_tensor_tensor(out=U[:, tt, cols], in0=o[:, 0:MHD], scalar=small[:, 92:93],
                                                            in1=sig_o[:, tt, cols], op0=ALU.mult, op1=ALU.mult).then_inc(dve_out.sem, dve_out.up())

                for h in range(MH + 1):
                    if h < MH:
                        keep_up(("mb", h))
                        dve.wait_ge(psum_full.sem, filled(("mb", h)))
                        o = bank_of(("mb", h))
                        a0, a1 = small[:, 192 + h:193 + h], small[:, 196 + h:197 + h]
                        t_ = tri[:, 0:P]
                        r = m_arg[:, h % 2, :]
                        v.scalar_tensor_tensor(out=r[:, 0:P], in0=o[:, 0:P], scalar=a0, in1=t_, op0=ALU.add, op1=ALU.add)
                        v.tensor_scalar(r[:, P:T], o[:, P:T], a0, None, ALU.add)
                        v.scalar_tensor_tensor(out=r[:, T:T + P], in0=o[:, P:T], scalar=a1, in1=t_, op0=ALU.add, op1=ALU.add).then_inc(dve_out.sem, dve_out.up())
                        keep_up(("ms", h))
                        dve.wait_ge(psum_full.sem, filled(("ms", h)))
                        o = bank_of(("ms", h))
                        dve.wait_ge(act_part.sem, act_part.next())
                        v.scalar_tensor_tensor(out=m_s[:, h % 2, :], in0=o[:, 0:384], scalar=1.0 / 16.0, in1=r,
                                                            op0=ALU.mult, op1=ALU.mult).then_inc(dve_out.sem, dve_out.up())
                    if h:
                        mvalues(h - 1)
                for u in range(4):
                    low_scaled(("hmT", u), (V_MO + 2 * u, V_MO + 2 * u + 1),
                               lambda j: yl[:, (2 * u + j) * T:(2 * u + j + 1) * T], lambda j: yh[:, (2 * u + j) * T:(2 * u + j + 1) * T])
                dve.wait_ge(out_of(("gm", 1, 1)), emptied(("gm", 1, 1)))
                for c in range(2):
                    for tt in range(TT):
                        cols = slice(c * BANK, (c + 1) * BANK)
                        keep_up(("bm", c, tt))
                        dve.wait_ge(psum_full.sem, filled(("bm", c, tt)))
                        v.tensor_tensor(merged[:, tt, cols], bank_of(("bm", c, tt)), sig_g[:, tt, cols], ALU.mult).then_inc(dve_out.sem, dve_out.up())
                for name in (("aq", 0), ("aq", 1), ("ak", 0)):
                    for tt in range(TT):
                        keep_up((*name, tt))
                        dve.wait_ge(psum_full.sem, filled((*name, tt)))
                        o = bank_of((*name, tt))
                        dve.wait_ge(act_part.sem, act_part.next())
                        nh = 8 if name[0] == "aq" else AKV
                        sq = a_prob[tt][:, 0:nh * AHD].rearrange("p (h d) -> p h d", d=AHD)
                        v.tensor_reduce(small[:, 208:208 + nh], sq, AX, ALU.add).then_inc(squares_used.sem, squares_used.up())
                        dve.wait_ge(squares_used.sem, squares_used.now())
                        v.tensor_scalar(small[:, 216:216 + nh], small[:, 208:208 + nh], 1.0 / AHD, EPS, ALU.mult, ALU.add).then_inc(var_ready.sem, var_ready.up())
                        dve.wait_ge(rstd_dve.sem, rstd_dve.next())
                        r = small[:, 224:224 + nh].unsqueeze(2).to_broadcast([P, nh, AHD])
                        x = o[:, 0:nh * AHD].rearrange("p (h d) -> p h d", d=AHD)
                        if name[0] == "aq":
                            dst = qn[:, tt, name[1] * BANK:(name[1] + 1) * BANK].rearrange("p (h d) -> p h d", d=AHD)
                            v.tensor_tensor(dst, x, r, ALU.mult).then_inc(dve_out.sem, dve_out.up())
                        else:
                            dst = kn[:, tt, :].rearrange("p (h b d) -> p h b d", b=2, d=AHD)
                            v.tensor_tensor(dst[:, :, 0, :], x, r, ALU.mult)
                            v.tensor_tensor(dst[:, :, 1, :], x, r, ALU.mult).then_inc(dve_out.sem, dve_out.up())
                v.tensor_scalar(small[:, 232:248], sink, float(AHD) ** 0.5, None, ALU.mult).then_inc(dve_own.sem, dve_own.up())
                dve.wait_ge(dve_own.sem, dve_own.now())
                for n in range(len(a_groups) + 2):
                    if n < len(a_groups):
                        qt, heads = a_groups[n]
                        nh = len(heads)
                        c, hs = 16 * qt + heads[0], slice(heads[0], heads[-1] + 1, 2)
                        keep_up(("as", n))
                        dve.wait_ge(psum_full.sem, filled(("as", n)))
                        o = bank_of(("as", n)).rearrange("p (h k) -> p h k", h=nh)
                        mask = tri[:, 256:384] if qt == 0 else tri[:, 128:384]
                        v.tensor_tensor(o, o, mask.unsqueeze(1).to_broadcast([P, nh, BANK // nh]), ALU.add).then_inc(dve_own.sem, dve_own.up())
                        dve.wait_ge(dve_own.sem, dve_own.now())
                        mx, es = (small[:, k + c:k + c + 2 * nh - 1:2] for k in (96, 160))
                        v.tensor_reduce(mx, o, AX, ALU.max).then_inc(dve_own.sem, dve_own.up())
                        dve.wait_ge(dve_own.sem, dve_own.now())
                        v.tensor_tensor(mx, mx, small[:, 232:248][:, hs], ALU.max).then_inc(dve_own.sem, dve_own.up())
                        dve.wait_ge(dve_own.sem, dve_own.now())
                        v.tensor_scalar(mx, mx, -(float(AHD) ** -0.5), None, ALU.mult).then_inc(dve_own.sem, dve_own.up())
                        dve.wait_ge(dve_own.sem, dve_own.now())
                        v.tensor_tensor(es, mx, sink[:, hs], ALU.add).then_inc(dve_part.sem, dve_part.up())
                    if 1 <= n <= len(a_groups) and units[("at", n - 1)]["owner"] == "dve":
                        keep_up(("at", n - 1))
                        dve.wait_ge(psum_full.sem, filled(("at", n - 1)))
                        o = bank_of(("at", n - 1))
                        if n >= 3:
                            s_, v_ = seen[("a", n - 3)]
                            dve.wait_ge(s_.sem, s_.at(v_))
                        v.tensor_copy(a_probT[:, (n - 1) % 2, :], o).then_inc(dve_out.sem, dve_out.up())
                    if n >= 2:
                        qt, heads = a_groups[n - 2]
                        per = 2 if qt == 0 else 4
                        m = n - 2 if qt == 0 else n - 6
                        if m % per == per - 1:
                            u = m // per
                            keep_up(("ao", qt, u))
                            dve.wait_ge(psum_full.sem, filled(("ao", qt, u)))
                            o = bank_of(("ao", qt, u)).rearrange("p (h d) -> p h d", h=8)
                            dve.wait_ge(out_of(("as", n - 2)), emptied(("as", n - 2)))
                            c = 16 * qt + 8 * u
                            den = small[:, 128 + c:136 + c]
                            v.tensor_tensor(den, den, small[:, 160 + c:168 + c], ALU.add).then_inc(dve_own.sem, dve_own.up())
                            dve.wait_ge(dve_own.sem, dve_own.now())
                            v.reciprocal(den, den).then_inc(dve_own.sem, dve_own.up())
                            dve.wait_ge(dve_own.sem, dve_own.now())
                            dst = U[:, qt, u * BANK:(u + 1) * BANK].rearrange("p (h d) -> p h d", h=8)
                            v.tensor_tensor(dst, o, den.unsqueeze(2).to_broadcast([P, 8, AHD]), ALU.mult).then_inc(dve_out.sem, dve_out.up())
                for u in range(4):
                    low(("haT", u), yl[:, u * 512:(u + 1) * 512], yh[:, u * 512:(u + 1) * 512])
                dve.wait_ge(out_of(("ga", 1, 1)), emptied(("ga", 1, 1)))
                for c in range(2):
                    for tt in range(TT):
                        cols = slice(c * BANK, (c + 1) * BANK)
                        keep_up(("ba", c, tt))
                        dve.wait_ge(psum_full.sem, filled(("ba", c, tt)))
                        o = bank_of(("ba", c, tt))
                        v.tensor_tensor(o, o, sig_g[:, tt, cols], ALU.mult).then_inc(dve_own.sem, dve_own.up())
                        dve.wait_ge(dve_own.sem, dve_own.now())
                        v.tensor_tensor(merged[:, tt, cols], o, merged[:, tt, cols], ALU.add).then_inc(dve_out.sem, dve_out.up())
                low_x("mg", range(2))
                add_to_x("wo", 1.0)
                normed("f2", V_FFN2)
                feed_forward(2)
                normed("pl", V_PLE)
                low(("pT",), yl[:, 0:512], yh[:, 0:512])
                for c in range(2):
                    for tt in range(TT):
                        cols = slice(c * BANK, (c + 1) * BANK)
                        keep_up(("pp", c, tt))
                        dve.wait_ge(psum_full.sem, filled(("pp", c, tt)))
                        o = bank_of(("pp", c, tt))
                        dve.wait_ge(out_of(("pg", c, tt)), emptied(("pg", c, tt)))
                        v.tensor_tensor(o, o, sig_g[:, tt, cols], ALU.mult).then_inc(dve_own.sem, dve_own.up())
                        dve.wait_ge(dve_own.sem, dve_own.now())
                        v.tensor_tensor(X[:, tt, cols], o, X[:, tt, cols], ALU.add).then_inc(dve_out.sem, dve_out.up())

            start["dve"] = {n: s_.sent for n, s_ in signals.items()}
            assert dve_out.sent == start["owned"]["dve"], (dve_out.sent, start["owned"])
            split.update(base=start["split"], limit=len(split_blocks))
            with dve.Fori(0, DEPTH) as i:
                loop["i"] = i
                dve.wait_ge(dve_out.sem, dve_out.now())
                for n, s_ in enumerate((layer_start, layer_start_act, layer_start_pool)):
                    v.memset(small[:, 328 + n:329 + n], 0.0).then_inc(s_.sem, s_.up())
                hybrid_layer()
            loop["i"] = None

        @block.gpsimd
        def _(pool):
            g = nc.gpsimd

            def rstd(ve, dst, n, signal_):
                pool.wait_ge(var_ready.sem, var_ready.next())
                g.tensor_tensor(dst, ve, small[:, 336:336 + n], ALU.pow).then_inc(signal_.sem, signal_.up())

            def ln_table(layer, j):
                pool.wait_ge(tab_free.sem, tab_free.next())
                for k, x in enumerate((a["ln_g"], a["ln_b"])):
                    pool.dma_start(ln_gb[:, k, :], x[layer, j:j + 1, :].to_broadcast([P, D])).then_inc(ln_in.sem, ln_in.up())

            def ln_rstd(n):
                rstd(small[:, 88:88 + n], small[:, 92:92 + n], n, rstd_dve)

            def load_bias(h):
                if h >= 2:
                    pool.wait_ge(bias_used.sem, bias_used.next())
                for rr in range(2):
                    dst = n_bias[rr * GRID_W:(rr + 1) * GRID_W, h % 2, :].rearrange("p (e k) -> p e k", k=GRID_W)
                    src = a["nat_rpb"][0, h]
                    src = bass.AP(src.tensor, src.offset + (5 - rr) * NAT_BIAS_COLS + 15 - (GRID_W - 1),
                                  [[1, GRID_W], [NAT_BIAS_COLS, 6], [1, GRID_W]])
                    pool.dma_start(dst, src).then_inc(bias_in[h % 2].sem, bias_in[h % 2].up())

            g.memset(small[:, 336:352], -0.5).then_inc(pool_own.sem, pool_own.up())
            pool.wait_ge(pool_own.sem, pool_own.now())
            for h in range(RET_HEADS):
                rstd(small[:, 88:92], small[:, 92:96], 4, rstd_dve)
            ln_table(0, 0)
            ln_rstd(4)
            ln_table(0, 1)
            load_bias(0)
            load_bias(1)
            ln_rstd(4)
            for h in range(NAT_HEADS):
                pool.wait_ge(bias_in[h % 2].sem, bias_in[h % 2].next(2))
                b = n_bias[:, h % 2, :].rearrange("p (e k) -> p e k", k=GRID_W)
                win = cst[:, C_WIN:C_WIN + GRID_W].unsqueeze(1).to_broadcast([P, 6, GRID_W])
                if h == 0:
                    pool.wait_ge(const_in.sem, const_in.at(16))
                g.tensor_tensor(b, b, win, ALU.add).then_inc(bias_ready.sem, bias_ready.up())
                if h + 2 < NAT_HEADS:
                    load_bias(h + 2)
            ln_table(1, 0)
            ln_rstd(2)
            ln_table(1, 1)
            ln_rstd(2)
            if upto < 1:
                return
            pool.wait_ge(tab_free.sem, tab_free.next())
            pool.dma_start(tri, a["consts"][:, C_TRI:C_TRI + 384]).then_inc(tri_in.sem, tri_in.up())
            start["pool"] = {n: s_.sent for n, s_ in signals.items()}
            with pool.Fori(0, DEPTH) as i:
                loop["i"] = i
                pool.wait_ge(layer_start_pool.sem, layer_start_pool.next())
                rows = [(V_FFN1, "ffn1_norm_2"), (V_MIX, "mix_norm_2"), (V_CW, "m_conv_w_2"), (V_CB, "m_conv_b_2"),
                        (V_MO, "m_out_norm_2"), (V_FFN2, "ffn2_norm_2"), (V_PLE, "ple_norm_2")]
                for r, name in rows:
                    x = a[name][i]
                    x = x.rearrange("(r n) -> r n", n=P) if len(x.shape) == 1 else x.rearrange("k (r n) -> (k r) n", n=P)
                    pool.dma_start(l_rows[r:r + x.shape[0], :], x).then_inc(lay_in.sem, lay_in.up())
                for r, name in ((V_AQ, "a_q_norm_2"), (V_AK, "a_k_norm_2")):
                    for c in (0, AHD):
                        pool.dma_start(l_rows[r:r + 1, c:c + AHD], a[name][i].unsqueeze(0)).then_inc(lay_in.sem, lay_in.up())
                pool.dma_start(sink, a["a_sinks_2"][i].unsqueeze(0).to_broadcast([P, AH])).then_inc(lay_in.sem, lay_in.up())
                pool.dma_start(gbias[:, 0:MH], a["m_igate_b_2"][i].unsqueeze(0).to_broadcast([P, MH])).then_inc(lay_in.sem, lay_in.up())
                pool.dma_start(gbias[:, MH:2 * MH], a["m_fgate_b_2"][i].unsqueeze(0).to_broadcast([P, MH])).then_inc(lay_in.sem, lay_in.up())
                pool.dma_start(l_p, a["p_2"][i][0].rearrange("(t p) n -> p t n", p=P)).then_inc(lay_in.sem, lay_in.up())
                for _ in range(2):
                    rstd(small[:, 82:84], small[:, 84:86], 2, rstd_act)
                for _ in range(MH * TT):
                    rstd(small[:, 90:91], small[:, 91:92], 1, rstd_dve)
                for nh in (8, 8, 8, 8, AKV, AKV):
                    rstd(small[:, 216:216 + nh], small[:, 224:224 + nh], nh, rstd_dve)
                for _ in range(2):
                    rstd(small[:, 82:84], small[:, 84:86], 2, rstd_act)
            loop["i"] = None

        @block.sync
        def _(sp):
            def load(n):
                b = blocks[n]
                if n >= RING:
                    sig, val = blocks[n - RING]["release"]
                    sp.wait_ge(sig.sem, sig.at(val))
                i = loop.get("i")
                raw_in[b["slot"]]
                dst = raw[:, b["slot"], :b["size"]].rearrange("p (a b) -> p a b", a=b["shape"][1])
                sp.dma_start(dst, b["source"](0 if i is None else i)).then_inc(raw_in[b["slot"]].sem, 16)

            for n in range(start.get("blocks", len(blocks))):
                load(n)
            if upto >= 1:
                assert all(blocks[start["blocks"] - 1 - k]["release"][0] is split_done for k in range(RING))
                with sp.Fori(0, DEPTH) as i:
                    loop["i"] = i
                    for n in range(start["blocks"], len(blocks)):
                        load(n)
                loop["i"] = None
                end = dve_out.sent + (dve_out.sent - start["dve"]["dve_out"])
                sp.wait_ge(dve_out.sem, end)
            else:
                sp.wait_ge(x_ready.sem, x_ready.sent)
            sp.dma_start(out[0].rearrange("(t p) n -> p t n", p=P), X[:, 0:TT, :]).then_inc(out_done.sem, out_done.up())
            sp.wait_ge(out_done.sem, out_done.at(16))

        if counts is not None:
            counts.update({n: (s_.sent, s_.taken) for n, s_ in signals.items()}, start=start)


_INS = ["x", "c", "ctx", "c_ctx", "ada_w", "ada_b", "ret_w_in", "ret_w_o", "ret_decay", "nat_w_in", "nat_w_o", "nat_rpb",
        "mlp_w1", "mlp_w2", "ln_g", "ln_b", "p_2", "ffn1_norm_2", "ffn1_w_gate_2", "ffn1_w_up_2", "ffn1_w_down_2",
        "mix_norm_2", "w_in_2", "m_conv_w_2", "m_conv_b_2", "m_igate_b_2", "m_fgate_b_2", "m_out_norm_2",
        "a_q_norm_2", "a_k_norm_2", "a_sinks_2", "w_branch_m_2", "w_branch_a_2", "w_out_2", "ffn2_norm_2",
        "ffn2_w_gate_2", "ffn2_w_up_2", "ffn2_w_down_2", "ple_norm_2", "ple_gate_w_2", "ple_proj_w_2"]


def kernel(**inputs):
    import concourse.bacc as bacc
    from concourse.bass_utils import run_bass_kernel_spmd

    nc = bacc.Bacc("TRN2", target_bir_lowering=False, num_devices=1)
    arrays, args = {}, {}
    for name in _INS:
        arrays[name] = np.ascontiguousarray(inputs[name])
    arrays["consts"] = constants()
    for name, x in arrays.items():
        args[name] = nc.dram_tensor(name, x.shape, mybir.dt.from_np(x.dtype), kind="ExternalInput").ap()
    out = nc.dram_tensor("y", (1, T, D), F32, kind="ExternalOutput").ap()
    build(nc, args, out)
    r = run_bass_kernel_spmd(nc, [arrays], core_ids=[0])
    return r.results[0]["y"]
```

```python
from contextlib import ExitStack

import numpy as np
import concourse.bass as bass
from concourse import mybir

F32 = mybir.dt.float32
F32R = mybir.dt.float32r
ALU = mybir.AluOpType
ACT = mybir.ActivationFunctionType
AX = mybir.AxisListType.X

P = 128
D = 1024
KT = D // P
T = 256
TT = T // P
BANK = 512
DEPTH = 2
LAG = 2
N_LAG = 4
N_BUFS = 3
A_BUFS = 3
ALPHA = (2.0 * DEPTH) ** 0.25
LN_EPS = 1e-5
EPS = 1e-6
GRID_W = 64
ROWS = T // GRID_W
RET_HEADS = 4
RET_V = 512
NAT_HEADS = 32
NAT_HD = 32
NAT_BIAS_ROWS = 15
NAT_BIAS_COLS = 31
MLP_CHUNKS = 4
D_FF = 2752
FF_TILES = 22
FF_GROUPS = 11
MH = 4
MHD = 256
AH = 16
AKV = 4
AHD = 64
CONV_K = 4
BIG = -1e30
RING = 3
N_LAYER_DMAS = 14
BLOCK = 2048

O_QK, O_V, O_O, O_I, O_AQ, O_AK, O_GM, O_GA = 0, 2048, 3072, 4096, 4104, 5128, 5640, 6664

C_ID, C_ROPE, C_WIN, C_PAIR, C_HEAD, C_ABS, C_REL, C_MF, C_MB, C_TRI = 0, 128, 264, 328, 330, 334, 718, 1102, 1486, 1870
C_ALL = C_TRI + 384

V_FFN1, V_MIX, V_CW, V_CB, V_MO, V_FFN2, V_PLE, V_AQ, V_AK, V_ROWS = 0, 8, 16, 80, 96, 104, 112, 120, 121, 122

PER_LAYER = {
    "psum_full": 185, "weights_used": 65, "values_done": 8, "act_out": 53, "dve_out": 132, "act_part":
    96, "dve_part": 26, "act_own": 1, "dve_own": 197, "high_done": 120, "split_done": 120, "x_ready": 1,
    "u_ready": 8, "var_ready": 18, "rstd_dve": 18, "layer_start": 1, "layer_start_act": 1,
    "layer_start_pool": 1, "row_ready": 1, "conv_done": 1, "q_ready": 32, "probs_ready": 64,
    "squares_used": 6, "raw_in0": 640, "raw_in1": 640, "raw_in2": 640, "lay_in": 224, "p_in": 16,
}


def constants():
    c = np.zeros((P, C_ALL), np.float32)
    p = np.arange(P)
    c[:, C_ID:C_ID + P] = np.eye(P)
    inv = (1.0 / (np.float32(10000.0) ** (np.arange(0, P, 2, dtype=np.float32) / np.float32(P)))).astype(np.float32)
    sign = np.where(p < 64, -1.0, 1.0)[:, None]
    for off, n in ((0, ROWS), (2 * ROWS, GRID_W)):
        ang = (inv[p % 64][:, None] * np.arange(n, dtype=np.float32)[None]).astype(np.float32)
        c[:, C_ROPE + off:C_ROPE + off + n] = np.cos(ang)
        c[:, C_ROPE + off + n:C_ROPE + off + 2 * n] = np.sin(ang) * sign
    q = (GRID_W - 1 - p % GRID_W)[:, None]
    start = np.clip(q - 8, 0, GRID_W - 16)
    kc = np.arange(GRID_W)[None]
    c[:, C_WIN:C_WIN + GRID_W] = np.where((kc >= start) & (kc < start + 16), 0.0, BIG)
    c[0:4, C_PAIR:C_PAIR + 2] = np.tile(np.eye(2), (2, 1))
    c[:, C_HEAD:C_HEAD + 4] = p[:, None] // NAT_HD == np.arange(4)[None]
    rel = np.arange(384)[None] - 128 - p[:, None]
    c[:, C_ABS:C_ABS + 384] = np.abs(rel)
    c[:, C_REL:C_REL + 384] = rel
    c[:, C_MF:C_MF + 384] = (rel >= 0) / 16.0
    c[:, C_MB:C_MB + 384] = (rel <= 0) / 16.0
    f = np.arange(P)[None]
    c[:, C_TRI:C_TRI + P] = np.where(p[:, None] > f, BIG, 0.0)
    c[:, C_TRI + P:C_TRI + 2 * P] = np.where(f <= p[:, None], BIG, 0.0)
    c[:, C_TRI + 2 * P:C_TRI + 3 * P] = np.where(f > p[:, None], BIG, 0.0)
    return c


class Signal:

    def __init__(self, sem, name, loop, unit=1):
        self.sem, self.name, self.loop, self.unit = sem, name, loop, unit
        self.sent = self.taken = 0

    def up(self):
        self.sent += self.unit
        return self.unit

    def at(self, value):
        assert value > 0, self.name
        i, step = self.loop.get("i"), PER_LAYER.get(self.name, 0)
        return value if i is None or not step else i * step + value

    def now(self):
        return self.at(self.sent)

    def next(self, n=1):
        self.taken += n * self.unit
        return self.at(self.taken)


def build(nc, a, out, upto=99, counts=None):
    loop = {}
    with ExitStack() as ctx:
        def sb(name, shape, dt=F32):
            return ctx.enter_context(nc.sbuf_tensor(name, shape, dt))

        signals = {}

        def signal(name, unit=1):
            signals[name] = Signal(ctx.enter_context(nc.semaphore(name)), name, loop, unit)
            return signals[name]

        psum = ctx.enter_context(nc.psum_tensor("psum", [P, 8, BANK], F32))
        raw = sb("raw", [P, RING, BLOCK])
        wgt_hi = sb("wgt_hi", [P, RING, BLOCK], F32R)
        wgt_lo = sb("wgt_lo", [P, RING, BLOCK], F32R)
        X = sb("X", [P, 4, D])
        xh = sb("xh", [P, KT, 2 * T], F32R)
        xl = sb("xl", [P, KT, 2 * T], F32R)
        yh = sb("yh", [P, 4096], F32R)
        yl = sb("yl", [P, 4096], F32R)
        W = sb("W", [P, 13200])
        cst = sb("cst", [P, C_ABS])
        vt = sb("vt", [P, P])
        mod = sb("mod", [P, DEPTH, 6, KT, 2])
        silc = sb("silc", [P, KT, 2])
        sil4 = sb("sil4", [P, KT, 4], F32R)
        small = sb("small", [P, 352])
        yh_pad, yl_pad = xh[0:P // 2, 5, T:2 * T], xl[0:P // 2, 5, T:2 * T]

        ident = cst[:, C_ID:C_ID + P]
        pair_sum = cst[0:4, C_PAIR:C_PAIR + 2]
        U = X[:, 2:4, :]

        psum_full = signal("psum_full")
        weights_used = signal("weights_used")
        rows_used = signal("rows_used")
        values_done = signal("values_done")
        act_out = signal("act_out")
        dve_out = signal("dve_out")
        act_part = signal("act_part")
        dve_part = signal("dve_part")
        act_own = signal("act_own")
        dve_own = signal("dve_own")
        pool_own = signal("pool_own")
        high_done = signal("high_done")
        split_done = signal("split_done")
        x_ready = signal("x_ready")
        u_ready = signal("u_ready")
        var_ready = signal("var_ready")
        rstd_dve = signal("rstd_dve")
        bias_ready = signal("bias_ready")
        tab_free = signal("tab_free")
        layer_start = signal("layer_start")
        layer_start_act = signal("layer_start_act")
        layer_start_pool = signal("layer_start_pool")
        row_ready = signal("row_ready")
        conv_done = signal("conv_done")
        q_ready = signal("q_ready")
        probs_ready = signal("probs_ready")
        squares_used = signal("squares_used")
        raw_in = [signal(f"raw_in{s}", 16) for s in range(RING)]
        x_in = signal("x_in", 16)
        decay_in = signal("decay_in", 16)
        tab_in = signal("tab_in", 16)
        tri_in = signal("tri_in", 16)
        out_done = signal("out_done", 16)
        const_in = signal("const_in", 16)
        rows_in = signal("rows_in", 16)
        lay_in = signal("lay_in", 16)
        p_in = signal("p_in", 16)
        ln_in = signal("ln_in", 16)
        bias_in = [signal(f"bias_in{s}", 16) for s in range(2)]

        units = {}
        blocks, split_blocks = [], []
        bank = {"last": [None] * 8}
        owned = {"act": 0, "dve": 0}
        freed = {"act": act_out, "dve": dve_out}

        def open_unit(pe, key, owner):
            b = min((k for k in range(8) if not bank["last"][k] or "full" in units[bank["last"][k]]),
                    key=lambda k: units[bank["last"][k]]["full"] if bank["last"][k] else 0)
            if bank["last"][b]:
                last = units[bank["last"][b]]
                pe.wait_ge(freed[last["owner"]].sem, freed[last["owner"]].at(last["freed"]))
            assert key not in units, key
            units[key] = {"bank": b, "owner": owner}
            bank["last"][b] = key
            return psum[:, b, :]

        def close_unit(key, ins):
            u = units[key]
            owned[u["owner"]] += 1
            u["freed"] = owned[u["owner"]]
            ins.then_inc(psum_full.sem, psum_full.up())
            u["full"] = psum_full.sent
            u["need"] = len(split_blocks)

        def out_of(key):
            return freed[units[key]["owner"]].sem

        def emptied(key):
            return freed[units[key]["owner"]].at(units[key]["freed"])

        def filled(key):
            return psum_full.at(units[key]["full"])

        def bank_of(key):
            return psum[:, units[key]["bank"], :]

        def take_block(pe, source):
            n, shape = len(blocks), source(0).shape
            slot = n % RING
            raw_in[slot].sent += 16
            blocks.append({"index": n, "source": source, "shape": shape, "size": shape[1] * shape[2], "slot": slot,
                           "landed": raw_in[slot].sent, "release": (split_done, n + 1)})
            split_blocks.append({"block": blocks[n], "release": None})
            view = lambda t: t[:, slot, :blocks[n]["size"]].rearrange("p (a b) -> p a b", a=shape[1])
            pe.wait_ge(split_done.sem, split_done.at(n + 1))
            return view(wgt_hi), view(wgt_lo), n

        def release(s, ins=None, key=None):
            if key is None:
                ins.then_inc(weights_used.sem, weights_used.up())
            split_blocks[s]["release"] = (weights_used, weights_used.sent) if key is None else (psum_full, units[key]["full"])

        def wblock(w, k0, kn, c0, cn):
            return lambda i: w[k0 * P:(k0 + kn) * P, c0:c0 + cn].rearrange("(k p) n -> p k n", p=P)

        def lblock(w, k0, kn, c0, cn):
            return lambda i: w[i][k0 * P:(k0 + kn) * P, c0:c0 + cn].rearrange("(k p) n -> p k n", p=P)

        def view(lo, a_, b_):
            return W[:, lo:lo + a_ * b_].rearrange("p (a b) -> p a b", a=a_)

        gate_b, ln_gb = view(0, 2, D), view(2048, 2, D)
        r_tab, r_strip = view(2048, 4, 384), view(3584, 2, 384)
        rq, rk = view(4352, 2, 2 * T), view(5376, 2, 2 * T)
        rv, rg, rs = view(6400, 4, RET_V), view(8448, 4, RET_V), view(10496, 6, T)
        r_exp, r_swap = view(10496, 4, 384), view(12032, 2, T)
        mod_rows = [W[0:4, 12544:12544 + BANK], W[0:4, 10240:10240 + BANK]]
        nq, nk, nv = view(0, KT, T), view(2048, KT, 2 * T), view(6144, 4, D)
        n_bias = view(12288, 2, 384)
        n_q = view(11776, 2, T)
        n_prob, n_probT = view(10240, N_BUFS, 512), X[:, 2:4, :].rearrange("p a (b n) -> p (a b) n", n=512)
        nat_steps = [(qt, h) for h in range(NAT_HEADS) for qt in range(TT)]
        tri = W[:, 0:384]
        l_rows, sink, gbias = W[:, 12976:13104], W[:, 13104:13120], W[:, 13120:13128]
        l_p = view(640, TT, 256)
        rowv = [W[0:MH, 1152 + 256 * n:1408 + 256 * n] for n in range(8)]
        qk_post, qk_pre = view(3200, 16, T), view(7296, 16, T + 3)
        v_ext = W[:, 7296:7296 + 2 * MH * 257].rearrange("p (s h n) -> p s h n", s=2, h=MH)
        sig_o = view(9352, TT, D)
        m_arg, m_s = view(11440, 2, 384), view(12208, 2, 384)
        sig_g, merged = view(3200, TT, D), view(5248, TT, D)
        qn, kn, kT, av = view(7296, TT, D), view(9344, TT, 512), view(1152, AKV, T), view(2176, TT, 256)
        qT = view(10368, KT, T)
        squares = [W[:, 12416:12928], W[:, 2688:3200]]
        a_prob, a_probT = view(7296, A_BUFS, 512), view(8832, A_BUFS, 512)
        f_sil, f_v = view(11440, 2, T), view(11952, 2, T)
        diag = view(384, TT, P)
        v_ext_ones = v_ext[:, :, :, MHD:MHD + 1]
        a_groups = [(0, range(8 * (g // 2) + g % 2, 8 * (g // 2) + 8, 2)) for g in range(4)] + \
            [(1, range(8 * (g // 4) + g % 4 // 2 + 4 * (g % 2), 8 * (g // 4) + g % 4 // 2 + 4 * (g % 2) + 4, 2)) for g in range(8)]

        def a_buf(t, n):
            return t[:, n % A_BUFS, :]

        def hid(t, n_tok):
            return lambda kt, tt: t[:, kt * n_tok + tt * P:kt * n_tok + (tt + 1) * P]

        def x_op(t):
            return lambda kt, tt: t[:, kt, tt * P:(tt + 1) * P]

        def ff_at(t, x, kt):
            return t[:, kt * T:(kt + 1) * T] if kt < 16 else x[:, kt - 16, T:2 * T]

        seen = {}

        def rows_of(x):
            return x.rearrange("p (r c) -> p r c", c=GRID_W)

        def turned(x):
            return rows_of(x)[:, :, ::-1]

        block = ctx.enter_context(nc.Block())
        start = {}

        @block.tensor
        def _(pe):
            def mm(o, l, r, start_, stop):
                return pe.matmul(o, l, r, start=start_, stop=stop, skip_group_check=True)

            def mm3(o, lh, ll, rh, rl, start_, stop):
                mm(o, lh, rh, start_, False)
                mm(o, lh, rl, False, False)
                return mm(o, ll, rh, False, stop)

            def transposes(key, owner, tiles):
                o = open_unit(pe, key, owner)
                at = 0
                for t in tiles:
                    n, m = t.shape
                    ins = pe.transpose(o[0:m, at:at + n], t, ident[0:n, 0:n])
                    at += n
                close_unit(key, ins)

            def tokens_by_features(name, kts, col0, ncols, tts, oh, ol, owner, mkblock, split_k=None, after=None, ready=None):
                split_k = split_k or [(k, min(4, kts - k)) for k in range(0, kts, 4)]
                for c in range(ncols // BANK):
                    outs = {}
                    for k0, kn_ in split_k:
                        wh, wl, n = take_block(pe, mkblock(k0, kn_, col0 + c * BANK, BANK))
                        for tt in tts:
                            if k0 == 0:
                                outs[tt] = open_unit(pe, (name, c, tt), owner)
                            for k in range(kn_):
                                kt = k0 + k
                                if ready and c == 0 and tt == tts[0]:
                                    pe.wait_ge(out_of(ready(kt)), emptied(ready(kt)))
                                ins = mm3(outs[tt], oh(kt, tt), ol(kt, tt), wh[:, k, :], wl[:, k, :],
                                          kt == 0, kt == kts - 1)
                            if kt == kts - 1:
                                close_unit((name, c, tt), ins)
                        if kt < kts - 1:
                            release(n, ins)
                        else:
                            release(n, key=(name, c, tts[-1]))
                        if after:
                            after(c * len(split_k) + split_k.index((k0, kn_)))

            def features_by_tokens(name, col0, ntiles, n_tok, owner, mkblock, base=0, after=None, ready=None):
                for g in range(ntiles // 2):
                    wh, wl, n = take_block(pe, mkblock(0, KT, col0 + g * 2 * P, 2 * P))
                    for j in range(2):
                        key = (name, base + 2 * g + j)
                        o = open_unit(pe, key, owner)
                        for kt in range(KT):
                            if ready and g == j == 0:
                                pe.wait_ge(out_of(ready(kt)), emptied(ready(kt)))
                            ins = mm3(o[:, 0:n_tok], wh[:, kt, j * P:(j + 1) * P], wl[:, kt, j * P:(j + 1) * P],
                                      xh[:, kt, 0:n_tok], xl[:, kt, 0:n_tok], kt == 0, kt == KT - 1)
                        close_unit(key, ins)
                    release(n, key=key)
                    if after:
                        after(g)

            def modulation(layer, part, n):
                c, half = n // 2, n % 2
                wh, wl, s = take_block(pe, wblock(a["ada_w"][layer], 4 * half, 4, part * D + c * BANK, BANK))
                key = ("modr", layer, part, c)
                o = open_unit(pe, key, "act") if half == 0 else bank_of(key)
                for k in range(4):
                    kt = 4 * half + k
                    mm(o[0:4, :], sil4[:, kt, :], wh[:, k, :], kt == 0, False)
                    ins = mm(o[0:4, :], sil4[:, kt, :], wl[:, k, :], False, kt == KT - 1)
                if half == 0:
                    release(s, ins)
                else:
                    close_unit(key, ins)
                    release(s, key=key)
                if n == 2:
                    modulation_columns(layer, part, 0)

            def modulation_columns(layer, part, c=1):
                row, key = ("modr", layer, part, c), ("mod", layer, part)
                pe.wait_ge(out_of(row), emptied(row))
                o = open_unit(pe, key, "dve") if c == 0 else bank_of(key)
                for j in range(4):
                    kt = 4 * c + j
                    ins = mm(o[:, 2 * kt:2 * kt + 2], mod_rows[layer][:, j * P:(j + 1) * P], pair_sum, True, True)
                if c == 0:
                    ins.then_inc(rows_used.sem, rows_used.up())
                else:
                    close_unit(key, ins)

            def gates(layer, part, streams):
                pe.wait_ge(out_of(("mod", layer, part)), emptied(("mod", layer, part)))
                for s in range(streams):
                    for c in range(2):
                        key = ("gate", layer, part, s, c)
                        o = open_unit(pe, key, "act")
                        for j in range(4):
                            col = mod[:, layer, part, 4 * c + j, s:s + 1]
                            ins = mm(o[:, j * P:(j + 1) * P], col.to_broadcast([P, P]), ident, True, True)
                        close_unit(key, ins)

            def features_of(name, src, tts):
                per = 4 // len(tts)
                for u in range(KT // per):
                    transposes((name, u), "dve", [src[:, tt, kt * P:(kt + 1) * P]
                                                  for kt in range(per * u, per * u + per) for tt in tts])
                return lambda kt: (name, kt // per)

            def mlp(layer, tts, ready):
                n_tok = len(tts) * P
                for c in range(MLP_CHUNKS):
                    in_up = {1: 0, 3: 1} if layer == 0 else {}
                    in_down = {0: 2, 1: 3} if layer == 0 else {}
                    features_by_tokens(("up", layer), c * D, KT, n_tok, "dve",
                                       lambda *k: wblock(a["mlp_w1"][layer], *k), base=c * KT,
                                       after=lambda b: b in in_up and modulation(1, c, in_up[b]),
                                       ready=ready if c == 0 else None)
                    tokens_by_features(("down", layer, c), KT, 0, D, tts, hid(yh, n_tok), hid(yl, n_tok), "dve",
                                       lambda k0, kn_, c0, cn: wblock(a["mlp_w2"][layer], c * KT + k0, kn_, c0, cn),
                                       after=lambda b: b in in_down and modulation(1, c, in_down[b]),
                                       ready=lambda kt: (("up", layer), c * KT + kt))
                    if layer == 0:
                        modulation_columns(1, c)

            pe.wait_ge(const_in.sem, const_in.at(16))
            pe.wait_ge(rows_in.sem, rows_in.at(16 * 4))
            transposes(("vec",), "dve", [W[0:112, 0:P]])
            pe.wait_ge(act_part.sem, act_part.at(1))
            pe.wait_ge(out_of(("vec",)), emptied(("vec",)))
            pe.wait_ge(x_ready.sem, x_ready.next())
            for n in range(4):
                modulation(0, 0, n)
            for n in range(4):
                modulation(0, 1, n)
                if n == 0:
                    modulation_columns(0, 0)
            modulation_columns(0, 1)
            pe.wait_ge(x_in.sem, x_in.at(32))
            ready = features_of("h0", X, range(4))

            wb = lambda *k: wblock(a["ret_w_in"][0], *k)
            for h in range(RET_HEADS):
                features_by_tokens(("rq", h), h * T, 2, 2 * T, "dve", wb, ready=ready if h == 0 else None)
                modulation(0, 2 + h, 0)
                features_by_tokens(("rk", h), D + h * T, 2, 2 * T, "dve", wb)
                modulation(0, 2 + h, 1)
                tokens_by_features(("rv", h), KT, 2 * D + h * RET_V, RET_V, range(4), x_op(xh), x_op(xl), "act", wb)
                modulation(0, 2 + h, 2)
                pe.wait_ge(out_of((("rk", h), 1)), emptied((("rk", h), 1)))
                pe.wait_ge(out_of((("rv", h), 0, 3)), emptied((("rv", h), 0, 3)))
                for s in range(4):
                    n = T if s < 2 else 2 * T
                    o = open_unit(pe, ("rs", h, s), "dve")
                    for d in range(2):
                        ins = mm(o[:, 0:n], rk[:, d, s * P:(s + 1) * P], rq[:, d, 0:n], d == 0, d == 1)
                    close_unit(("rs", h, s), ins)
                modulation(0, 2 + h, 3)
                modulation_columns(0, 2 + h)
                pe.wait_ge(out_of(("rs", h, 3)), emptied(("rs", h, 3)))
                for tt in range(4):
                    o = open_unit(pe, ("ro", h, tt), "dve")
                    if tt < 2:
                        pairs = [(s, rs[:, s, tt * P:(tt + 1) * P]) for s in range(4)]
                    else:
                        pairs = [(s, rs[:, s + 2, (tt - 2) * P:(tt - 1) * P]) for s in (2, 3)]
                    for n, (s, l) in enumerate(pairs):
                        ins = mm(o, l, rv[:, s, :], n == 0, n == len(pairs) - 1)
                    close_unit(("ro", h, tt), ins)
                tokens_by_features(("rg", h), KT, 4 * D + h * RET_V, RET_V, range(4), x_op(xh), x_op(xl), "act", wb)
                if h == 0:
                    gates(0, 2, 2)
                pe.wait_ge(out_of(("ro", h, 3)), emptied(("ro", h, 3)))
                for f in range(4):
                    transposes(("ron", h, f), "dve", [rg[:, tt, f * P:(f + 1) * P] for tt in range(4)])
                tokens_by_features(("ry", h), 4, 0, D, range(4), hid(yh, 2 * T), hid(yl, 2 * T), "dve",
                                   lambda k0, kn_, c0, cn: wblock(a["ret_w_o"][0], 4 * h + k0, kn_, c0, cn),
                                   ready=lambda kt: ("ron", h, kt))
            gates(0, 5, 2)
            pe.wait_ge(x_ready.sem, x_ready.next(4))
            mlp(0, range(4), features_of("h0m", X, range(4)))

            pe.wait_ge(x_ready.sem, x_ready.next(4))
            wb = lambda *k: wblock(a["nat_w_in"][0], *k)
            features_by_tokens("nq", 0, KT, T, "act", wb, ready=features_of("h1", X, range(4)))
            features_by_tokens("nk", D, KT, 2 * T, "act", wb, after=lambda b: modulation(1, 4, b))
            tokens_by_features("nv", KT, 2 * D, D, range(4), x_op(xh), x_op(xl), "act", wb,
                               after=lambda b: (modulation(1, 5, b), b == 0 and modulation_columns(1, 4)))
            modulation_columns(1, 5)
            pe.wait_ge(out_of(("nv", 1, 3)), emptied(("nv", 1, 3)))

            def nat_scores(n):
                qt, h = nat_steps[n]
                if qt == 0:
                    pe.wait_ge(q_ready.sem, q_ready.next())
                o = open_unit(pe, ("ns", n), "act")
                close_unit(("ns", n), mm(o, n_q[:, h % 2, qt * P:(qt + 1) * P], nk[:, h // 4, :], True, True))

            def nat_transposes(n):
                pe.wait_ge(probs_ready.sem, probs_ready.next())
                transposes(("nt", n), "act", [n_prob[:, n % N_BUFS, s * P:(s + 1) * P] for s in range(4)])

            def nat_values(n):
                qt, h = nat_steps[n]
                key = ("no", h // 4)
                if h % 4 == qt == 0:
                    open_unit(pe, key, "dve")
                o = bank_of(key)[NAT_HD * (h % 4):NAT_HD * (h % 4 + 1), qt * P:(qt + 1) * P]
                pe.wait_ge(out_of(("nt", n)), emptied(("nt", n)))
                for s in range(4):
                    ins = mm(o, nv[:, s, h * NAT_HD:(h + 1) * NAT_HD], n_probT[:, n % N_BUFS, s * P:(s + 1) * P],
                             s == 0, s == 3)
                if h % 4 == 3 and qt == 1:
                    close_unit(key, ins)
                    seen["n", n] = (psum_full, units[key]["full"])
                else:
                    ins.then_inc(values_done.sem, values_done.up())
                    seen["n", n] = (values_done, values_done.sent)

            n_steps = len(nat_steps)
            for n in range(n_steps + N_LAG):
                if n < n_steps:
                    nat_scores(n)
                if LAG <= n < n_steps + LAG:
                    nat_transposes(n - LAG)
                if n >= N_LAG:
                    nat_values(n - N_LAG)
            gates(1, 2, 1)
            tokens_by_features("ny", KT, 0, D, range(2), hid(yh, T), hid(yl, T), "dve", lambda *k: wblock(a["nat_w_o"][0], *k),
                               ready=lambda kt: ("no", kt))
            gates(1, 5, 1)
            pe.wait_ge(x_ready.sem, x_ready.next(2))
            ready = features_of("h1m", X, range(2))
            mlp(1, range(2), ready)
            start["pe"] = {n: s_.sent for n, s_ in signals.items()}
            start.update(units=len(units), blocks=len(blocks), split=len(split_blocks), owned=dict(owned))
            if upto < 1:
                return

            def normed(name):
                pe.wait_ge(u_ready.sem, u_ready.next(2))
                for u in range(KT // 2):
                    o = open_unit(pe, (name, u), "dve")
                    for n in range(4):
                        kt, tt = 2 * u + n // 2, n % 2
                        ins = mm(o[:, n * P:(n + 1) * P], X[:, tt, kt * P:(kt + 1) * P], diag[:, tt, :], True, True)
                    close_unit((name, u), ins)
                return lambda kt: (name, kt // 2)

            def feed_forward(n, ready):
                gate, up, down = (a[f"ffn{n}_w_{x}_2"] for x in ("gate", "up", "down"))
                for g in range(FF_GROUPS):
                    cn, at = (2 * P, P) if g < FF_GROUPS - 1 else (D_FF - 2 * P * g, P // 2)
                    outs = {}
                    for half, w in ((0, gate), (1, up)):
                        wh, wl, s = take_block(pe, lblock(w, 0, KT, g * 2 * P, cn))
                        for j in range(2):
                            key = ("ff", n, 2 * g + j)
                            if half == 0:
                                outs[j] = open_unit(pe, key, "dve")
                            for kt in range(KT):
                                if g == half == j == 0:
                                    pe.wait_ge(out_of(ready(kt)), emptied(ready(kt)))
                                ins = mm3(outs[j][:, half * T:(half + 1) * T], wh[:, kt, j * at:j * at + P],
                                          wl[:, kt, j * at:j * at + P], xh[:, kt, 0:T], xl[:, kt, 0:T],
                                          kt == 0, kt == KT - 1)
                            if half:
                                close_unit(key, ins)
                        if half == 0:
                            release(s, ins)
                        else:
                            release(s, key=key)

                def rows(k0, kn_, c0, cn):
                    r0 = k0 * P if k0 < FF_TILES - 1 else D_FF - P
                    return lambda i: down[i][r0:r0 + kn_ * P, c0:c0 + cn].rearrange("(k p) n -> p k n", p=P)

                op = lambda t, x: lambda kt, tt: ff_at(t, x, kt)[:, tt * P:(tt + 1) * P]
                tokens_by_features(("fd", n), FF_TILES, 0, D, range(2), op(yh, xh), op(yl, xl), "dve", rows,
                                   [(0, 4), (4, 4), (8, 4), (12, 4), (16, 4), (20, 1), (21, 1)],
                                   ready=lambda kt: ("ff", n, kt))

            def hybrid_layer():
                pe.wait_ge(lay_in.sem, lay_in.at(16 * N_LAYER_DMAS))
                transposes(("lvec",), "act", [l_rows[0:V_ROWS, :]])
                feed_forward(1, normed("f1"))
                w = a["w_in_2"]
                wb = lambda *k: lblock(w, *k)
                ready = normed("mx")
                for g in range(8):
                    wh, wl, s = take_block(pe, wb(0, KT, O_QK + g * 2 * P, 2 * P))
                    o = open_unit(pe, ("mqk", g), "act")
                    for j in range(2):
                        for kt in range(KT):
                            if g == j == 0:
                                pe.wait_ge(out_of(ready(kt)), emptied(ready(kt)))
                            ins = mm3(o[:, j * T:(j + 1) * T], wh[:, kt, j * P:(j + 1) * P], wl[:, kt, j * P:(j + 1) * P],
                                      xh[:, kt, 0:T], xl[:, kt, 0:T], kt == 0, kt == KT - 1)
                    close_unit(("mqk", g), ins)
                    release(s, key=("mqk", g))
                wh, wl, s = take_block(pe, wb(0, KT, O_I, 2 * MH))
                o = open_unit(pe, ("mif",), "dve")
                for tt in range(TT):
                    for kt in range(KT):
                        ins = mm3(o[:, tt * 8:tt * 8 + 8], xh[:, kt, tt * P:(tt + 1) * P], xl[:, kt, tt * P:(tt + 1) * P],
                                  wh[:, kt, :], wl[:, kt, :], kt == 0, kt == KT - 1)
                close_unit(("mif",), ins)
                release(s, key=("mif",))
                tokens_by_features("mv", KT, O_V, D, range(2), x_op(xh), x_op(xl), "act", wb)
                pe.wait_ge(out_of(("mif",)), emptied(("mif",)))
                g8 = small[:, 64:80].rearrange("p (t g) -> p t g", t=TT)
                transposes(("mifT",), "dve", [g8[:, tt, c:c + MH] for c in (0, MH) for tt in range(TT)])
                tokens_by_features("mo", KT, O_O, D, range(2), x_op(xh), x_op(xl), "act", wb)
                pe.wait_ge(x_ready.sem, x_ready.next())
                pe.wait_ge(row_ready.sem, row_ready.next())
                o = open_unit(pe, ("mcol",), "dve")
                for n in range(4):
                    ins = mm(o[:, MH * n:MH * (n + 1)], rowv[4 if n < 2 else 7][:, (n % 2) * P:(n % 2 + 1) * P],
                             ident[0:MH, 0:MH], True, True)
                close_unit(("mcol",), ins)

                def mscores(h):
                    o = open_unit(pe, ("mb", h), "dve")
                    close_unit(("mb", h), mm(o[:, 0:T], ident[0:MH, h:h + 1].to_broadcast([MH, P]), rowv[6], True, True))
                    if h == 0:
                        pe.wait_ge(conv_done.sem, conv_done.next())
                    o = open_unit(pe, ("ms", h), "dve")
                    for lo, s, t0 in ((0, 0, 0), (T, 1, P)):
                        for d in range(2):
                            ins = mm(o[:, lo:lo + T - t0], qk_post[:, 8 + 2 * h + d, s * P:(s + 1) * P],
                                     qk_post[:, 2 * h + d, t0:T], d == 0, d == 1)
                    close_unit(("ms", h), ins)

                def mvalues(h):
                    pe.wait_ge(out_of(("ms", h)), emptied(("ms", h)))
                    if h == 0:
                        pe.wait_ge(out_of(("mv", 1, 1)), emptied(("mv", 1, 1)))
                    for tt in range(TT):
                        o = open_unit(pe, ("mn", h, tt), "dve")
                        for n, lo in enumerate((0,) if tt == 0 else (P, T)):
                            ins = mm(o[:, 0:MHD + 1], m_s[:, h % 2, lo:lo + P], v_ext[:, n, h, :], n == 0, n == tt)
                        close_unit(("mn", h, tt), ins)

                for h in range(MH + 1):
                    if h < MH:
                        mscores(h)
                    if h:
                        mvalues(h - 1)
                tokens_by_features("gm", KT, O_GM, D, range(2), x_op(xh), x_op(xl), "act", wb)
                pe.wait_ge(out_of(("mn", MH - 1, 1)), emptied(("mn", MH - 1, 1)))
                ready = features_of("hmT", U, range(2))
                tokens_by_features("bm", KT, 0, D, range(2), hid(yh, T), hid(yl, T), "dve",
                                   lambda *k: lblock(a["w_branch_m_2"], *k), ready=ready)
                tokens_by_features("aq", KT, O_AQ, D, range(2), x_op(xh), x_op(xl), "dve", wb)
                tokens_by_features("ak", KT, O_AK, BANK, range(2), x_op(xh), x_op(xl), "dve", wb)
                tokens_by_features("ga", KT, O_GA, D, range(2), x_op(xh), x_op(xl), "act", wb)
                pe.wait_ge(out_of(("aq", 1, 1)), emptied(("aq", 1, 1)))
                for u in range(4):
                    transposes(("qT", u), "act", [qn[:, tt, kt * P:(kt + 1) * P] for kt in (2 * u, 2 * u + 1) for tt in range(TT)])
                pe.wait_ge(out_of(("ak", 0, 1)), emptied(("ak", 0, 1)))
                for u in range(2):
                    transposes(("kT", u), "act", [kn[:, tt, j * P:(j + 1) * P] for j in (2 * u, 2 * u + 1) for tt in range(TT)])
                pe.wait_ge(out_of(("kT", 1)), emptied(("kT", 1)))

                def ascores(n):
                    qt, heads = a_groups[n]
                    o = open_unit(pe, ("as", n), "act")
                    w_ = BANK // len(heads)
                    for j, h in enumerate(heads):
                        p0 = AHD * (h % 2)
                        ins = mm(o[:, j * w_:(j + 1) * w_], qT[p0:p0 + AHD, h // 2, qt * P:(qt + 1) * P],
                                 kT[p0:p0 + AHD, h // 4, 0:w_], True, True)
                    close_unit(("as", n), ins)

                def atransposes(n):
                    pe.wait_ge(out_of(("as", n)), emptied(("as", n)))
                    transposes(("at", n), "act" if n % 2 else "dve", [a_buf(a_prob, n)[:, s * P:(s + 1) * P] for s in range(4)])

                def avalues(n):
                    qt, heads = a_groups[n]
                    per = 2 if qt == 0 else 4
                    m = n if qt == 0 else n - 4
                    key = ("ao", qt, m // per)
                    if m % per == 0:
                        open_unit(pe, key, "dve")
                    o = psum[:, units[key]["bank"], :]
                    pe.wait_ge(out_of(("at", n)), emptied(("at", n)))
                    for j, h in enumerate(heads):
                        c = (h % 8) * AHD
                        for s in range(qt + 1):
                            at = (j * (qt + 1) + s) * P
                            ins = mm(o[:, c:c + AHD], a_buf(a_probT, n)[:, at:at + P],
                                     av[:, s, (h // 4) * AHD:(h // 4 + 1) * AHD], s == 0, s == qt)
                    if m % per == per - 1:
                        close_unit(key, ins)
                        seen["a", n] = (psum_full, units[key]["full"])
                    else:
                        ins.then_inc(values_done.sem, values_done.up())
                    seen["a", n] = (values_done, values_done.sent)

                for n in range(len(a_groups) + N_LAG):
                    if n < len(a_groups):
                        ascores(n)
                    if LAG <= n < len(a_groups) + LAG:
                        atransposes(n - LAG)
                    if n >= N_LAG:
                        avalues(n - N_LAG)
                pe.wait_ge(out_of(("ao", 1, 1)), emptied(("ao", 1, 1)))
                ready = features_of("haT", U, range(2))
                tokens_by_features("ba", KT, 0, D, range(2), hid(yh, T), hid(yl, T), "dve",
                                   lambda *k: lblock(a["w_branch_a_2"], *k), ready=ready)
                pe.wait_ge(out_of(("ba", 1, 1)), emptied(("ba", 1, 1)))
                ready = features_of("mg", merged, range(2))
                tokens_by_features("wo", KT, 0, D, range(2), x_op(xh), x_op(xl), "dve",
                                   lambda *k: lblock(a["w_out_2"], *k), ready=ready)
                feed_forward(2, normed("f2"))
                ready = normed("pl")
                pe.wait_ge(p_in.sem, p_in.at(16))
                transposes(("pT",), "dve", [l_p[:, tt, kt * P:(kt + 1) * P] for kt in range(2) for tt in range(TT)])
                tokens_by_features("pg", KT, 0, D, range(2), x_op(xh), x_op(xl), "act",
                                   lambda *k: lblock(a["ple_gate_w_2"], *k), ready=ready)
                pe.wait_ge(out_of(("pT",)), emptied(("pT",)))
                wh, wl, s = take_block(pe, lblock(a["ple_proj_w_2"], 0, 2, 0, D))
                for c in range(2):
                    for tt in range(TT):
                        o = open_unit(pe, ("pp", c, tt), "dve")
                        for kt in range(2):
                            ins = mm3(o, hid(yh, T)(kt, tt), hid(yl, T)(kt, tt), wh[:, kt, c * BANK:(c + 1) * BANK],
                                      wl[:, kt, c * BANK:(c + 1) * BANK], kt == 0, kt == 1)
                        close_unit(("pp", c, tt), ins)
                release(s, key=("pp", 1, 1))

            with pe.Fori(0, DEPTH) as i:
                loop["i"] = i
                pe.wait_ge(act_out.sem, act_out.at(owned["act"]))
                pe.wait_ge(dve_out.sem, dve_out.at(owned["dve"]))
                pe.wait_ge(layer_start.sem, layer_start.next())
                bank["last"] = [None] * 8
                hybrid_layer()
            loop["i"] = None

        @block.scalar
        def _(act):
            def act_(o, i, f=ACT.Copy, **k):
                return nc.scalar.activation(o, i, f, **k)

            def operand(key, dst, affine=()):
                act.wait_ge(psum_full.sem, filled(key))
                o = bank_of(key)
                for n, (c, sc, sh) in enumerate(affine):
                    ins = act_(o[:, c[0]:c[1]], o[:, c[0]:c[1]], ACT.Identity, scale=sc, bias=sh)
                if affine:
                    ins.then_inc(act_own.sem, act_own.up())
                    act.wait_ge(act_own.sem, act_own.now())
                act_(dst, o[:, 0:int(np.prod(dst.shape[1:]))]).then_inc(act_part.sem, act_part.up())

            def operand_x(name, layer, part, streams):
                dve_owner = ("mod", layer, part + 1)
                act.wait_ge(out_of(dve_owner), emptied(dve_owner))
                for kt in range(KT):
                    m = lambda j, s: mod[:, layer, part + j, kt, s:s + 1]
                    if streams == 2:
                        operand((name, kt), xh[:, kt, :],
                                [((s * T, (s + 1) * T), m(1, s), m(0, s)) for s in range(2)])
                    elif kt % 2:
                        k0 = kt - 1
                        operand((name, kt // 2), xh[:, k0:k0 + 2, 0:T],
                                [((j * T, (j + 1) * T), mod[:, layer, part + 1, k0 + j, 0:1],
                                  mod[:, layer, part, k0 + j, 0:1]) for j in range(2)])

            def mod_row(layer, part, c):
                act.wait_ge(psum_full.sem, filled(("modr", layer, part, c)))
                before = ("mod", *divmod(6 * layer + part - 1, 6))
                if c == 1:
                    act.wait_ge(rows_used.sem, rows_used.next())
                elif before in units:
                    act.wait_ge(psum_full.sem, filled(before))
                o = bank_of(("modr", layer, part, c))
                act_(mod_rows[layer], o[0:4, :]).then_inc(act_out.sem, act_out.up())

            def gates(layer, part, streams, used=None):
                if used:
                    act.wait_ge(out_of(used), emptied(used))
                for s in range(streams):
                    for c in range(2):
                        act.wait_ge(psum_full.sem, filled(("gate", layer, part, s, c)))
                        o = bank_of(("gate", layer, part, s, c))
                        act_(gate_b[:, s, c * BANK:(c + 1) * BANK], o).then_inc(act_out.sem, act_out.up())

            def mlp(layer, tts):
                n = len(tts) * P
                for t in range(MLP_CHUNKS * KT):
                    if layer == 0 and t and t % KT == 0:
                        mod_row(1, t // KT - 1, 0)
                        mod_row(1, t // KT - 1, 1)
                    kt = t % KT
                    act.wait_ge(psum_full.sem, filled((("up", layer), t)))
                    o = bank_of((("up", layer), t))[:, 0:n]
                    act_(o, o, ACT.Relu).then_inc(act_own.sem, act_own.up())
                    act.wait_ge(act_own.sem, act_own.now())
                    act_(o, o, ACT.Square).then_inc(act_own.sem, act_own.up())
                    act.wait_ge(act_own.sem, act_own.now())
                    act_(yh[:, kt * n:(kt + 1) * n], o).then_inc(act_part.sem, act_part.up())
                if layer == 0:
                    mod_row(1, MLP_CHUNKS - 1, 0)
                    mod_row(1, MLP_CHUNKS - 1, 1)

            def load_bias(h):
                for rr in range(2):
                    dst = n_bias[rr * GRID_W:(rr + 1) * GRID_W, h % 2, :].rearrange("p (e k) -> p e k", k=GRID_W)
                    src = a["nat_rpb"][0, h]
                    src = bass.AP(src.tensor, src.offset + (5 - rr) * NAT_BIAS_COLS + 15 - (GRID_W - 1),
                                  [[1, GRID_W], [NAT_BIAS_COLS, 6], [1, GRID_W]])
                    act.dma_start(dst, src).then_inc(bias_in[h % 2].sem, bias_in[h % 2].up())

            for r, x, n in ((0, a["c"], 8), (8, a["c_ctx"].unsqueeze(0), 8), (16, a["ada_b"][0:1], 48), (64, a["ada_b"][1:2], 48)):
                act.dma_start(W[r:r + n, 0:P], x.rearrange("a (r n) -> (a r) n", n=P)).then_inc(rows_in.sem, rows_in.up())
            act.dma_start(cst[:, :], a["consts"][:, 0:C_ABS]).then_inc(const_in.sem, const_in.up())
            act.dma_start(small[:, 0:8], a["ret_decay"].rearrange("a b h -> a (b h)").to_broadcast([P, 8])).then_inc(decay_in.sem, decay_in.up())
            act.dma_start(X[:, 0:TT, :], a["x"][0].rearrange("(t p) n -> p t n", p=P)).then_inc(x_in.sem, x_in.up())
            act.dma_start(X[:, TT:2 * TT, :], a["ctx"][0].rearrange("(t p) n -> p t n", p=P)).then_inc(x_in.sem, x_in.up())
            act.dma_start(r_tab, a["consts"][:, C_ABS:C_ABS + 1536].rearrange("p (a b) -> p a b", a=4)).then_inc(tab_in.sem, tab_in.up())
            act.wait_ge(psum_full.sem, filled(("vec",)))
            o = bank_of(("vec",))
            act_(silc[:, :, :], o[:, 0:16].rearrange("p (s k) -> p k s", s=2), ACT.Silu).then_inc(act_part.sem, act_part.up())
            act.wait_ge(decay_in.sem, decay_in.at(16))
            act_(small[:, 8:16], small[:, 0:8], ACT.Exp).then_inc(act_part.sem, act_part.up())
            for part in range(2):
                for c in range(2):
                    mod_row(0, part, c)
            operand_x("h0", 0, 0, 2)

            for h in range(RET_HEADS):
                if h == 0:
                    act.wait_ge(dve_part.sem, dve_part.next())
                    act.wait_ge(tab_in.sem, tab_in.at(16))
                f, b = small[:, 16 + h:17 + h], small[:, 20 + h:21 + h]
                b_pos = small[:, 12 + h:13 + h]
                f256, b256 = small[:, 24 + h:25 + h], small[:, 28 + h:29 + h]
                act_(r_exp[:, 0, :], r_tab[:, 0, :], ACT.Exp, scale=f)
                act_(r_exp[:, 1, :], r_tab[:, 0, :], ACT.Exp, scale=b)
                act_(r_exp[:, 2, :], r_tab[:, 1, :], ACT.Exp, scale=f, bias=f256)
                act_(r_exp[:, 3, :], r_tab[:, 1, :], ACT.Exp, scale=b_pos, bias=b256).then_inc(act_part.sem, act_part.up())
                for name, dst in (("rq", rq), ("rk", rk)):
                    for d in range(2):
                        key = ((name, h), d)
                        act.wait_ge(psum_full.sem, filled(key))
                        o = bank_of(key)
                        prev = (("rq", h), d) if name == "rk" else (("rk", h - 1), d)
                        if prev in units:
                            act.wait_ge(out_of(prev), emptied(prev))
                        sw = r_swap[:, d, :]
                        act_(sw[0:64, :], o[64:128, 0:T])
                        act_(sw[64:128, :], o[0:64, 0:T])
                        act_(dst[:, d, T:2 * T], o[:, T:2 * T]).then_inc(act_part.sem, act_part.up())
                mod_row(0, 2 + h, 0)
                for tt in range(4):
                    act.wait_ge(psum_full.sem, filled((("rv", h), 0, tt)))
                    act_(rv[:, tt, :], bank_of((("rv", h), 0, tt))).then_inc(act_out.sem, act_out.up())
                mod_row(0, 2 + h, 1)
                for tt in range(4):
                    act.wait_ge(psum_full.sem, filled((("rg", h), 0, tt)))
                    act_(rg[:, tt, :], bank_of((("rg", h), 0, tt)), ACT.Silu).then_inc(act_out.sem, act_out.up())
                if h == 0:
                    gates(0, 2, 2)
                for ft in range(4):
                    operand(("ron", h, ft), yh[:, ft * 2 * T:(ft + 1) * 2 * T])

            gates(0, 5, 2, (("ry", RET_HEADS - 1), 1, 3))
            operand_x("h0m", 0, 3, 2)
            load_bias(0)
            load_bias(1)
            mlp(0, range(4))

            operand_x("h1", 1, 0, 2)
            for t in range(KT):
                act.wait_ge(psum_full.sem, filled(("nq", t)))
                act_(rows_of(nq[:, t, :]), turned(bank_of(("nq", t))[:, 0:T]), scale=NAT_HD ** -0.5).then_inc(act_out.sem, act_out.up())
            for t in range(KT):
                act.wait_ge(psum_full.sem, filled(("nk", t)))
                act_(nk[:, t, :], bank_of(("nk", t))).then_inc(act_out.sem, act_out.up())
                if t % 4 == 3:
                    mod_row(1, 4, t // 4)
            for c in range(2):
                for tt in range(4):
                    act.wait_ge(psum_full.sem, filled(("nv", c, tt)))
                    act_(nv[:, tt, c * BANK:(c + 1) * BANK], bank_of(("nv", c, tt))).then_inc(act_out.sem, act_out.up())
                mod_row(1, 5, c)
            n_steps = len(nat_steps)
            for n in range(n_steps + N_LAG):
                if n < n_steps:
                    qt, h = nat_steps[n]
                    c = 32 * qt + h
                    act.wait_ge(dve_part.sem, dve_part.next())
                    if n >= N_BUFS:
                        act.wait_ge(psum_full.sem, psum_full.at(units[("nt", n - N_BUFS)]["full"]))
                    o = psum[:, units[("ns", n)]["bank"], :]
                    act_(n_prob[:, n % N_BUFS, :], o, ACT.Exp, bias=small[:, 192 + c:193 + c],
                                      accum_out=small[:, 256 + c:257 + c]).then_inc(act_out.sem, act_out.up())
                    if qt == 1 and h + 2 < NAT_HEADS:
                        load_bias(h + 2)
                m = n - LAG
                if 0 <= m < n_steps:
                    act.wait_ge(psum_full.sem, filled(("nt", m)))
                    if m >= N_BUFS:
                        s_, v_ = seen["n", m - N_BUFS]
                        act.wait_ge(s_.sem, s_.at(v_))
                    act_(n_probT[:, m % N_BUFS, :], bank_of(("nt", m))).then_inc(act_out.sem, act_out.up())
                m = n - N_LAG
                if m >= 0 and m % 8 == 7:
                    kt = m // 8
                    act.wait_ge(psum_full.sem, filled(("no", kt)))
                    act_(rows_of(yh[:, kt * T:(kt + 1) * T]), turned(bank_of(("no", kt))[:, 0:T])).then_inc(act_part.sem, act_part.up())
            gates(1, 2, 1)
            gates(1, 5, 1, ("ny", 1, 1))
            operand_x("h1m", 1, 3, 1)
            mlp(1, range(2))
            if upto < 1:
                return

            def normed(name, col, final):
                for c in range(2):
                    for tt in range(TT):
                        if final is not None:
                            act.wait_ge(out_of((*final, c, tt)), emptied((*final, c, tt)))
                        at = 80 + 2 * c + tt
                        cols = slice(c * BANK, (c + 1) * BANK)
                        ins = act_(U[:, tt, cols], X[:, tt, cols], ACT.Square, accum_out=small[:, at:at + 1])
                ins.then_inc(act_part.sem, act_part.up())
                for u in range(4):
                    act.wait_ge(psum_full.sem, filled((name, u)))
                    o = bank_of((name, u))
                    for j in range(2):
                        ins = act_(xh[:, 2 * u + j, 0:T], o[:, j * T:(j + 1) * T], scale=vt[:, col + 2 * u + j:col + 2 * u + j + 1])
                    ins.then_inc(act_part.sem, act_part.up())

            def feed_forward(n):
                for t in range(FF_TILES):
                    act.wait_ge(psum_full.sem, filled(("ff", n, t)))
                    o = bank_of(("ff", n, t))
                    if t >= 2:
                        act.wait_ge(out_of(("ff", n, t - 2)), emptied(("ff", n, t - 2)))
                    act_(f_sil[:, t % 2, :], o[:, 0:T], ACT.Silu).then_inc(act_part.sem, act_part.up())

            def hybrid_layer():
                act.wait_ge(psum_full.sem, filled(("lvec",)))
                act_(vt[:, 0:V_ROWS], bank_of(("lvec",))[:, 0:V_ROWS]).then_inc(act_out.sem, act_out.up())
                act.wait_ge(out_of(("lvec",)), emptied(("lvec",)))
                normed("f1", V_FFN1, None)
                feed_forward(1)
                normed("mx", V_MIX, (("fd", 1),))
                for g in range(8):
                    act.wait_ge(psum_full.sem, filled(("mqk", g)))
                    o = bank_of(("mqk", g))
                    act_(qk_pre[:, 2 * g:2 * g + 2, 3:T + 3], o.rearrange("p (j t) -> p j t", j=2)).then_inc(act_out.sem, act_out.up())
                for g in range(4):
                    act.wait_ge(dve_part.sem, dve_part.next())
                    ins = act_(qk_post[:, 4 * g:4 * g + 4, :], qk_post[:, 4 * g:4 * g + 4, :], ACT.Silu)
                ins.then_inc(conv_done.sem, conv_done.up())
                for c in range(2):
                    for tt in range(TT):
                        act.wait_ge(psum_full.sem, filled(("mv", c, tt)))
                        o = bank_of(("mv", c, tt)).rearrange("p (h n) -> p h n", h=2)
                        act_(v_ext[:, tt, 2 * c:2 * c + 2, 0:MHD], o).then_inc(act_out.sem, act_out.up())
                act.wait_ge(dve_part.sem, dve_part.next())
                act_(rowv[2], rowv[2], ACT.Exp).then_inc(act_own.sem, act_own.up())
                act.wait_ge(act_own.sem, act_own.now())
                act_(rowv[2], rowv[2], ACT.Ln, bias=1.0).then_inc(act_part.sem, act_part.up())
                act.wait_ge(dve_part.sem, dve_part.next())
                act_(rowv[7], rowv[5], ACT.Exp, scale=-1.0).then_inc(row_ready.sem, row_ready.up())
                for c in range(2):
                    for tt in range(TT):
                        act.wait_ge(psum_full.sem, filled(("mo", c, tt)))
                        act_(sig_o[:, tt, c * BANK:(c + 1) * BANK], bank_of(("mo", c, tt)), ACT.Sigmoid).then_inc(act_out.sem, act_out.up())
                for h in range(MH + 1):
                    if h < MH:
                        act.wait_ge(out_of(("mb", h)), emptied(("mb", h)))
                        act_(m_arg[:, h % 2, :], m_arg[:, h % 2, :], ACT.Exp).then_inc(act_part.sem, act_part.up())
                    if h:
                        for tt in range(TT):
                            act.wait_ge(psum_full.sem, filled(("mn", h - 1, tt)))
                            o = bank_of(("mn", h - 1, tt))
                            act.wait_ge(dve_part.sem, dve_part.next())
                            act_(U[:, tt, (h - 1) * MHD:h * MHD], o[:, 0:MHD], ACT.Square, scale=small[:, 88:89],
                                               accum_out=small[:, 89:90]).then_inc(act_part.sem, act_part.up())
                for c in range(2):
                    for tt in range(TT):
                        act.wait_ge(psum_full.sem, filled(("gm", c, tt)))
                        act_(sig_g[:, tt, c * BANK:(c + 1) * BANK], bank_of(("gm", c, tt)), ACT.Sigmoid).then_inc(act_out.sem, act_out.up())
                for u in range(4):
                    act.wait_ge(psum_full.sem, filled(("hmT", u)))
                    o = bank_of(("hmT", u))
                    for j in range(2):
                        ins = act_(yh[:, (2 * u + j) * T:(2 * u + j + 1) * T], o[:, j * T:(j + 1) * T],
                                   scale=vt[:, V_MO + 2 * u + j:V_MO + 2 * u + j + 1])
                    ins.then_inc(act_part.sem, act_part.up())
                for name in (("aq", 0), ("aq", 1), ("ak", 0)):
                    for tt in range(TT):
                        act.wait_ge(psum_full.sem, filled((*name, tt)))
                        o = bank_of((*name, tt))
                        n = 512 if name[0] == "aq" else 256
                        if name[0] == "ak":
                            act_(av[:, tt, :], o[:, 256:512])
                        if name != ("aq", 0):
                            act.wait_ge(squares_used.sem, squares_used.next())
                        act_(squares[tt][:, 0:n], o[:, 0:n], ACT.Square).then_inc(act_part.sem, act_part.up())
                act.wait_ge(squares_used.sem, squares_used.next(2))
                act.wait_ge(out_of(("bm", 1, 1)), emptied(("bm", 1, 1)))
                for c in range(2):
                    for tt in range(TT):
                        act.wait_ge(psum_full.sem, filled(("ga", c, tt)))
                        act_(sig_g[:, tt, c * BANK:(c + 1) * BANK], bank_of(("ga", c, tt)), ACT.Sigmoid).then_inc(act_out.sem, act_out.up())
                for u in range(4):
                    act.wait_ge(psum_full.sem, filled(("qT", u)))
                    o = bank_of(("qT", u)).rearrange("p (j t) -> p j t", j=2)
                    act_(qT[:, 2 * u:2 * u + 2, :], o, scale=vt[:, V_AQ:V_AQ + 1]).then_inc(act_out.sem, act_out.up())
                for u in range(2):
                    act.wait_ge(psum_full.sem, filled(("kT", u)))
                    o = bank_of(("kT", u)).rearrange("p (j t) -> p j t", j=2)
                    act_(kT[:, 2 * u:2 * u + 2, :], o, scale=vt[:, V_AK:V_AK + 1]).then_inc(act_out.sem, act_out.up())
                for n in range(len(a_groups) + LAG):
                    if n < len(a_groups):
                        qt, heads = a_groups[n]
                        w_ = BANK // len(heads)
                        act.wait_ge(dve_part.sem, dve_part.next())
                        if n >= A_BUFS:
                            act.wait_ge(psum_full.sem, psum_full.at(units[("at", n - A_BUFS)]["full"]))
                        o = psum[:, units[("as", n)]["bank"], :]
                        for j, h in enumerate(heads):
                            c = 16 * qt + h
                            ins = act_(a_buf(a_prob, n)[:, j * w_:(j + 1) * w_], o[:, j * w_:(j + 1) * w_], ACT.Exp,
                                       scale=AHD ** -0.5, bias=small[:, 96 + c:97 + c], accum_out=small[:, 128 + c:129 + c])
                        c = 16 * qt + heads[0]
                        es = small[:, 160 + c:160 + c + 2 * len(heads) - 1:2]
                        act_(es, es, ACT.Exp).then_inc(act_out.sem, act_out.up())
                    m = n - LAG
                    if m >= 0 and units[("at", m)]["owner"] == "act":
                        act.wait_ge(psum_full.sem, filled(("at", m)))
                        if m >= A_BUFS:
                            s_, v_ = seen["a", m - A_BUFS]
                            act.wait_ge(s_.sem, s_.at(v_))
                        act_(a_buf(a_probT, m), bank_of(("at", m))).then_inc(act_out.sem, act_out.up())
                for u in range(4):
                    operand(("haT", u), yh[:, u * 512:(u + 1) * 512])
                for u in range(4):
                    operand(("mg", u), xh[:, 2 * u:2 * u + 2, 0:T])
                normed("f2", V_FFN2, ("wo",))
                feed_forward(2)
                normed("pl", V_PLE, (("fd", 2),))
                operand(("pT",), yh[:, 0:512])
                for c in range(2):
                    for tt in range(TT):
                        act.wait_ge(psum_full.sem, filled(("pg", c, tt)))
                        act_(sig_g[:, tt, c * BANK:(c + 1) * BANK], bank_of(("pg", c, tt)), ACT.Sigmoid).then_inc(act_out.sem, act_out.up())

            start["act"] = {n: s_.sent for n, s_ in signals.items()}
            with act.Fori(0, DEPTH) as i:
                loop["i"] = i
                act.wait_ge(layer_start_act.sem, layer_start_act.next())
                hybrid_layer()
            loop["i"] = None

        @block.vector
        def _(dve):
            v = nc.vector
            split = {"next": 0, "limit": start["split"]}

            def keep_up(key, ahead=2):
                u = units[key]
                while split["next"] < min(u["need"] + ahead, split["limit"]):
                    s = split["next"]
                    b = split_blocks[s]["block"]
                    split["next"] += 1
                    size = b["size"]
                    dve.wait_ge(raw_in[b["slot"]].sem, raw_in[b["slot"]].at(b["landed"]))
                    if s - RING >= split["base"]:
                        sig, val = split_blocks[s - RING]["release"]
                        dve.wait_ge(sig.sem, sig.at(val))
                    r = raw[:, b["slot"], :size]
                    v.tensor_copy(wgt_hi[:, s % RING, :size], r).then_inc(high_done.sem, high_done.up())
                    dve.wait_ge(high_done.sem, high_done.now())
                    v.tensor_tensor(wgt_lo[:, s % RING, :size], r, wgt_hi[:, s % RING, :size], ALU.subtract).then_inc(split_done.sem, split_done.up())

            split["base"] = 0

            def low(key, dst_lo, dst_hi, ahead=2):
                keep_up(key, ahead)
                dve.wait_ge(psum_full.sem, filled(key))
                o = bank_of(key)
                dve.wait_ge(act_part.sem, act_part.next())
                n = int(np.prod(dst_lo.shape[1:]))
                v.tensor_tensor(dst_lo, like(o[:, 0:n], dst_lo), dst_hi, ALU.subtract).then_inc(dve_out.sem, dve_out.up())

            def like(o, dst):
                return o if len(dst.shape) == 2 else o.rearrange("p (a b) -> p a b", a=dst.shape[1])

            def low_scaled(key, cols, lo, hi):
                keep_up(key, 1)
                dve.wait_ge(psum_full.sem, filled(key))
                o = bank_of(key)
                dve.wait_ge(act_part.sem, act_part.next())
                for j, c in enumerate(cols):
                    ins = v.scalar_tensor_tensor(out=lo(j), in0=o[:, j * T:(j + 1) * T], scalar=vt[:, c:c + 1],
                                                 in1=hi(j), op0=ALU.mult, op1=ALU.subtract)
                ins.then_inc(dve_out.sem, dve_out.up())

            def low_x(name, tts):
                for u in range(KT // (4 // len(tts))):
                    if len(tts) == 4:
                        low((name, u), xl[:, u, :], xh[:, u, :], 1)
                    else:
                        low((name, u), xl[:, 2 * u:2 * u + 2, 0:T], xh[:, 2 * u:2 * u + 2, 0:T], 1)

            def modulation(layer, part):
                keep_up(("mod", layer, part), 1)
                dve.wait_ge(psum_full.sem, filled(("mod", layer, part)))
                o = bank_of(("mod", layer, part))
                c = 16 + 48 * layer + 8 * part
                bias = vt[:, c:c + 8].unsqueeze(2).to_broadcast([P, KT, 2])
                v.scalar_tensor_tensor(
                    out=mod[:, layer, part], in0=o[:, 0:16].rearrange("p (k s) -> p k s", s=2),
                    scalar=1.0 if part in (1, 4) else 0.0, in1=bias, op0=ALU.add, op1=ALU.add).then_inc(dve_out.sem, dve_out.up())

            def prescale(tts):
                for tt in tts:
                    ins = v.tensor_scalar(X[:, tt, :], X[:, tt, :], ALPHA, None, ALU.mult)
                ins.then_inc(dve_own.sem, dve_own.up())
                dve.wait_ge(dve_own.sem, dve_own.now())

            def add_gated(key, tt, c, gate, ahead=2):
                keep_up(key, ahead)
                dve.wait_ge(psum_full.sem, filled(key))
                o = bank_of(key)
                s = tt // TT
                dve.wait_ge(out_of(gate), emptied(gate))
                v.tensor_tensor(o, o, gate_b[:, s, c * BANK:(c + 1) * BANK], ALU.mult).then_inc(dve_own.sem, dve_own.up())
                dve.wait_ge(dve_own.sem, dve_own.now())
                x = X[:, tt, c * BANK:(c + 1) * BANK]
                v.tensor_tensor(x, o, x, ALU.add).then_inc(dve_out.sem, dve_out.up())

            def add_and_norm(tts, key, gate):
                stats = small[:, 32:32 + 12 * len(tts)].rearrange("p (t s) -> p t s", t=len(tts))
                for c in range(2):
                    for tt in tts:
                        add_gated(key(c, tt), tt, c, gate, 2 - 2 * c)
                        x, st, mv = X[:, tt, :], stats[:, tt, :], small[:, 80 + 2 * tt:82 + 2 * tt]
                        dve.wait_ge(dve_out.sem, dve_out.now())
                        v.bn_stats(st[:, 6 * c:6 * c + 6], X[:, tt, c * BANK:(c + 1) * BANK]).then_inc(dve_own.sem, dve_own.up())
                        if c == 0:
                            continue
                        dve.wait_ge(dve_own.sem, dve_own.now())
                        v.bn_aggr(mv, st).then_inc(dve_own.sem, dve_own.up())
                        dve.wait_ge(dve_own.sem, dve_own.now())
                        v.tensor_scalar(small[:, 88 + tt:89 + tt], mv[:, 1:2], LN_EPS, None, ALU.add).then_inc(var_ready.sem, var_ready.up())
                        if tt == tts[0]:
                            dve.wait_ge(ln_in.sem, ln_in.next(2))
                        v.scalar_tensor_tensor(out=x, in0=x, scalar=mv[:, 0:1], in1=ln_gb[:, 0, :],
                                               op0=ALU.subtract, op1=ALU.mult).then_inc(dve_own.sem, dve_own.up())
                        dve.wait_ge(dve_own.sem, dve_own.now())
                        dve.wait_ge(rstd_dve.sem, rstd_dve.next())
                        v.scalar_tensor_tensor(out=x, in0=x, scalar=small[:, 92 + tt:93 + tt], in1=ln_gb[:, 1, :],
                                               op0=ALU.mult, op1=ALU.add).then_inc(x_ready.sem, x_ready.up())

            def mlp(layer, tts):
                n = len(tts) * P
                for c in range(MLP_CHUNKS):
                    for kt in range(KT):
                        low((("up", layer), c * KT + kt), yl[:, kt * n:(kt + 1) * n], yh[:, kt * n:(kt + 1) * n])
                    gate = ("gate", layer, 5, len(tts) // 2 - 1, 1)
                    if c == MLP_CHUNKS - 1:
                        add_and_norm(tts, lambda g, tt: (("down", layer, c), g, tt), gate)
                    else:
                        for g in range(2):
                            for tt in tts:
                                add_gated((("down", layer, c), g, tt), tt, g, gate)
                    if layer == 0:
                        modulation(1, c)

            keep_up(("vec",))
            dve.wait_ge(psum_full.sem, filled(("vec",)))
            o = bank_of(("vec",))
            dve.wait_ge(act_part.sem, act_part.next())
            v.tensor_copy(vt[:, 0:112], o[:, 0:112]).then_inc(dve_out.sem, dve_out.up())
            dve.wait_ge(dve_out.sem, dve_out.now())
            dve.wait_ge(act_part.sem, act_part.next())
            v.tensor_scalar(small[:, 16:24], small[:, 8:16], -1.0, None, ALU.mult)
            v.tensor_scalar(small[:, 24:32], small[:, 8:16], -256.0, None, ALU.mult).then_inc(dve_part.sem, dve_part.up())
            v.tensor_copy(sil4[:, :, 0:2], silc[:, :, :]).then_inc(dve_own.sem, dve_own.up())
            dve.wait_ge(dve_own.sem, dve_own.now())
            v.tensor_tensor(sil4[:, :, 2:4], silc[:, :, :], sil4[:, :, 0:2], ALU.subtract).then_inc(x_ready.sem, x_ready.up())
            modulation(0, 0)
            modulation(0, 1)
            low_x("h0", range(4))
            prescale(range(4))

            rows4 = lambda t: t.rearrange("p (a b) -> p a b", a=ROWS)
            for h in range(RET_HEADS):
                dve.wait_ge(act_part.sem, act_part.next())
                v.tensor_tensor(r_exp[:, 0, :], r_exp[:, 0, :], r_tab[:, 2, :], ALU.mult)
                v.tensor_tensor(r_exp[:, 1, :], r_exp[:, 1, :], r_tab[:, 3, :], ALU.mult)
                v.tensor_tensor(r_exp[:, 2, :], r_exp[:, 2, :], r_exp[:, 3, :], ALU.add).then_inc(dve_own.sem, dve_own.up())
                dve.wait_ge(dve_own.sem, dve_own.now())
                v.tensor_tensor(r_strip[:, 0, :], r_exp[:, 0, :], r_exp[:, 1, :], ALU.add)
                v.tensor_scalar(r_strip[:, 1, :], r_exp[:, 2, :], 1.0 / 16.0, None, ALU.mult).then_inc(dve_own.sem, dve_own.up())
                dve.wait_ge(dve_own.sem, dve_own.now())
                for name, dst in (("rq", rq), ("rk", rk)):
                    for d in range(2):
                        keep_up(((name, h), d))
                        dve.wait_ge(psum_full.sem, filled(((name, h), d)))
                        o = rows4(bank_of(((name, h), d))[:, 0:T])
                        dve.wait_ge(act_part.sem, act_part.next())
                        c0 = C_ROPE + 8 * d
                        n = ROWS if d == 0 else GRID_W
                        cos, sin = cst[:, c0:c0 + n], cst[:, c0 + n:c0 + 2 * n]
                        if d == 0:
                            cos, sin = (x.unsqueeze(2).to_broadcast([P, ROWS, GRID_W]) for x in (cos, sin))
                        else:
                            cos, sin = (x.unsqueeze(1).to_broadcast([P, ROWS, GRID_W]) for x in (cos, sin))
                        sw, lat = rows4(r_swap[:, d, :]), rows4(dst[:, d, 0:T])
                        v.tensor_tensor(lat, o, cos, ALU.mult)
                        v.tensor_tensor(sw, sw, sin, ALU.mult).then_inc(dve_own.sem, dve_own.up())
                        dve.wait_ge(dve_own.sem, dve_own.now())
                        v.tensor_tensor(lat, lat, sw, ALU.add).then_inc(dve_out.sem, dve_out.up())
                for s in range(4):
                    keep_up(("rs", h, s))
                    dve.wait_ge(psum_full.sem, filled(("rs", h, s)))
                    o = bank_of(("rs", h, s))
                    u = s % 2
                    lo = P - P * u
                    strip = r_strip[:, 0 if s < 2 else 1, lo:lo + T]
                    ins = v.tensor_tensor(rs[:, s, :], o[:, 0:T], strip, ALU.mult)
                    if s >= 2:
                        ins = v.tensor_tensor(rs[:, s + 2, :], o[:, T:2 * T], r_strip[:, 0, lo:lo + T], ALU.mult)
                    ins.then_inc(dve_out.sem, dve_out.up())
                modulation(0, 2 + h)
                st, mv = small[:, 32:56], small[:, 80:88]
                for tt in range(4):
                    keep_up(("ro", h, tt))
                    dve.wait_ge(psum_full.sem, filled(("ro", h, tt)))
                    o = bank_of(("ro", h, tt))
                    ins = v.bn_stats(st[:, 6 * tt:6 * tt + 6], o)
                ins.then_inc(dve_own.sem, dve_own.up())
                dve.wait_ge(dve_own.sem, dve_own.now())
                for tt in range(4):
                    ins = v.bn_aggr(mv[:, 2 * tt:2 * tt + 2], st[:, 6 * tt:6 * tt + 6])
                ins.then_inc(dve_own.sem, dve_own.up())
                dve.wait_ge(dve_own.sem, dve_own.now())
                v.tensor_scalar(small[:, 88:92], mv.rearrange("p (t s) -> p t s", s=2)[:, :, 1], LN_EPS, None, ALU.add).then_inc(var_ready.sem, var_ready.up())
                dve.wait_ge(rstd_dve.sem, rstd_dve.next())
                for tt in range(4):
                    o = psum[:, units[("ro", h, tt)]["bank"], :]
                    ins = v.tensor_scalar(o, o, mv[:, 2 * tt:2 * tt + 1], small[:, 92 + tt:93 + tt], ALU.subtract, ALU.mult)
                ins.then_inc(dve_own.sem, dve_own.up())
                dve.wait_ge(dve_own.sem, dve_own.now())
                keep_up(("ron", h, 0))
                for tt in range(4):
                    dve.wait_ge(out_of((("rg", h), 0, tt)), emptied((("rg", h), 0, tt)))
                    o = psum[:, units[("ro", h, tt)]["bank"], :]
                    v.tensor_tensor(rg[:, tt, :], o, rg[:, tt, :], ALU.mult).then_inc(dve_out.sem, dve_out.up())
                for ft in range(4):
                    low(("ron", h, ft), yl[:, ft * 2 * T:(ft + 1) * 2 * T], yh[:, ft * 2 * T:(ft + 1) * 2 * T])
                if h == RET_HEADS - 1:
                    v.memset(small[:, 320:321], 0.0).then_inc(tab_free.sem, tab_free.up())
                if h < RET_HEADS - 1:
                    for c in range(2):
                        for tt in range(4):
                            add_gated((("ry", h), c, tt), tt, c, ("gate", 0, 2, 1, 1))
                else:
                    add_and_norm(range(4), lambda c, tt: (("ry", h), c, tt), ("gate", 0, 2, 1, 1))
            low_x("h0m", range(4))
            prescale(range(4))
            v.memset(small[:, 321:322], 0.0).then_inc(tab_free.sem, tab_free.up())
            mlp(0, range(4))

            low_x("h1", range(4))
            prescale(range(2))
            modulation(1, 4)
            modulation(1, 5)
            n_steps = len(nat_steps)
            for n in range(n_steps + N_LAG + 1):
                this, before = n < n_steps, 1 <= n <= n_steps
                if this:
                    qt, h = nat_steps[n]
                    keep_up(("ns", n))
                    dve.wait_ge(psum_full.sem, filled(("ns", n)))
                    o = bank_of(("ns", n))
                    if qt == 0:
                        dve.wait_ge(bias_ready.sem, bias_ready.next())
                    e0 = 2 - 2 * qt
                    b = n_bias[:, h % 2, :].rearrange("p (e k) -> p e k", k=GRID_W)[:, e0:e0 + ROWS, :]
                    v.tensor_tensor(rows4(o[:, 0:T]), rows4(o[:, 0:T]), b, ALU.add).then_inc(dve_own.sem, dve_own.up())
                    biased = dve_own.now()
                    mx = small[:, 192 + 32 * qt + h:193 + 32 * qt + h]
                if before:
                    q_, h_ = nat_steps[n - 1]
                    total = small[:, 256 + 32 * q_ + h_:257 + 32 * q_ + h_]
                    dve.wait_ge(out_of(("ns", n - 1)), emptied(("ns", n - 1)))
                    v.reciprocal(total, total).then_inc(dve_own.sem, dve_own.up())
                    inverted = dve_own.now()
                if this:
                    dve.wait_ge(dve_own.sem, biased)
                    v.tensor_reduce(mx, o, AX, ALU.max).then_inc(dve_own.sem, dve_own.up())
                    maximum = dve_own.now()
                if before:
                    x = n_prob[:, (n - 1) % N_BUFS, :]
                    dve.wait_ge(dve_own.sem, inverted)
                    v.tensor_scalar(x, x, total, None, ALU.mult).then_inc(probs_ready.sem, probs_ready.up())
                if this:
                    dve.wait_ge(dve_own.sem, maximum)
                    v.tensor_scalar(mx, mx, -1.0, None, ALU.mult).then_inc(dve_part.sem, dve_part.up())
                m = n - N_LAG - 1
                if m >= 0 and m % 8 == 7:
                    kt = m // 8
                    keep_up(("no", kt))
                    dve.wait_ge(psum_full.sem, filled(("no", kt)))
                    dve.wait_ge(act_part.sem, act_part.next())
                    v.tensor_tensor(rows_of(yl[:, kt * T:(kt + 1) * T]), turned(bank_of(("no", kt))[:, 0:T]),
                                    rows_of(yh[:, kt * T:(kt + 1) * T]), ALU.subtract).then_inc(dve_out.sem, dve_out.up())
            v.memset(small[:, 322:323], 0.0).then_inc(tab_free.sem, tab_free.up())
            add_and_norm(range(2), lambda c, tt: ("ny", c, tt), ("gate", 1, 2, 0, 1))
            low_x("h1m", range(2))
            prescale(range(2))
            v.memset(small[:, 323:324], 0.0).then_inc(tab_free.sem, tab_free.up())
            mlp(1, range(2))
            if upto < 1:
                return

            v.memset(yh_pad.bitcast(F32), 0.0)
            v.memset(yl_pad.bitcast(F32), 0.0)
            v.memset(small[:, 324:325], 0.0).then_inc(tab_free.sem, tab_free.up())

            def normed(name, col, last=None):
                if last:
                    keep_up(last, 1)
                dve.wait_ge(act_part.sem, act_part.next())
                v.tensor_tensor(small[:, 84:86], small[:, 80:82], small[:, 82:84], ALU.add).then_inc(dve_own.sem, dve_own.up())
                dve.wait_ge(dve_own.sem, dve_own.now())
                v.tensor_scalar(small[:, 84:86], small[:, 84:86], 1.0 / D, EPS, ALU.mult, ALU.add).then_inc(var_ready.sem, var_ready.up())
                dve.wait_ge(rstd_dve.sem, rstd_dve.next())
                for tt in range(TT):
                    v.tensor_scalar(diag[:, tt, :], ident, small[:, 86 + tt:87 + tt], None, ALU.mult).then_inc(u_ready.sem, u_ready.up())
                for u in range(4):
                    low_scaled((name, u), (col + 2 * u, col + 2 * u + 1),
                               lambda j: xl[:, 2 * u + j, 0:T], lambda j: xh[:, 2 * u + j, 0:T])

            def add_to_x(name, factor):
                for c in range(2):
                    for tt in range(TT):
                        x = X[:, tt, c * BANK:(c + 1) * BANK]
                        keep_up((name, c, tt), 2 - 2 * c)
                        dve.wait_ge(psum_full.sem, filled((name, c, tt)))
                        o = bank_of((name, c, tt))
                        v.scalar_tensor_tensor(out=x, in0=o, scalar=factor, in1=x,
                                                            op0=ALU.mult, op1=ALU.add).then_inc(dve_out.sem, dve_out.up())

            def feed_forward(n):
                for t in range(FF_TILES):
                    keep_up(("ff", n, t))
                    dve.wait_ge(psum_full.sem, filled(("ff", n, t)))
                    o = bank_of(("ff", n, t))
                    dve.wait_ge(act_part.sem, act_part.next())
                    p0 = 0 if t < FF_TILES - 1 else P // 2
                    f = f_v[p0:, t % 2, :]
                    hi, lo = ff_at(yh, xh, t)[p0:], ff_at(yl, xl, t)[p0:]
                    v.tensor_tensor(f, f_sil[p0:, t % 2, :], o[p0:, T:2 * T], ALU.mult).then_inc(dve_own.sem, dve_own.up())
                    dve.wait_ge(dve_own.sem, dve_own.now())
                    v.tensor_copy(hi, f).then_inc(dve_own.sem, dve_own.up())
                    dve.wait_ge(dve_own.sem, dve_own.now())
                    v.tensor_tensor(lo, f, hi, ALU.subtract).then_inc(dve_out.sem, dve_out.up())
                add_to_x(("fd", n), 0.5)

            def hybrid_layer():
                v.memset(qk_pre[:, :, 0:3], 0.0)
                dve.wait_ge(out_of(("lvec",)), emptied(("lvec",)))
                normed("f1", V_FFN1)
                feed_forward(1)
                normed("mx", V_MIX, (("fd", 1), 1, 1))
                for g in range(4):
                    keep_up(("mqk", 2 * g + 1))
                    dve.wait_ge(out_of(("mqk", 2 * g + 1)), emptied(("mqk", 2 * g + 1)))
                    for j in range(CONV_K):
                        for t in range(4 * g, 4 * g + 4):
                            w = vt[:, V_CW + 16 * j + t:V_CW + 16 * j + t + 1]
                            x = qk_pre[:, t, j:j + T]
                            if j == 0:
                                ins = v.tensor_scalar(qk_post[:, t, :], x, w, vt[:, V_CB + t:V_CB + t + 1], ALU.mult, ALU.add)
                            else:
                                ins = v.scalar_tensor_tensor(out=qk_post[:, t, :], in0=x, scalar=w, in1=qk_post[:, t, :],
                                                             op0=ALU.mult, op1=ALU.add)
                        if j < CONV_K - 1:
                            ins.then_inc(dve_own.sem, dve_own.up())
                            dve.wait_ge(dve_own.sem, dve_own.now())
                    ins.then_inc(dve_part.sem, dve_part.up())
                keep_up(("mif",))
                dve.wait_ge(psum_full.sem, filled(("mif",)))
                o = bank_of(("mif",))
                dve.wait_ge(lay_in.sem, lay_in.at(16 * N_LAYER_DMAS))
                g8 = small[:, 64:80].rearrange("p (t g) -> p t g", t=TT)
                v.tensor_tensor(g8, o[:, 0:16].rearrange("p (t g) -> p t g", t=TT),
                                             gbias.unsqueeze(1).to_broadcast([P, TT, 8]), ALU.add).then_inc(dve_out.sem, dve_out.up())
                v.memset(v_ext_ones, 1.0)
                keep_up(("mifT",))
                dve.wait_ge(psum_full.sem, filled(("mifT",)))
                v.tensor_copy(W[0:MH, 1152:1664], bank_of(("mifT",))[0:MH, :]).then_inc(dve_out.sem, dve_out.up())
                dve.wait_ge(dve_out.sem, dve_out.now())
                v.scalar_tensor_tensor(out=rowv[2], in0=rowv[1], scalar=-1.0, in1=rowv[1], op0=ALU.mult, op1=ALU.min).then_inc(dve_part.sem, dve_part.up())
                v.memset(rowv[5], 0.0)
                dve.wait_ge(act_part.sem, act_part.next())
                v.scalar_tensor_tensor(out=rowv[3], in0=rowv[1], scalar=0.0, in1=rowv[2], op0=ALU.min, op1=ALU.subtract).then_inc(dve_own.sem, dve_own.up())
                dve.wait_ge(dve_own.sem, dve_own.now())
                v.tensor_tensor_scan(rowv[1], rowv[3], rowv[5], 0.0, ALU.add, ALU.add).then_inc(dve_own.sem, dve_own.up())
                dve.wait_ge(dve_own.sem, dve_own.now())
                v.tensor_tensor(rowv[4], rowv[0], rowv[1], ALU.subtract).then_inc(dve_own.sem, dve_own.up())
                dve.wait_ge(dve_own.sem, dve_own.now())
                v.tensor_tensor_scan(rowv[6], rowv[4], rowv[4], 0.0, ALU.max, ALU.max).then_inc(dve_own.sem, dve_own.up())
                dve.wait_ge(dve_own.sem, dve_own.now())
                v.tensor_tensor(rowv[5], rowv[1], rowv[6], ALU.add).then_inc(dve_part.sem, dve_part.up())
                dve.wait_ge(dve_part.sem, dve_part.now())
                v.tensor_scalar(rowv[6], rowv[6], -1.0, None, ALU.mult).then_inc(x_ready.sem, x_ready.up())
                keep_up(("mcol",))
                dve.wait_ge(psum_full.sem, filled(("mcol",)))
                v.tensor_copy(small[:, 192:208], bank_of(("mcol",))[:, 0:16]).then_inc(dve_out.sem, dve_out.up())
                dve.wait_ge(dve_out.sem, dve_out.now())

                def mvalues(h):
                    for tt in range(TT):
                        keep_up(("mn", h, tt))
                        dve.wait_ge(psum_full.sem, filled(("mn", h, tt)))
                        o = bank_of(("mn", h, tt))
                        e = small[:, 200 + 4 * tt + h:201 + 4 * tt + h]
                        den = o[:, MHD:MHD + 1]
                        v.tensor_scalar(small[:, 93:94], den, -1.0, e, ALU.mult, ALU.max).then_inc(dve_own.sem, dve_own.up())
                        dve.wait_ge(dve_own.sem, dve_own.now())
                        v.tensor_tensor(small[:, 93:94], den, small[:, 93:94], ALU.max).then_inc(dve_own.sem, dve_own.up())
                        dve.wait_ge(dve_own.sem, dve_own.now())
                        v.reciprocal(small[:, 88:89], small[:, 93:94]).then_inc(dve_part.sem, dve_part.up())
                        dve.wait_ge(dve_part.sem, dve_part.now())
                        dve.wait_ge(act_part.sem, act_part.next())
                        v.tensor_scalar(small[:, 90:91], small[:, 89:90], 1.0 / MHD, EPS, ALU.mult, ALU.add).then_inc(var_ready.sem, var_ready.up())
                        dve.wait_ge(rstd_dve.sem, rstd_dve.next())
                        v.tensor_tensor(small[:, 92:93], small[:, 88:89], small[:, 91:92], ALU.mult).then_inc(dve_own.sem, dve_own.up())
                        dve.wait_ge(dve_own.sem, dve_own.now())
                        if h == 0:
                            dve.wait_ge(out_of(("mo", 1, tt)), emptied(("mo", 1, tt)))
                        cols = slice(h * MHD, (h + 1) * MHD)
                        v.scalar_tensor_tensor(out=U[:, tt, cols], in0=o[:, 0:MHD], scalar=small[:, 92:93],
                                                            in1=sig_o[:, tt, cols], op0=ALU.mult, op1=ALU.mult).then_inc(dve_out.sem, dve_out.up())

                dve.wait_ge(tri_in.sem, tri_in.at(16))
                for h in range(MH + 1):
                    if h < MH:
                        keep_up(("mb", h))
                        dve.wait_ge(psum_full.sem, filled(("mb", h)))
                        o = bank_of(("mb", h))
                        a0, a1 = small[:, 192 + h:193 + h], small[:, 196 + h:197 + h]
                        t_ = tri[:, 0:P]
                        r = m_arg[:, h % 2, :]
                        v.scalar_tensor_tensor(out=r[:, 0:P], in0=o[:, 0:P], scalar=a0, in1=t_, op0=ALU.add, op1=ALU.add)
                        v.tensor_scalar(r[:, P:T], o[:, P:T], a0, None, ALU.add)
                        v.scalar_tensor_tensor(out=r[:, T:T + P], in0=o[:, P:T], scalar=a1, in1=t_, op0=ALU.add, op1=ALU.add).then_inc(dve_out.sem, dve_out.up())
                        keep_up(("ms", h))
                        dve.wait_ge(psum_full.sem, filled(("ms", h)))
                        o = bank_of(("ms", h))
                        dve.wait_ge(act_part.sem, act_part.next())
                        v.scalar_tensor_tensor(out=m_s[:, h % 2, :], in0=o[:, 0:384], scalar=1.0 / 16.0, in1=r,
                                                            op0=ALU.mult, op1=ALU.mult).then_inc(dve_out.sem, dve_out.up())
                    if h:
                        mvalues(h - 1)
                for u in range(4):
                    low_scaled(("hmT", u), (V_MO + 2 * u, V_MO + 2 * u + 1),
                               lambda j: yl[:, (2 * u + j) * T:(2 * u + j + 1) * T], lambda j: yh[:, (2 * u + j) * T:(2 * u + j + 1) * T])
                dve.wait_ge(out_of(("gm", 1, 1)), emptied(("gm", 1, 1)))
                for c in range(2):
                    for tt in range(TT):
                        cols = slice(c * BANK, (c + 1) * BANK)
                        keep_up(("bm", c, tt))
                        dve.wait_ge(psum_full.sem, filled(("bm", c, tt)))
                        v.tensor_tensor(merged[:, tt, cols], bank_of(("bm", c, tt)), sig_g[:, tt, cols], ALU.mult).then_inc(dve_out.sem, dve_out.up())
                for name in (("aq", 0), ("aq", 1), ("ak", 0)):
                    for tt in range(TT):
                        keep_up((*name, tt))
                        dve.wait_ge(psum_full.sem, filled((*name, tt)))
                        o = bank_of((*name, tt))
                        dve.wait_ge(act_part.sem, act_part.next())
                        nh = 8 if name[0] == "aq" else AKV
                        sq = squares[tt][:, 0:nh * AHD].rearrange("p (h d) -> p h d", d=AHD)
                        v.tensor_reduce(small[:, 208:208 + nh], sq, AX, ALU.add).then_inc(squares_used.sem, squares_used.up())
                        dve.wait_ge(squares_used.sem, squares_used.now())
                        v.tensor_scalar(small[:, 216:216 + nh], small[:, 208:208 + nh], 1.0 / AHD, EPS, ALU.mult, ALU.add).then_inc(var_ready.sem, var_ready.up())
                        dve.wait_ge(rstd_dve.sem, rstd_dve.next())
                        r = small[:, 224:224 + nh].unsqueeze(2).to_broadcast([P, nh, AHD])
                        x = o[:, 0:nh * AHD].rearrange("p (h d) -> p h d", d=AHD)
                        if name[0] == "aq":
                            dst = qn[:, tt, name[1] * BANK:(name[1] + 1) * BANK].rearrange("p (h d) -> p h d", d=AHD)
                            v.tensor_tensor(dst, x, r, ALU.mult).then_inc(dve_out.sem, dve_out.up())
                        else:
                            dst = kn[:, tt, :].rearrange("p (h b d) -> p h b d", b=2, d=AHD)
                            v.tensor_tensor(dst[:, :, 0, :], x, r, ALU.mult)
                            v.tensor_tensor(dst[:, :, 1, :], x, r, ALU.mult).then_inc(dve_out.sem, dve_out.up())
                v.tensor_scalar(small[:, 232:248], sink, float(AHD) ** 0.5, None, ALU.mult).then_inc(dve_own.sem, dve_own.up())
                dve.wait_ge(dve_own.sem, dve_own.now())
                for n in range(len(a_groups) + N_LAG):
                    if n < len(a_groups):
                        qt, heads = a_groups[n]
                        nh = len(heads)
                        c, hs = 16 * qt + heads[0], slice(heads[0], heads[-1] + 1, 2)
                        keep_up(("as", n))
                        dve.wait_ge(psum_full.sem, filled(("as", n)))
                        o = bank_of(("as", n)).rearrange("p (h k) -> p h k", h=nh)
                        mask = tri[:, 256:384] if qt == 0 else tri[:, 128:384]
                        v.tensor_tensor(o, o, mask.unsqueeze(1).to_broadcast([P, nh, BANK // nh]), ALU.add).then_inc(dve_own.sem, dve_own.up())
                        dve.wait_ge(dve_own.sem, dve_own.now())
                        mx, es = (small[:, k + c:k + c + 2 * nh - 1:2] for k in (96, 160))
                        v.tensor_reduce(mx, o, AX, ALU.max).then_inc(dve_own.sem, dve_own.up())
                        dve.wait_ge(dve_own.sem, dve_own.now())
                        v.tensor_tensor(mx, mx, small[:, 232:248][:, hs], ALU.max).then_inc(dve_own.sem, dve_own.up())
                        dve.wait_ge(dve_own.sem, dve_own.now())
                        v.tensor_scalar(mx, mx, -(float(AHD) ** -0.5), None, ALU.mult).then_inc(dve_own.sem, dve_own.up())
                        dve.wait_ge(dve_own.sem, dve_own.now())
                        v.tensor_tensor(es, mx, sink[:, hs], ALU.add).then_inc(dve_part.sem, dve_part.up())
                    m = n - LAG
                    if 0 <= m < len(a_groups) and units[("at", m)]["owner"] == "dve":
                        keep_up(("at", m))
                        dve.wait_ge(psum_full.sem, filled(("at", m)))
                        if m >= A_BUFS:
                            s_, v_ = seen["a", m - A_BUFS]
                            dve.wait_ge(s_.sem, s_.at(v_))
                        v.tensor_copy(a_buf(a_probT, m), bank_of(("at", m))).then_inc(dve_out.sem, dve_out.up())
                    done = n - N_LAG
                    if done >= 0:
                        qt, heads = a_groups[done]
                        per = 2 if qt == 0 else 4
                        m = done if qt == 0 else done - 4
                        if m % per == per - 1:
                            u = m // per
                            keep_up(("ao", qt, u))
                            dve.wait_ge(psum_full.sem, filled(("ao", qt, u)))
                            o = bank_of(("ao", qt, u)).rearrange("p (h d) -> p h d", h=8)
                            dve.wait_ge(out_of(("as", done)), emptied(("as", done)))
                            c = 16 * qt + 8 * u
                            den = small[:, 128 + c:136 + c]
                            v.tensor_tensor(den, den, small[:, 160 + c:168 + c], ALU.add).then_inc(dve_own.sem, dve_own.up())
                            dve.wait_ge(dve_own.sem, dve_own.now())
                            v.reciprocal(den, den).then_inc(dve_own.sem, dve_own.up())
                            dve.wait_ge(dve_own.sem, dve_own.now())
                            dst = U[:, qt, u * BANK:(u + 1) * BANK].rearrange("p (h d) -> p h d", h=8)
                            v.tensor_tensor(dst, o, den.unsqueeze(2).to_broadcast([P, 8, AHD]), ALU.mult).then_inc(dve_out.sem, dve_out.up())
                for u in range(4):
                    low(("haT", u), yl[:, u * 512:(u + 1) * 512], yh[:, u * 512:(u + 1) * 512])
                dve.wait_ge(out_of(("ga", 1, 1)), emptied(("ga", 1, 1)))
                for c in range(2):
                    for tt in range(TT):
                        cols = slice(c * BANK, (c + 1) * BANK)
                        keep_up(("ba", c, tt))
                        dve.wait_ge(psum_full.sem, filled(("ba", c, tt)))
                        o = bank_of(("ba", c, tt))
                        v.tensor_tensor(o, o, sig_g[:, tt, cols], ALU.mult).then_inc(dve_own.sem, dve_own.up())
                        dve.wait_ge(dve_own.sem, dve_own.now())
                        v.tensor_tensor(merged[:, tt, cols], o, merged[:, tt, cols], ALU.add).then_inc(dve_out.sem, dve_out.up())
                low_x("mg", range(2))
                add_to_x("wo", 1.0)
                normed("f2", V_FFN2, ("wo", 1, 1))
                feed_forward(2)
                normed("pl", V_PLE, (("fd", 2), 1, 1))
                low(("pT",), yl[:, 0:512], yh[:, 0:512])
                for c in range(2):
                    for tt in range(TT):
                        cols = slice(c * BANK, (c + 1) * BANK)
                        keep_up(("pp", c, tt))
                        dve.wait_ge(psum_full.sem, filled(("pp", c, tt)))
                        o = bank_of(("pp", c, tt))
                        dve.wait_ge(out_of(("pg", c, tt)), emptied(("pg", c, tt)))
                        v.tensor_tensor(o, o, sig_g[:, tt, cols], ALU.mult).then_inc(dve_own.sem, dve_own.up())
                        dve.wait_ge(dve_own.sem, dve_own.now())
                        v.tensor_tensor(X[:, tt, cols], o, X[:, tt, cols], ALU.add).then_inc(dve_out.sem, dve_out.up())

            start["dve"] = {n: s_.sent for n, s_ in signals.items()}
            assert dve_out.sent == start["owned"]["dve"], (dve_out.sent, start["owned"])
            split.update(base=start["split"], limit=len(split_blocks))
            with dve.Fori(0, DEPTH) as i:
                loop["i"] = i
                dve.wait_ge(dve_out.sem, dve_out.now())
                for n, s_ in enumerate((layer_start, layer_start_act, layer_start_pool)):
                    v.memset(small[:, 328 + n:329 + n], 0.0).then_inc(s_.sem, s_.up())
                hybrid_layer()
            loop["i"] = None

        @block.gpsimd
        def _(pool):
            g = nc.gpsimd

            def rstd(ve, dst, n, signal_):
                pool.wait_ge(var_ready.sem, var_ready.next())
                g.tensor_tensor(dst, ve, small[:, 336:336 + n], ALU.pow).then_inc(signal_.sem, signal_.up())

            def ln_table(layer, j):
                pool.wait_ge(tab_free.sem, tab_free.next())
                for k, x in enumerate((a["ln_g"], a["ln_b"])):
                    pool.dma_start(ln_gb[:, k, :], x[layer, j:j + 1, :].to_broadcast([P, D])).then_inc(ln_in.sem, ln_in.up())

            def ln_rstd(n):
                for tt in range(n):
                    rstd(small[:, 88 + tt:89 + tt], small[:, 92 + tt:93 + tt], 1, rstd_dve)

            def load_vectors(layer):
                rows = [(V_FFN1, "ffn1_norm_2"), (V_MIX, "mix_norm_2"), (V_CW, "m_conv_w_2"), (V_CB, "m_conv_b_2"),
                        (V_MO, "m_out_norm_2"), (V_FFN2, "ffn2_norm_2"), (V_PLE, "ple_norm_2")]
                for r, name in rows:
                    x = a[name][layer]
                    x = x.rearrange("(r n) -> r n", n=P) if len(x.shape) == 1 else x.rearrange("k (r n) -> (k r) n", n=P)
                    pool.dma_start(l_rows[r:r + x.shape[0], :], x).then_inc(lay_in.sem, lay_in.up())
                for r, name in ((V_AQ, "a_q_norm_2"), (V_AK, "a_k_norm_2")):
                    for c in (0, AHD):
                        pool.dma_start(l_rows[r:r + 1, c:c + AHD], a[name][layer].unsqueeze(0)).then_inc(lay_in.sem, lay_in.up())
                pool.dma_start(sink, a["a_sinks_2"][layer].unsqueeze(0).to_broadcast([P, AH])).then_inc(lay_in.sem, lay_in.up())
                pool.dma_start(gbias[:, 0:MH], a["m_igate_b_2"][layer].unsqueeze(0).to_broadcast([P, MH])).then_inc(lay_in.sem, lay_in.up())
                pool.dma_start(gbias[:, MH:2 * MH], a["m_fgate_b_2"][layer].unsqueeze(0).to_broadcast([P, MH])).then_inc(lay_in.sem, lay_in.up())

            g.memset(small[:, 336:352], -0.5).then_inc(pool_own.sem, pool_own.up())
            pool.wait_ge(pool_own.sem, pool_own.now())
            for h in range(RET_HEADS):
                rstd(small[:, 88:92], small[:, 92:96], 4, rstd_dve)
            ln_table(0, 0)
            ln_rstd(4)
            ln_table(0, 1)
            ln_rstd(4)
            pool.wait_ge(out_of(("nq", KT - 1)), emptied(("nq", KT - 1)))
            pool.wait_ge(const_in.sem, const_in.at(16))
            for h in range(NAT_HEADS):
                if h >= 2:
                    pool.wait_ge(psum_full.sem, filled(("ns", 2 * (h - 2) + 1)))
                g.tensor_scalar(n_q[:, h % 2, :], nq[:, h // 4, :], cst[:, C_HEAD + h % 4:C_HEAD + h % 4 + 1], None, ALU.mult).then_inc(q_ready.sem, q_ready.up())
                pool.wait_ge(bias_in[h % 2].sem, bias_in[h % 2].next(2))
                b = n_bias[:, h % 2, :].rearrange("p (e k) -> p e k", k=GRID_W)
                win = cst[:, C_WIN:C_WIN + GRID_W].unsqueeze(1).to_broadcast([P, 6, GRID_W])
                g.tensor_tensor(b, b, win, ALU.add).then_inc(bias_ready.sem, bias_ready.up())
            ln_table(1, 0)
            ln_rstd(2)
            ln_table(1, 1)
            if upto >= 1:
                load_vectors(0)
            ln_rstd(2)
            if upto < 1:
                return
            pool.wait_ge(tab_free.sem, tab_free.next())
            pool.dma_start(tri, a["consts"][:, C_TRI:C_TRI + 384]).then_inc(tri_in.sem, tri_in.up())
            start["pool"] = {n: s_.sent for n, s_ in signals.items()}
            with pool.Fori(0, DEPTH) as i:
                loop["i"] = i
                pool.wait_ge(layer_start_pool.sem, layer_start_pool.next())
                pool.dma_start(l_p, a["p_2"][i][0].rearrange("(t p) n -> p t n", p=P)).then_inc(p_in.sem, p_in.up())
                for _ in range(2):
                    rstd(small[:, 84:86], small[:, 86:88], 2, rstd_dve)
                for _ in range(MH * TT):
                    rstd(small[:, 90:91], small[:, 91:92], 1, rstd_dve)
                for nh in (8, 8, 8, 8, AKV, AKV):
                    rstd(small[:, 216:216 + nh], small[:, 224:224 + nh], nh, rstd_dve)
                rstd(small[:, 84:86], small[:, 86:88], 2, rstd_dve)
                load_vectors(1)
                rstd(small[:, 84:86], small[:, 86:88], 2, rstd_dve)
            loop["i"] = None

        @block.sync
        def _(sp):
            def load(n):
                b = blocks[n]
                if n >= RING:
                    sig, val = blocks[n - RING]["release"]
                    sp.wait_ge(sig.sem, sig.at(val))
                i = loop.get("i")
                dst = raw[:, b["slot"], :b["size"]].rearrange("p (a b) -> p a b", a=b["shape"][1])
                sp.dma_start(dst, b["source"](0 if i is None else i)).then_inc(raw_in[b["slot"]].sem, 16)

            for n in range(start.get("blocks", len(blocks))):
                load(n)
            if upto >= 1:
                assert all(blocks[start["blocks"] - 1 - k]["release"][0] is split_done for k in range(RING))
                with sp.Fori(0, DEPTH) as i:
                    loop["i"] = i
                    for n in range(start["blocks"], len(blocks)):
                        load(n)
                loop["i"] = None
                end = dve_out.sent + (dve_out.sent - start["dve"]["dve_out"])
                sp.wait_ge(dve_out.sem, end)
                sp.wait_ge(lay_in.sem, 16 * N_LAYER_DMAS * (1 + DEPTH))
            else:
                sp.wait_ge(x_ready.sem, x_ready.sent)
            sp.dma_start(out[0].rearrange("(t p) n -> p t n", p=P), X[:, 0:TT, :]).then_inc(out_done.sem, out_done.up())
            sp.wait_ge(out_done.sem, out_done.at(16))

        if counts is not None:
            counts.update({n: (s_.sent, s_.taken) for n, s_ in signals.items()}, start=start)


_INS = ["x", "c", "ctx", "c_ctx", "ada_w", "ada_b", "ret_w_in", "ret_w_o", "ret_decay", "nat_w_in", "nat_w_o", "nat_rpb",
        "mlp_w1", "mlp_w2", "ln_g", "ln_b", "p_2", "ffn1_norm_2", "ffn1_w_gate_2", "ffn1_w_up_2", "ffn1_w_down_2",
        "mix_norm_2", "w_in_2", "m_conv_w_2", "m_conv_b_2", "m_igate_b_2", "m_fgate_b_2", "m_out_norm_2",
        "a_q_norm_2", "a_k_norm_2", "a_sinks_2", "w_branch_m_2", "w_branch_a_2", "w_out_2", "ffn2_norm_2",
        "ffn2_w_gate_2", "ffn2_w_up_2", "ffn2_w_down_2", "ple_norm_2", "ple_gate_w_2", "ple_proj_w_2"]


def kernel(**inputs):
    import concourse.bacc as bacc
    from concourse.bass_utils import run_bass_kernel_spmd

    nc = bacc.Bacc("TRN2", target_bir_lowering=False, num_devices=1)
    arrays, args = {}, {}
    for name in _INS:
        arrays[name] = np.ascontiguousarray(inputs[name])
    arrays["consts"] = constants()
    for name, x in arrays.items():
        args[name] = nc.dram_tensor(name, x.shape, mybir.dt.from_np(x.dtype), kind="ExternalInput").ap()
    out = nc.dram_tensor("y", (1, T, D), F32, kind="ExternalOutput").ap()
    build(nc, args, out)
    r = run_bass_kernel_spmd(nc, [arrays], core_ids=[0])
    return r.results[0]["y"]
```
